# Optimizing a Trainium2 kernel written in Bass

```python
import jax, jax.numpy as jnp
from jax import lax
import numpy as np

D_MODEL = 1024
BATCH = 1
SEQ = 512
DEPTH = 1

N_HEADS = 8
HEAD_DIM = 128
ATTN_WIDTH = N_HEADS * HEAD_DIM
ROPE_THETA = 10000.0
IDX_HEADS = 8
IDX_DIM = 64
IDX_TOPK_MAX = 256
Q_BLOCK = 32
SGU_GROUPS = 8
SGU_WIDTH = 1024
SGU_GROUP_DIM = SGU_WIDTH // SGU_GROUPS
CHUNK = 128
N_GROUPS = 4
EXPERTS_PER_GROUP = 8
N_EXPERTS = N_GROUPS * EXPERTS_PER_GROUP
TOP_K_INNER = 2
D_EXPERT = 256
NORM_EPS = 1e-6

SPLIT_SIZES = (ATTN_WIDTH, ATTN_WIDTH, ATTN_WIDTH,
               IDX_HEADS * IDX_DIM, IDX_DIM, IDX_HEADS,
               SGU_WIDTH, SGU_WIDTH,
               D_MODEL, D_MODEL)
D_IN_PROJ = sum(SPLIT_SIZES)


def rms_norm(x, g):
    xf = x.astype(jnp.float32)
    xf = xf * lax.rsqrt(jnp.mean(xf * xf, axis=-1, keepdims=True) + NORM_EPS)
    return (xf * g.astype(jnp.float32)).astype(x.dtype)

def layer_norm(x, g):
    xf = x.astype(jnp.float32)
    mu = jnp.mean(xf, axis=-1, keepdims=True)
    var = jnp.mean(jnp.square(xf - mu), axis=-1, keepdims=True)
    return ((xf - mu) * lax.rsqrt(var + NORM_EPS) * g.astype(jnp.float32)).astype(x.dtype)

def rope(x, positions):
    d = x.shape[-1]
    inv = ROPE_THETA ** (-jnp.arange(0, d, 2, dtype=jnp.float32) / d)
    ang = positions.astype(jnp.float32)[..., None] * inv
    cos = jnp.cos(ang)[:, :, None, :]
    sin = jnp.sin(ang)[:, :, None, :]
    x1, x2 = jnp.split(x.astype(jnp.float32), 2, axis=-1)
    out = jnp.concatenate([x1 * cos - x2 * sin, x2 * cos + x1 * sin], axis=-1)
    return out.astype(x.dtype)

def split_columns(proj):
    parts, start = [], 0
    for size in SPLIT_SIZES:
        parts.append(proj[..., start:start + size])
        start += size
    return parts

def dsa_attention(q, k, v, qi, ki, wi):
    B, L = q.shape[0], q.shape[1]
    top_k = min(IDX_TOPK_MAX, L // 4)
    nb = L // Q_BLOCK

    def to_blocks(a):
        return jnp.moveaxis(a.reshape(B, nb, Q_BLOCK, *a.shape[2:]), 1, 0)

    starts = jnp.arange(nb, dtype=jnp.int32) * Q_BLOCK
    key_pos = jnp.arange(L, dtype=jnp.int32)
    gather = jax.vmap(lambda src, idx: src[idx])

    def block(args):
        qb, qib, wb, start = args
        qpos = start + jnp.arange(Q_BLOCK, dtype=jnp.int32)
        rel = jax.nn.relu(jnp.einsum('bqhd,bsd->bqhs', qib, ki))
        score = jnp.einsum('bqh,bqhs->bqs', wb, rel).astype(jnp.float32)
        causal = key_pos[None, :] <= qpos[:, None]
        score = jnp.where(causal[None], score, -jnp.inf)
        _, sel = lax.top_k(score, top_k)
        valid = sel <= qpos[None, :, None]
        kg = gather(k, sel)
        vg = gather(v, sel)
        logits = jnp.einsum('bqhd,bqkhd->bhqk', qb, kg).astype(jnp.float32) * (HEAD_DIM ** -0.5)
        logits = jnp.where(valid[:, None], logits, -jnp.inf)
        p = jax.nn.softmax(logits, axis=-1).astype(v.dtype)
        return jnp.einsum('bhqk,bqkhd->bqhd', p, vg)

    out = lax.map(block, (to_blocks(q), to_blocks(qi), to_blocks(wi), starts))
    return jnp.moveaxis(out, 0, 1).reshape(B, L, ATTN_WIDTH)

def spatial_gating(u, v, norm_g, w_s, b_s):
    B, L, _ = u.shape
    nc = L // CHUNK
    v = layer_norm(v, norm_g)
    vc = v.reshape(B, nc, CHUNK, SGU_GROUPS, SGU_GROUP_DIM)
    mask = jnp.tril(jnp.ones((CHUNK, CHUNK), dtype=bool))
    w = jnp.where(mask[None], w_s, jnp.zeros_like(w_s))
    mixed = jnp.einsum('gts,bcsgd->bctgd', w, vc) + b_s.T[None, None, :, :, None]
    return u * mixed.reshape(B, L, SGU_WIDTH)

def hier_moe(xn, w_group, b_group, w_er, b_er, w_e_in, w_e_out):
    B, L, D = xn.shape
    T = B * L
    xt = xn.reshape(T, D)
    g_logits = (xt @ w_group).astype(jnp.float32) + b_group.astype(jnp.float32)
    g_sel = jnp.argmax(g_logits, axis=-1)
    g_prob = jnp.take_along_axis(jax.nn.softmax(g_logits, axis=-1), g_sel[:, None], axis=1)
    e_logits = ((xt @ w_er).astype(jnp.float32) + b_er.astype(jnp.float32)).reshape(T, N_GROUPS, EXPERTS_PER_GROUP)
    e_in_group = jnp.take_along_axis(e_logits, g_sel[:, None, None], axis=1)[:, 0]
    top_v, top_i = lax.top_k(e_in_group, TOP_K_INNER)
    gates = g_prob * jax.nn.softmax(top_v, axis=-1)
    expert_id = (g_sel[:, None] * EXPERTS_PER_GROUP + top_i).reshape(-1)
    token_id = jnp.repeat(jnp.arange(T, dtype=jnp.int32), TOP_K_INNER)
    order = jnp.argsort(expert_id)
    tok_sorted = token_id[order]
    group_sizes = jnp.bincount(expert_id, length=N_EXPERTS).astype(jnp.int32)
    xs = xt[tok_sorted]
    hdn = lax.ragged_dot(xs, w_e_in, group_sizes)
    gate_h, up_h = jnp.split(hdn, 2, axis=-1)
    act = jax.nn.silu(gate_h) * up_h
    ys = lax.ragged_dot(act, w_e_out, group_sizes)
    ys = ys * gates.reshape(-1)[order][:, None].astype(ys.dtype)
    return jnp.zeros_like(xt).at[tok_sorted].add(ys).reshape(B, L, D)

def first_inputs(seed: int = 0) -> dict:
    key = jax.random.key(seed)
    ks = jax.random.split(key, 20)
    f32 = jnp.float32
    nrm = lambda k, shape, scale: jax.random.normal(k, shape, f32) * scale
    x = jax.random.normal(ks[0], (BATCH, SEQ, D_MODEL), f32)
    offset = jax.random.randint(ks[1], (BATCH, 1), 0, 1024, dtype=jnp.int32)
    positions = offset + jnp.arange(SEQ, dtype=jnp.int32)[None, :]
    return {
        "x": x,
        "positions": positions,
        "norm1_g": 1.0 + nrm(ks[2], (DEPTH, D_MODEL), 0.02),
        "w_in": nrm(ks[3], (DEPTH, D_MODEL, D_IN_PROJ), D_MODEL ** -0.5),
        "sgu_norm_g": 1.0 + nrm(ks[4], (DEPTH, SGU_WIDTH), 0.02),
        "sgu_w": nrm(ks[5], (DEPTH, SGU_GROUPS, CHUNK, CHUNK), CHUNK ** -0.5),
        "sgu_b": 1.0 + nrm(ks[6], (DEPTH, SGU_GROUPS, CHUNK), 0.1),
        "w_branch_a": nrm(ks[7], (DEPTH, SGU_WIDTH, D_MODEL), SGU_WIDTH ** -0.5),
        "w_branch_b": nrm(ks[8], (DEPTH, ATTN_WIDTH, D_MODEL), ATTN_WIDTH ** -0.5),
        "w_out": nrm(ks[9], (DEPTH, D_MODEL, D_MODEL), D_MODEL ** -0.5),
        "norm2_g": 1.0 + nrm(ks[10], (DEPTH, D_MODEL), 0.02),
        "w_router_group": nrm(ks[11], (DEPTH, D_MODEL, N_GROUPS), D_MODEL ** -0.5),
        "b_router_group": nrm(ks[12], (DEPTH, N_GROUPS), 0.01),
        "w_router_expert": nrm(ks[13], (DEPTH, D_MODEL, N_EXPERTS), D_MODEL ** -0.5),
        "b_router_expert": nrm(ks[14], (DEPTH, N_EXPERTS), 0.01),
        "w_expert_in": nrm(ks[15], (DEPTH, N_EXPERTS, D_MODEL, 2 * D_EXPERT), D_MODEL ** -0.5),
        "w_expert_out": nrm(ks[16], (DEPTH, N_EXPERTS, D_EXPERT, D_MODEL), D_EXPERT ** -0.5),
        "norm_f_g": 1.0 + nrm(ks[17], (D_MODEL,), 0.02),
    }

def first_block(x, positions, norm1_g, w_in, sgu_norm_g, sgu_w, sgu_b, w_branch_a, w_branch_b,
              w_out, norm2_g, w_router_group, b_router_group, w_router_expert, b_router_expert,
              w_expert_in, w_expert_out, norm_f_g):
    B, L, _ = x.shape
    h = x
    for l in range(DEPTH):
        xn = rms_norm(h, norm1_g[l])
        proj = xn @ w_in[l]
        q, k, v, qi, ki, wi, su, sv, ga, gb = split_columns(proj)
        q = rope(q.reshape(B, L, N_HEADS, HEAD_DIM), positions)
        k = rope(k.reshape(B, L, N_HEADS, HEAD_DIM), positions)
        v = v.reshape(B, L, N_HEADS, HEAD_DIM)
        qi = rope(qi.reshape(B, L, IDX_HEADS, IDX_DIM), positions)
        ki = rope(ki[:, :, None, :], positions)[:, :, 0]
        y_attn = dsa_attention(q, k, v, qi, ki, wi)
        y_sgu = spatial_gating(jax.nn.gelu(su), jax.nn.gelu(sv), sgu_norm_g[l], sgu_w[l], sgu_b[l])
        merged = (jax.nn.sigmoid(ga) * (y_sgu @ w_branch_a[l])
                  + jax.nn.sigmoid(gb) * (y_attn @ w_branch_b[l]))
        h = h + merged @ w_out[l]
        h = h + hier_moe(rms_norm(h, norm2_g[l]), w_router_group[l], b_router_group[l],
                         w_router_expert[l], b_router_expert[l], w_expert_in[l], w_expert_out[l])
    return rms_norm(h, norm_f_g)


N_META = 16
BLOCK = 128
LEAD_PAD = BLOCK - N_META
SB_HEAD_DIM = 64
SB_WIDTH = D_MODEL // 2
SB_HEADS = SB_WIDTH // SB_HEAD_DIM
HG_HEAD_DIM = 128
HG_WIDTH = D_MODEL - SB_WIDTH
HG_HEADS = HG_WIDTH // HG_HEAD_DIM
MIX_WIDTH = SB_WIDTH + HG_WIDTH
IN_SPLITS = [SB_WIDTH, SB_WIDTH, SB_WIDTH, HG_WIDTH, HG_WIDTH, HG_WIDTH, HG_WIDTH]
IN_PROJ_WIDTH = sum(IN_SPLITS)
N_EXPERTS_2 = N_GROUPS * EXPERTS_PER_GROUP
TOP_K_IN_GROUP = 2
EXPERT_FF = D_MODEL // 2
MOE_BLOCK = 128
EPS = 1e-6


def rmsnorm(x, gain):
    xf = x.astype(jnp.float32)
    y = xf * lax.rsqrt(jnp.mean(xf * xf, axis=-1, keepdims=True) + EPS)
    return (y * gain.astype(jnp.float32)).astype(x.dtype)

def split_heads(t, n_heads, head_dim):
    b, l, _ = t.shape
    return t.reshape(b, l, n_heads, head_dim).transpose(0, 2, 1, 3)

def merge_heads_norm(o, gain):
    b, h, l, d = o.shape
    o = rmsnorm(o.transpose(0, 2, 1, 3), gain.reshape(h, d))
    return o.reshape(b, l, h * d)

def stick_breaking_attention(q, k, v):
    L = q.shape[2]
    scale = SB_HEAD_DIM ** -0.5
    outs = []
    for blk in range(L // BLOCK):
        t0 = blk * BLOCK
        t1 = t0 + BLOCK
        z = jnp.einsum('bhtd,bhsd->bhts', q[:, :, t0:t1], k[:, :, :t1]).astype(jnp.float32) * scale
        t_pos = jnp.arange(t0, t1)[:, None]
        s_pos = jnp.arange(t1)[None, :]
        valid = (s_pos < t_pos) & (s_pos >= LEAD_PAD)
        log_beta = jax.nn.log_sigmoid(z)
        log_keep = jnp.where(valid, jax.nn.log_sigmoid(-z), 0.0)
        log_tail = lax.cumsum(log_keep, axis=3, reverse=True) - log_keep
        w = jnp.where(valid, jnp.exp(log_beta + log_tail), 0.0)
        outs.append(jnp.einsum('bhts,bhsd->bhtd', w.astype(v.dtype), v[:, :, :t1]))
    return jnp.concatenate(outs, axis=2)

def hgrn2_chunked(q, k, v, log_f):
    b, h, L, dk = q.shape
    dv = v.shape[-1]
    nc = L // BLOCK

    def to_chunks(t):
        return jnp.moveaxis(t.reshape(b, h, nc, BLOCK, t.shape[-1]), 2, 0)

    causal = jnp.tril(jnp.ones((BLOCK, BLOCK), bool))[:, :, None]

    def step(state, inp):
        qc, kc, vc, gc = inp
        bc = jnp.cumsum(gc, axis=2)
        diff = bc[:, :, :, None, :] - bc[:, :, None, :, :]
        decay = jnp.exp(jnp.where(causal, diff, -jnp.inf))
        scores = jnp.einsum('bhtd,bhsd,bhtsd->bhts', qc, kc, decay)
        o = jnp.einsum('bhts,bhsv->bhtv', scores, vc) + jnp.einsum('bhtd,bhdv->bhtv', qc * jnp.exp(bc), state)
        b_last = bc[:, :, -1, :]
        state = jnp.exp(b_last)[..., None] * state + jnp.einsum(
            'bhsd,bhsv->bhdv', kc * jnp.exp(b_last[:, :, None, :] - bc), vc)
        return state, o

    s0 = jnp.zeros((b, h, dk, dv), jnp.float32)
    _, o = lax.scan(step, s0, (to_chunks(q), to_chunks(k), to_chunks(v), to_chunks(log_f)))
    return jnp.moveaxis(o, 0, 2).reshape(b, h, L, dv)

def hierarchical_moe(x2, w_rg, b_rg, w_re, b_re, w_gate, w_up, w_down):
    n_tok = x2.shape[0]
    grp_probs = jax.nn.softmax(jnp.dot(x2, w_rg).astype(jnp.float32) + b_rg.astype(jnp.float32), axis=-1)
    grp = jnp.argmax(grp_probs, axis=-1)
    p_grp = jnp.max(grp_probs, axis=-1)
    exp_logits = (jnp.dot(x2, w_re).astype(jnp.float32) + b_re.astype(jnp.float32)).reshape(
        n_tok, N_GROUPS, EXPERTS_PER_GROUP)
    in_grp = exp_logits[jnp.arange(n_tok), grp]
    top_val, top_idx = lax.top_k(in_grp, TOP_K_IN_GROUP)
    gate = jax.nn.softmax(top_val, axis=-1) * p_grp[:, None]
    expert_id = (grp[:, None] * EXPERTS_PER_GROUP + top_idx).reshape(-1).astype(jnp.int32)
    gate_flat = gate.reshape(-1)
    token_id = jnp.repeat(jnp.arange(n_tok, dtype=jnp.int32), TOP_K_IN_GROUP)
    n_assign = n_tok * TOP_K_IN_GROUP
    n_slots = -(-n_assign // MOE_BLOCK) * MOE_BLOCK + N_EXPERTS_2 * MOE_BLOCK
    n_blocks = n_slots // MOE_BLOCK
    counts = jnp.zeros((N_EXPERTS_2,), jnp.int32).at[expert_id].add(1)
    padded = (counts + MOE_BLOCK - 1) // MOE_BLOCK * MOE_BLOCK
    padded_end = jnp.cumsum(padded)
    padded_start = padded_end - padded
    start = jnp.cumsum(counts) - counts
    order = jnp.argsort(expert_id)
    sorted_e = expert_id[order]
    dest = padded_start[sorted_e] + jnp.arange(n_assign, dtype=jnp.int32) - start[sorted_e]
    slot_tok = jnp.zeros((n_slots,), jnp.int32).at[dest].set(token_id[order])
    slot_gate = jnp.zeros((n_slots,), jnp.float32).at[dest].set(gate_flat[order])
    block_e = jnp.clip(jnp.searchsorted(padded_end, jnp.arange(n_blocks, dtype=jnp.int32) * MOE_BLOCK,
                                        side='right'), 0, N_EXPERTS_2 - 1)

    def run_block(args):
        tok, g, e = args
        xb = x2[tok]
        hb = jax.nn.silu(xb @ w_gate[e]) * (xb @ w_up[e])
        return (hb @ w_down[e]) * g[:, None].astype(x2.dtype)

    y_blocks = lax.map(run_block, (slot_tok.reshape(n_blocks, MOE_BLOCK),
                                   slot_gate.reshape(n_blocks, MOE_BLOCK), block_e))
    return jnp.zeros_like(x2).at[slot_tok].add(y_blocks.reshape(n_slots, -1))

def second_inputs(seed: int = 0) -> dict:
    key = jax.random.key(seed)
    ks = jax.random.split(key, 18)
    f32 = jnp.float32

    def nrm(k, shape, scale):
        return jax.random.normal(k, shape, f32) * scale

    return {
        'x': nrm(ks[0], (BATCH, SEQ, D_MODEL), 1.0),
        'meta_tokens': nrm(ks[1], (N_META, D_MODEL), 1.0),
        'lb_logits': nrm(ks[2], (DEPTH + 1, HG_WIDTH), 0.1).at[-1].add(2.0),
        'g_mix': 1.0 + nrm(ks[3], (DEPTH, D_MODEL), 0.02),
        'w_in': nrm(ks[4], (DEPTH, D_MODEL, IN_PROJ_WIDTH), D_MODEL ** -0.5),
        'sb_gain': 1.0 + nrm(ks[5], (DEPTH, SB_WIDTH), 0.02),
        'hg_gain': 1.0 + nrm(ks[6], (DEPTH, HG_WIDTH), 0.02),
        'w_out': nrm(ks[7], (DEPTH, MIX_WIDTH, D_MODEL), MIX_WIDTH ** -0.5),
        'g_ffn': 1.0 + nrm(ks[8], (DEPTH, D_MODEL), 0.02),
        'w_router_group': nrm(ks[9], (DEPTH, D_MODEL, N_GROUPS), D_MODEL ** -0.5),
        'b_router_group': nrm(ks[10], (DEPTH, N_GROUPS), 0.01),
        'w_router_expert': nrm(ks[11], (DEPTH, D_MODEL, N_EXPERTS_2), D_MODEL ** -0.5),
        'b_router_expert': nrm(ks[12], (DEPTH, N_EXPERTS_2), 0.01),
        'w_expert_gate': nrm(ks[13], (DEPTH, N_EXPERTS_2, D_MODEL, EXPERT_FF), D_MODEL ** -0.5),
        'w_expert_up': nrm(ks[14], (DEPTH, N_EXPERTS_2, D_MODEL, EXPERT_FF), D_MODEL ** -0.5),
        'w_expert_down': nrm(ks[15], (DEPTH, N_EXPERTS_2, EXPERT_FF, D_MODEL), EXPERT_FF ** -0.5),
        'g_final': 1.0 + nrm(ks[16], (D_MODEL,), 0.02),
    }

def second_block(x, meta_tokens, lb_logits, g_mix, w_in, sb_gain, hg_gain, w_out, g_ffn,
              w_router_group, b_router_group, w_router_expert, b_router_expert,
              w_expert_gate, w_expert_up, w_expert_down, g_final):
    b = x.shape[0]
    lead = jnp.zeros((b, LEAD_PAD, D_MODEL), x.dtype)
    meta = jnp.broadcast_to(meta_tokens.astype(x.dtype)[None], (b, N_META, D_MODEL))
    h = jnp.concatenate([lead, meta, x], axis=1)
    L = h.shape[1]
    real = (jnp.arange(L) >= LEAD_PAD)[None, :, None]
    lower_bounds = jnp.cumsum(jax.nn.softmax(lb_logits.astype(jnp.float32), axis=0), axis=0)
    split_idx = np.cumsum(IN_SPLITS)[:-1].tolist()

    for layer in range(DEPTH):
        a = rmsnorm(h, g_mix[layer])
        proj = jnp.einsum('bld,de->ble', a, w_in[layer])
        sb_q, sb_k, sb_v, hg_q, hg_f, hg_i, hg_g = jnp.split(proj, split_idx, axis=-1)

        o_sb = stick_breaking_attention(split_heads(sb_q, SB_HEADS, SB_HEAD_DIM),
                                        split_heads(sb_k, SB_HEADS, SB_HEAD_DIM),
                                        split_heads(sb_v, SB_HEADS, SB_HEAD_DIM))
        o_sb = merge_heads_norm(o_sb, sb_gain[layer]).astype(proj.dtype)

        lb = lower_bounds[layer]
        f_pre = hg_f.astype(jnp.float32)
        log_f = jnp.log(lb + (1.0 - lb) * jax.nn.sigmoid(f_pre))
        k_in = jnp.where(real, (1.0 - lb) * jax.nn.sigmoid(-f_pre), 0.0)
        q_in = jax.nn.silu(hg_q.astype(jnp.float32))
        o_hg = hgrn2_chunked(split_heads(q_in, HG_HEADS, HG_HEAD_DIM),
                             split_heads(k_in, HG_HEADS, HG_HEAD_DIM),
                             split_heads(hg_i.astype(jnp.float32), HG_HEADS, HG_HEAD_DIM),
                             split_heads(log_f, HG_HEADS, HG_HEAD_DIM))
        o_hg = (merge_heads_norm(o_hg, hg_gain[layer]) * jax.nn.silu(hg_g.astype(jnp.float32))).astype(proj.dtype)

        mixed = jnp.concatenate([o_sb, o_hg], axis=-1)
        h = h + jnp.einsum('ble,ed->bld', mixed, w_out[layer])

        m = rmsnorm(h[:, LEAD_PAD:], g_ffn[layer])
        n_pos = m.shape[1]
        y = hierarchical_moe(m.reshape(b * n_pos, D_MODEL), w_router_group[layer], b_router_group[layer],
                             w_router_expert[layer], b_router_expert[layer], w_expert_gate[layer],
                             w_expert_up[layer], w_expert_down[layer])
        h = h + jnp.pad(y.reshape(b, n_pos, D_MODEL), ((0, 0), (LEAD_PAD, 0), (0, 0)))

    out = rmsnorm(h[:, BLOCK:], g_final)
    return out


def setup_inputs(seed=0):
    out = dict(first_inputs(seed))
    for name, value in second_inputs(seed + 1).items():
        if name != "x":
            out[name + "_2"] = value
    return out


def reference(
    x, positions, norm1_g, w_in, sgu_norm_g, sgu_w, sgu_b, w_branch_a, w_branch_b, w_out,
    norm2_g, w_router_group, b_router_group, w_router_expert, b_router_expert, w_expert_in,
    w_expert_out, norm_f_g, meta_tokens_2, lb_logits_2, g_mix_2, w_in_2, sb_gain_2, hg_gain_2,
    w_out_2, g_ffn_2, w_router_group_2, b_router_group_2, w_router_expert_2, b_router_expert_2,
    w_expert_gate_2, w_expert_up_2, w_expert_down_2, g_final_2,
):
    x = first_block(
        x, positions, norm1_g, w_in, sgu_norm_g, sgu_w, sgu_b, w_branch_a, w_branch_b, w_out,
        norm2_g, w_router_group, b_router_group, w_router_expert, b_router_expert, w_expert_in,
        w_expert_out, norm_f_g,
    )
    return second_block(
        x, meta_tokens_2, lb_logits_2, g_mix_2, w_in_2, sb_gain_2, hg_gain_2, w_out_2, g_ffn_2,
        w_router_group_2, b_router_group_2, w_router_expert_2, b_router_expert_2,
        w_expert_gate_2, w_expert_up_2, w_expert_down_2, g_final_2,
    )


_drawn_inputs = setup_inputs


def setup_inputs(seed=0):
    import zlib

    import numpy as np

    out = dict(_drawn_inputs(seed))
    spreads = {}
    factors = {'sgu_norm_g': 3.725,
     'b_router_group': 2.747,
     'sb_gain_2': 10.021,
     'hg_gain_2': 17.275,
     'b_router_group_2': 14.6,
     'b_router_expert_2': 24.56,
     'g_final_2': 7.452,
     'b_router_expert': 6.842,
     'g_ffn_2': 5.787}
    for name, (base, spread) in spreads.items():
        noise = np.random.default_rng([zlib.crc32(name.encode()), seed]).standard_normal(out[name].shape)
        drawn = base * np.exp(spread * noise) if base else spread * noise
        out[name] = __import__('jax').numpy.asarray(drawn.astype(out[name].dtype))
    for name, factor in factors.items():
        out[name] = (out[name] * factor).astype(out[name].dtype)
    return out
```

```python
import concourse.bass as bass
from concourse import mybir
from contextlib import ExitStack
import numpy as np

F32 = mybir.dt.float32
I32 = mybir.dt.int32
U32 = mybir.dt.uint32
ALU = mybir.AluOpType
ACT = mybir.ActivationFunctionType
AX = mybir.AxisListType

P = 128
D = 1024
SEQ = 512
NT = SEQ // P
KC = D // P
HEADS, HD = 8, 128
IH, ID = 8, 64
TOPK = 128
GROUPS = 8
NG, EPG = 4, 8
NE = NG * EPG
SLOTS = 64
OVER = 2 * SEQ // SLOTS - 1
EPS = 1e-6
NEG = -1.0e30
TAKEN = -3.0e38
NT2 = NT + 1
L2 = NT2 * P
META = 16
SBH, SBD = 8, 64
HGH = 4
LEVELS = 7
BANKS = 8
RING = 3
TILE = 4096

CONST_COLS = {}


def constant_table():
    parts = []

    def put(name, a):
        a = np.broadcast_to(np.asarray(a, np.float32), (P, a.shape[-1]))
        start = sum(q.shape[1] for q in parts)
        CONST_COLS[name] = (start, start + a.shape[1])
        parts.append(a)

    i = np.arange(P)
    row, col = i[:, None], i[None, :]
    put("ident", (row == col) * 1.0)
    put("ones", np.ones((P, P)))
    put("tri_ge", (row >= col) * 1.0)
    put("tri_lt", (row < col) * 1.0)
    put("le", (row <= col) * 1.0)
    put("causal", np.where(col <= row, 0.0, NEG))
    put("strict", np.where(row < col, 0.0, NEG))
    put("pad_rows", np.where(row >= P - META, 0.0, NEG)[:, :1])
    put("invf", 10000.0 ** (-np.arange(0, HD, 2, dtype=np.float32) / np.float32(HD))[None, :])
    put("iota_m", (np.arange(NE) - 99.0)[None, :])
    put("iota_e", np.arange(NE)[None, :])
    put("iota_s", (np.arange(NE) * SLOTS)[None, :])
    put("iota_p", i[:, None])
    put("nhalf", np.full((1, 48), -0.5))
    levels = []
    for lv in range(LEVELS):
        h = P >> (lv + 1)
        same = (row // (2 * h)) == (col // (2 * h))
        levels.append((same & ((row // h) % 2 == 0) & ((col // h) % 2 == 1)) * 1.0)
    levels.append((row == col) * 1.0)
    put("levels", np.concatenate(levels, axis=1))
    return np.ascontiguousarray(np.concatenate(parts, axis=1).astype(np.float32))


CONSTANTS = constant_table()


class Units:

    def __init__(self):
        self.index, self.reader = {}, []

    def add(self, key, reader):
        assert key not in self.index, key
        self.index[key] = len(self.reader)
        self.reader.append(reader)

    def bank(self, key):
        return self.index[key] % BANKS

    def filled(self, key):
        return self.index[key] + 1

    def read_count(self, key):
        i = self.index[key]
        who = self.reader[i]
        return who, self.reader[:i + 1].count(who)

    def read_before(self, key):
        old = self.index[key] - BANKS
        if old < 0:
            return None, 0
        who = self.reader[old]
        return who, self.reader[:old + 1].count(who)


def attention_widths():
    starts = [0]
    for t in range(NT):
        starts.append(starts[-1] + (t + 1) * P)
    return starts


CAUSAL_AT = attention_widths()
CAUSAL = CAUSAL_AT[-1]
SCORE_AT = [None] + [a - P for a in CAUSAL_AT[1:NT]]

STREAM1 = (["qi", "sv0", "sv1", "su0", "su1", "ga0", "ga1", "wa0", "wa1", "q0", "q1", "k0", "k1", "v0", "v1",
            "gb0", "gb1", "wb0", "wb1", "wo0", "wo1"])
STREAM2 = ["sbq", "sbk", "sbv", "hi", "hq", "hg", "hf", "wo2_0", "wo2_1"]
PAIRS = NE // 2


def first_block_units():
    u = Units()
    for k in range(KC):
        u.add(("xT", k), "dve")
    for t in range(NT):
        u.add(("qi", t), "dve")
    u.add("kiwi", "dve")
    for t in range(NT):
        u.add(("qiT", t), "act")
    u.add("kiT", "act")
    for t in range(1, NT):
        for h in range(IH):
            u.add(("idx", t, h), "act")
    for n in range(2):
        for t in range(NT):
            u.add(("sv", n, t), "act")
    for name in ("su", "ga"):
        for m in range(KC):
            u.add((name, m), "act")
    for n in range(2):
        u.add(("wT", n), "dve")
    for g in range(GROUPS):
        u.add(("mix", g), "dve")
    for m in range(KC):
        u.add(("wa", m), "dve")
    for n in range(5):
        if n < 4:
            for t in range(NT):
                u.add(("qk", n, t), "dve")
        if n >= 1:
            for t in range(NT):
                u.add(("qkT", n - 1, t), "act")
    for n in range(2):
        for t in range(NT):
            u.add(("v", n, t), "act")
    for h in range(HEADS + 1):
        if h < HEADS:
            for t in range(NT):
                u.add(("S", h, t), "dve")
        if h >= 1:
            for t in range(NT):
                u.add(("T", h - 1, t), "act")
            u.add(("O", h - 1), "act")
    for m in range(KC):
        u.add(("gb", m), "act")
    for m in range(KC):
        u.add(("wb", m), "dve")
    for n in range(2):
        for t in range(NT):
            u.add(("wo", n, t), "dve")
    for k in range(KC):
        u.add(("x2T", k), "dve")
    u.add("router", "dve")
    u.add("ranks", "dve")
    return u


FIRST_T = [max(s, 1) - 1 for s in range(NT2)]
STICK_W = [SEQ - P * f for f in FIRST_T]
STICK_AT = [sum(STICK_W[:s]) for s in range(NT2)]
STICK = sum(STICK_W)


def second_block_units():
    u = Units()
    for n in range(2):
        u.add(("metaT", n), "dve")
    for k in range(KC):
        u.add(("hT", k), "dve")
    for m in range(4):
        u.add(("sbq", m), "act")
    for m in range(4):
        u.add(("sbk", m), "act")
    u.add("sbk_meta", "act")
    for t in range(NT2):
        u.add(("sbv", t), "act")
    for t in range(NT2):
        u.add(("hi", t), "act")
    for m in range(4):
        u.add(("hq", m), "act")
    for t in range(NT):
        u.add(("hg", t), "act")
    for m in range(4):
        u.add(("hf", m), "act")
    u.add("hf_meta", "act")
    for h in range(SBH + 2):
        if h < SBH:
            for s in range(NT2):
                u.add(("Z", h, s), "dve")
        if 1 <= h <= SBH:
            for s in range(NT2):
                u.add(("R", h - 1, s), "dve")
        if h >= 2:
            u.add(("SO", h - 2), "act")
    for h in range(HGH):
        for lv in range(LEVELS):
            if lv == 0:
                u.add(("KT", h), "act")
                u.add(("DG", h), "dve")
            u.add(("L", h, lv), "dve")
            if lv == 2:
                u.add(("KV", h), "dve")
            if lv == 1 and h >= 1:
                u.add(("HO", h - 1), "act")
    u.add(("HO", HGH - 1), "act")
    for k in range(KC):
        u.add(("mT", k), "act")
    for n in range(2):
        for t in range(NT):
            u.add(("wo2", n, t), "dve")
    for k in range(KC):
        u.add(("x2T", k), "dve")
    u.add("router", "dve")
    u.add("ranks", "dve")
    return u


def build(nc, x_in, pos_in, consts_in, g1_in, stream_a, kiwi_in, sgug_in, sguw_in, sgub_in, g2_in, wr_in, br_in,
          we_in, we_out, meta_in_dram, lb_in, gmix_in, stream_b, sbg_in, hgg_in, gffn_in, wr2_in, br2_in,
          wg2_in, wu2_in, wd2_in, gfin_in, gf_in, out, upto=99):
    ctx = ExitStack()
    with ctx:
        def sb(name, shape, dt=F32):
            return ctx.enter_context(nc.sbuf_tensor(name, shape, dt))

        def sem(name):
            return ctx.enter_context(nc.semaphore(name))

        def dram(name, shape, dt=F32):
            return nc.dram_tensor(name, shape, dt, kind="Internal").ap()

        bank = [ctx.enter_context(nc.psum_tensor(f"bank{i}", [P, 512], F32)) for i in range(BANKS)]

        cst = sb("cst", [P, CONSTANTS.shape[1]])
        x = sb("resid", [P, NT, D])
        ring = [sb(f"ring{i}", [P, TILE]) for i in range(RING)]
        arena = sb("arena", [P, 7 * TILE])
        misc = sb("misc", [P, 4096])

        def c(name, rows=P):
            a, b = CONST_COLS[name]
            return cst[0:rows, a:b]

        def at(base, start, shape, dt=F32):
            size = int(np.prod(shape))
            v = base[:, start:start + size]
            if dt is not F32:
                v = v.bitcast(dt)
            if len(shape) == 2:
                v = v.rearrange("p (a b) -> p a b", b=shape[1])
            if len(shape) == 3:
                v = v.rearrange("p (a b c) -> p a b c", b=shape[1], c=shape[2])
            return v

        def big(n, shape):
            return at(arena, n * TILE, shape)

        xnT = big(0, [KC, SEQ])
        xs = big(1, [NT, D])
        vn = big(1, [NT, D])
        suT = big(2, [KC, SEQ])
        gT = big(3, [KC, SEQ])
        sgu_w = at(arena, 4 * TILE, [GROUPS, P])
        wT = at(arena, 4 * TILE + 1024, [GROUPS, P])
        sgu_b = at(arena, 4 * TILE + 2048, [GROUPS, P])
        sgu_g = at(arena, 4 * TILE + 3072, [D])
        scores = at(arena, 5 * TILE, [CAUSAL - P])
        qiT = at(arena, 5 * TILE + 1152, [IH // 2, SEQ])
        kiT = at(arena, 5 * TILE + 3200, [SEQ])
        pT = at(arena, 5 * TILE + 1152, [NT, SEQ])
        rot_a = at(arena, 6 * TILE, [2, 512])
        rot_b = at(arena, 6 * TILE + 1024, [2, 512])
        rot = at(arena, 6 * TILE + 2048, [4, 512])
        yT = big(6, [KC, SEQ])
        qT = big(1, [HEADS, SEQ])
        kT = big(2, [HEADS, SEQ])
        v_rows = big(4, [NT, D])
        gbT = big(1, [KC, SEQ])
        zeros = at(arena, 3 * TILE, [D])
        rel = at(misc, 0, [3, 512])
        probs = [at(misc, 0, [CAUSAL]), at(misc, CAUSAL, [CAUSAL])]
        cos = at(misc, 2560, [NT, HD // 2])
        sin = at(misc, 2816, [NT, HD // 2])
        trig = at(misc, 0, [4, NT * HD // 2])
        kirot = at(misc, 3072, [NT, P])
        kiwi_w = at(arena, 2 * TILE, [KC, 72])
        wi = sb("wi", [P, NT, IH])
        g1 = sb("g1", [P, KC])
        pos_i = sb("pos_i", [P, NT], I32)
        pos_f = sb("pos_f", [P, NT])
        ssq = sb("ssq", [P, 16])
        rstd = sb("rstd", [P, 48])
        top8 = sb("top8", [P, 8])
        bn6 = sb("bn6", [P, NT, 2, 6])
        bn2 = sb("bn2", [P, NT, 2])
        mx = sb("mx", [P, HEADS, NT])
        nm = sb("nm", [P, HEADS, NT])
        sums = sb("sums", [P, HEADS, NT])
        inv = sb("inv", [P, HEADS, NT])

        U = first_block_units()
        def last_unit(name):
            kind, n = (name[:-1], int(name[-1])) if name[-1].isdigit() else (name, 0)
            if kind == "qi":
                return ("qi", NT - 1)
            if kind in ("q", "k"):
                return ("qk", n + 2 * (kind == "k"), NT - 1)
            if kind in ("sv", "v", "wo"):
                return (kind, n, NT - 1)
            return (kind, 4 * n + 3)

        n_stream = {name: n for n, name in enumerate(STREAM1)}

        psum_filled = sem("psum_filled")
        read_by = {"act": sem("bank_read_act"), "dve": sem("bank_read_dve")}
        weights = [sem(f"weights{i}") for i in range(RING)]
        
        consts_in_s = sem("consts_in"); x_in_s = sem("x_in_s"); small_in = sem("small_in"); sgu_in = sem("sgu_in")
        dve_step = sem("dve_step"); act_step = sem("act_step"); pool_step = sem("pool_step")
        sumsq = sem("sumsq"); rms = sem("rms"); scaled = sem("scaled")
        TILES_BEFORE = {"in": 0, "moe0": 4, "out1": 8, "in2": 12, "moe1": 17, "out2": 21}
        ROOTS_BEFORE = {"in": 0, "sgu": 1, "moe0": 2, "out1": 3, "in2": 4, "heads": 5, "moe1": 6, "out2": 7}
        
        angles_ready = sem("angles_ready"); trig_ready = sem("trig_ready")
        rotated = sem("rotated"); 
        
        rel_used = sem("rel_used")
        var_ready = sem("var_ready"); vn_ready = sem("vn_ready")
        vn_scaled = sem("vn_scaled")
        
        gated = sem("gated"); 
        logits_ready = sem("logits_ready"); exp_ready = sem("exp_ready"); probs_ready = sem("probs_ready")
        
        merged = sem("merged"); 
        stored = sem("stored")

        token_id = sb("token_id", [P, NT], I32)
        no_token = sb("no_token", [P, (NE + OVER + 1) * SLOTS // P], I32)
        ids_ready = sem("ids_ready")
        waits_passed = sem("waits_passed")

        def alone(eng):
            eng.sem_inc(waits_passed, 1)

        gather_in = [sem(f"gather_in{j}") for j in range(4)]

        STEPS = 4
        xg_in = [sem(f"xg_in{j}") for j in range(STEPS)]

        class Moe:

            def __init__(self, b, f_chunks, depth):
                self.b, self.F, self.depth = b, f_chunks, depth
                self.xg_base = b * 16 * (NE // STEPS)
                self.tiles, self.roots = TILES_BEFORE[f"moe{b}"], ROOTS_BEFORE[f"moe{b}"]
                self.tr_done = sem(f"tr_done{b}")
                self.h_done = sem(f"h_done{b}")
                self.y_done = sem(f"y_done{b}")
                self.xgT_ready = sem(f"xgT_ready{b}")
                self.sg_ready = sem(f"sg_ready{b}")
                self.act_ready = sem(f"act_ready{b}")
                self.y_free_act = sem(f"y_free_act{b}")
                self.y_free_dve = sem(f"y_free_dve{b}")
                self.routed = sem(f"routed{b}")
                self.rows_stored = sem(f"rows_stored{b}")
                self.router_in = sem(f"router_in{b}")
                self.slots_written = sem(f"slots_written{b}")
                self.table_in = sem(f"table_in{b}")
                self.over_stored = sem(f"over_stored{b}")
                self.over_in = sem(f"over_in{b}")
                self.over_tr = sem(f"over_tr{b}")
                self.over_h = sem(f"over_h{b}")
                self.over_y = sem(f"over_y{b}")
                self.over_xgT = sem(f"over_xgT{b}")
                self.over_sg = sem(f"over_sg{b}")
                self.over_act = sem(f"over_act{b}")
                self.over_y_act = sem(f"over_y_act{b}")
                self.over_y_dve = sem(f"over_y_dve{b}")
                self.table_cleared = sem(f"table_cleared{b}")
                self.rows_cleared = sem(f"rows_cleared{b}")
                self.moe_added = sem(f"moe_added{b}")
                self.index_copied = sem(f"index_copied{b}")
                self.exp_in = sem(f"exp_in{b}")
                self.exp_out = sem(f"exp_out{b}")
                self.normed = sem(f"normed{b}")
                self.y_stored = [sem(f"y_stored{b}_{j}") for j in range(2)]
                slots = [big(4 + i, [TILE]) for i in range(3)] + [r[:, :] for r in ring]
                if b == 0:
                    half = TILE // 2
                    self.places = [(slots[(0, 1, 3, 4)[j]], slots[(2, 2, 5, 5)[j]][:, (j % 2) * half:(j % 2 + 1) * half])
                                   for j in range(4)]
                else:
                    self.places = [tuple(slots[3 * j:3 * j + 3]) for j in range(2)]
                self.sources = (we_in, we_out) if b == 0 else (wg2_in, wu2_in, wd2_in)
                self.tile_in = [[sem(f"tile_in{b}_{j}_{i}") for i in range(len(self.places[0]))] for j in range(depth)]
                self.over_tile = [sem(f"over_tile{b}_{i}") for i in range(len(self.places[0]))]
                self.slot_token = dram(f"slot_token{b}", [(NE + OVER + 1) * SLOTS, 1], I32)
                self.xn_rows = dram(f"xn_rows{b}", [SEQ, D])
                self.y_rows = dram(f"y_rows{b}", [(NE + OVER + 1) * SLOTS, D])
                self.xg = big(1, [STEPS, D])
                self.xgT = at(arena, 2048, [2, KC, SLOTS])
                self.sg = at(arena, 3072, [2, 4 * SLOTS])
                self.actT = at(arena, 3584, [2, 4, SLOTS])
                self.y = at(arena, 0, [2, D])
                self.rows = big(1, [NT, D])
                self.xnT = big(2, [KC, SEQ])
                self.gathered = big(2, [4, D])
                self.gain = at(arena, 3 * TILE, [D])
                self.wr = at(arena, 3 * TILE + 1024, [KC, NG + NE])
                self.br = at(arena, 3 * TILE + 1312, [NG + NE])
                self.inputs = (g2_in, wr_in, br_in) if b == 0 else (gffn_in, wr2_in, br2_in)
                self.gates = sb(f"gates{b}", [P, 2, NT])
                self.slot_at = sb(f"slot_at{b}", [P, 2 * NT], I32)
                self.row_at = sb(f"row_at{b}", [P, 2 * NT], I32)
                self.over = sb(f"over{b}", [P, 16], I32)
                self.table = sb(f"table{b}", [SLOTS, NE], I32)
                self.index = sb(f"index{b}", [SLOTS, STEPS], I32)

            def tile_value(self, it, j):
                return it * (16 * STEPS // self.depth) + 16 * (j // self.depth + 1)

        moes = [Moe(0, 2, 4), Moe(1, 4, 2)]

        def moe_gate_up(pe, m, j, parity, done):
            for part in range(2):
                h = bank[2 + 2 * part + parity]
                if part == 1 and m.b == 1:
                    moe_wait(pe, m, j, 1)
                for f in range(m.F):
                    col = f * SLOTS
                    for k in range(KC):
                        if m.b == 0:
                            w = m.places[j % m.depth][0][:, k * 512 + (part * m.F + f) * P:k * 512 + (part * m.F + f + 1) * P]
                        else:
                            w = m.places[j % m.depth][part][:, k * 512 + f * P:k * 512 + (f + 1) * P]
                        last = nc.tensor.matmul(h[:, col:col + SLOTS], w, m.xgT[:, parity, k, :],
                                                start=(k == 0), stop=(k == KC - 1))
                last.then_inc(done, 1)

        def moe_down(m, j, parity, done):
            w = m.places[j % m.depth][-1]
            for n in range(2):
                for f in range(m.F):
                    last = nc.tensor.matmul(bank[6 + n][0:SLOTS, :], m.actT[:, parity, f, :],
                                            w[:, f * D + n * 512:f * D + n * 512 + 512],
                                            start=(f == 0), stop=(f == m.F - 1))
                last.then_inc(done, 1)

        def moe_transposes(m, j, done):
            for k in range(KC):
                last = nc.tensor.transpose(bank[j % 2][:, k * SLOTS:(k + 1) * SLOTS],
                                           m.xg[0:SLOTS, j, k * P:(k + 1) * P], c("ident", SLOTS)[:, 0:SLOTS])
            last.then_inc(done, 1)

        moe_expect = {}

        def moe_wait(pe, m, j, i):
            pe.wait_ge(*moe_expect[m.b, j, i])

        def moe_sp(sp, m, gates):
            b, n_tiles = m.b, len(m.places[0])

            def load(e, j, i):
                src = m.sources[i][bass.ds(e, 1), :, :].rearrange("e p c -> p (e c)") if not isinstance(e, int) \
                    else m.sources[i][e, :, :]
                sp.dma_start(m.places[j][i], src).then_inc(m.tile_in[j][i], 16)

            for j in range(m.depth):
                for i in range(n_tiles):
                    gates(b, j, i)
                    load(j, j, i)
            with sp.Fori(0, NE // m.depth - 1) as it:
                for j in range(m.depth):
                    for i in range(n_tiles):
                        done = m.y_done if i == n_tiles - 1 else m.h_done
                        gate_only = b == 1 and i == 0
                        sp.wait_ge(done, it * (2 * m.depth) + (2 * j + (1 if gate_only else 2)))
                        load(it * m.depth + (m.depth + j), j, i)
            alone(sp)
            n_over = sp.value_load(m.over[0:1, 0:1], min_val=0, max_val=OVER)
            with sp.Fori(0, OVER) as v:
                with sp.If(v < n_over):
                    sp.wait_ge(m.y_done, 2 * NE)
                    e = sp.value_load(m.over[0:1, bass.ds(v + 1, 1)], min_val=0, max_val=NE - 1)
                    for i in range(n_tiles):
                        src = m.sources[i][bass.ds(e, 1), :, :].rearrange("e p c -> p (e c)")
                        sp.dma_start(m.places[0][i], src).then_inc(m.over_tile[i], 16)
                    sp.wait_ge(m.over_y_act, v + 1)
                    sp.wait_ge(m.over_y_dve, v + 1)
                    sp.dma_start(m.y_rows[bass.ds(v * SLOTS + NE * SLOTS, SLOTS), :], m.y[0:SLOTS, 0, :])\
                        .then_inc(m.over_stored, 16)
                    sp.wait_ge(m.over_stored, v * 16 + 16)
                    alone(sp)

        def moe_pe(pe, m):
            pe.sem_inc(m.tr_done, STEPS)
            pe.wait_ge(xg_in[0], m.xg_base + 16)
            moe_transposes(m, 0, m.tr_done)

            def experts(it, is_last):
                for j in range(STEPS):
                    q = j % 2
                    pe.wait_ge(m.tile_in[j % m.depth][0], m.tile_value(it, j))
                    moe_expect[m.b, j, 1] = (m.tile_in[j % m.depth][1], m.tile_value(it, j))
                    pe.wait_ge(m.xgT_ready, it * STEPS + (j + 1))
                    moe_gate_up(pe, m, j, q, m.h_done)
                    if not (is_last and j == STEPS - 1):
                        pe.wait_ge(xg_in[(j + 1) % STEPS], it * 16 + (m.xg_base + 16 * (1 + (j + 1) // STEPS)))
                        alone(pe)
                        moe_transposes(m, (j + 1) % STEPS, m.tr_done)
                    pe.wait_ge(m.tile_in[j % m.depth][-1], m.tile_value(it, j))
                    pe.wait_ge(m.act_ready, it * STEPS + (j + 1))
                    pe.wait_ge(m.y_free_act, it * STEPS + (j + 1))
                    pe.wait_ge(m.y_free_dve, it * STEPS + (j + 1))
                    moe_down(m, j, q, m.y_done)

            with pe.Fori(0, NE // STEPS - 1) as it:
                experts(it, False)
            experts(NE // STEPS - 1, True)
            n_over = pe.value_load(m.over[0:1, 0:1], min_val=0, max_val=OVER)
            with pe.Fori(0, OVER) as v:
                with pe.If(v < n_over):
                    pe.wait_ge(m.y_free_act, NE + 1)
                    pe.wait_ge(m.y_free_dve, NE + 1)
                    pe.wait_ge(m.over_in, v * 32 + 32)
                    alone(pe)
                    moe_transposes(m, 0, m.over_tr)
                    pe.wait_ge(m.over_tile[0], v * 16 + 16)
                    moe_expect[m.b, 0, 1] = (m.over_tile[1], v * 16 + 16)
                    pe.wait_ge(m.over_xgT, v + 1)
                    moe_gate_up(pe, m, 0, 0, m.over_h)
                    pe.wait_ge(m.over_tile[-1], v * 16 + 16)
                    pe.wait_ge(m.over_act, v + 1)
                    moe_down(m, 0, 0, m.over_y)
                    pe.wait_ge(m.over_y_act, v + 1)
                    pe.wait_ge(m.over_y_dve, v + 1)
                    alone(pe)

        def moe_act(act, m):
            w = m.F * SLOTS
            act.sem_inc(m.y_free_act, 1)
            for q in range(2):
                act.sem_inc(m.y_stored[q], 16)
            with act.Fori(0, NE // STEPS) as it:
                for j in range(STEPS):
                    q = j % 2
                    act.wait_ge(m.h_done, it * (2 * STEPS) + (2 * j + 1))
                    nc.scalar.activation(m.sg[:, q, 0:w], bank[2 + q][:, 0:w], ACT.Silu).then_inc(m.sg_ready, 1)
                    act.wait_ge(m.y_done, it * (2 * STEPS) + (2 * j + 1))
                    act.wait_ge(m.y_stored[q], it * (8 * STEPS) + 16 * (j // 2 + 1))
                    nc.scalar.copy(m.y[0:SLOTS, q, 0:512], bank[6][0:SLOTS, :]).then_inc(m.y_free_act, 1)
                    act.wait_ge(m.y_free_act, it * STEPS + (j + 2))
                    act.wait_ge(m.y_free_dve, it * STEPS + (j + 2))
                    act.dma_start(m.y_rows[bass.ds(it * (STEPS * SLOTS) + j * SLOTS, SLOTS), :],
                                  m.y[0:SLOTS, q, :]).then_inc(m.y_stored[q], 16)
            n_over = act.value_load(m.over[0:1, 0:1], min_val=0, max_val=OVER)
            with act.Fori(0, OVER) as v:
                with act.If(v < n_over):
                    act.wait_ge(m.y_stored[0], 8 * NE + 16)
                    act.wait_ge(m.over_h, v * 2 + 1)
                    nc.scalar.activation(m.sg[:, 0, 0:w], bank[2][:, 0:w], ACT.Silu).then_inc(m.over_sg, 1)
                    act.wait_ge(m.over_y, v * 2 + 1)
                    nc.scalar.copy(m.y[0:SLOTS, 0, 0:512], bank[6][0:SLOTS, :]).then_inc(m.over_y_act, 1)
                    act.wait_ge(m.over_stored, v * 16 + 16)
                    alone(act)

        def moe_dve(dve, m, then):
            V, w = nc.vector, m.F * SLOTS
            dve.sem_inc(m.y_free_dve, 1)

            def hidden(q, ready):
                V.tensor_tensor(m.actT[:, q, 0:m.F, :].rearrange("p f s -> p (f s)"), m.sg[:, q, 0:w],
                                bank[4 + q][:, 0:w], ALU.mult).then_inc(ready, 1)

            def tokens(e, q):
                dve.wait_ge(m.tr_done, e)
                V.tensor_copy(m.xgT[:, q, :, :].rearrange("p k s -> p (k s)"), bank[q][:, :])\
                    .then_inc(m.xgT_ready, 1)

            def experts(it, is_last):
                for j in range(STEPS):
                    q = j % 2
                    dve.wait_ge(m.h_done, it * (2 * STEPS) + (2 * j + 2))
                    dve.wait_ge(m.sg_ready, it * STEPS + (j + 1))
                    hidden(q, m.act_ready)
                    if not (is_last and j == STEPS - 1):
                        tokens(it * STEPS + (STEPS + j + 2), 1 - q)
                    dve.wait_ge(m.y_done, it * (2 * STEPS) + (2 * j + 2))
                    dve.wait_ge(m.y_stored[q], it * (8 * STEPS) + 16 * (j // 2 + 1))
                    V.tensor_copy(m.y[0:SLOTS, q, 512:1024], bank[7][0:SLOTS, :]).then_inc(m.y_free_dve, 1)

            tokens(STEPS + 1, 0)
            with dve.Fori(0, NE // STEPS - 1) as it:
                experts(it, False)
            experts(NE // STEPS - 1, True)
            n_over = dve.value_load(m.over[0:1, 0:1], min_val=0, max_val=OVER)
            with dve.Fori(0, OVER) as v:
                with dve.If(v < n_over):
                    dve.wait_ge(m.y_stored[0], 8 * NE + 16)
                    dve.wait_ge(m.over_tr, v + 1)
                    V.tensor_copy(m.xgT[:, 0, :, :].rearrange("p k s -> p (k s)"), bank[0][:, :])\
                        .then_inc(m.over_xgT, 1)
                    dve.wait_ge(m.over_h, v * 2 + 2)
                    dve.wait_ge(m.over_sg, v + 1)
                    hidden(0, m.over_act)
                    dve.wait_ge(m.over_y, v * 2 + 2)
                    V.tensor_copy(m.y[0:SLOTS, 0, 512:1024], bank[7][0:SLOTS, :]).then_inc(m.over_y_dve, 1)
                    dve.wait_ge(m.over_stored, v * 16 + 16)
                    alone(dve)
            for n in range(2 * NT):
                k, t = n % 2, n // 2
                dve.wait_ge(gather_in[n % 4], 16 * (n // 4 + 1) + 32 * m.b)
                if k == 1:
                    dve.wait_ge(m.moe_added, n)
                V.scalar_tensor_tensor(x[:, t, :], m.gathered[:, n % 4, :], m.gates[:, k, t:t + 1], x[:, t, :],
                                       ALU.mult, ALU.add).then_inc(m.moe_added, 1)

        def moe_pool(pool, m):
            G = nc.gpsimd
            pool.wait_ge(m.routed, 1)
            pool.wait_ge(m.table_cleared, 16)
            for n in range(2 * NT):
                G.indirect_dma_start(m.slot_token[:, :], bass.IndirectOffsetOnAxis(ap=m.slot_at[:, n:n + 1], axis=0),
                                     token_id[:, n % NT:n % NT + 1], None).then_inc(m.slots_written, 16)
            pool.wait_ge(m.slots_written, 16 * 2 * NT)
            pool.dma_start(m.table[:, :], m.slot_token[0:NE * SLOTS, :].rearrange("(s e) o -> s (e o)", e=NE))\
                .then_inc(m.table_in, 16)
            pool.wait_ge(m.table_in, 16)
            pool.wait_ge(m.rows_stored, 16 * NT)
            with pool.Fori(0, NE // STEPS) as it:
                for j in range(STEPS):
                    pool.wait_ge(m.tr_done, it * STEPS + (j + 1))
                    G.tensor_copy(m.index[:, j:j + 1], m.table[:, bass.ds(it * STEPS + j, 1)])\
                        .then_inc(m.index_copied, 1)
                    pool.wait_ge(m.index_copied, it * STEPS + (j + 1))
                    alone(pool)
                    G.indirect_dma_start(m.xg[0:SLOTS, j, :], None, m.xn_rows[:, :],
                                         bass.IndirectOffsetOnAxis(ap=m.index[:, j:j + 1], axis=0))\
                        .then_inc(xg_in[j], 16)
            n_over = pool.value_load(m.over[0:1, 0:1], min_val=0, max_val=OVER)
            with pool.Fori(0, OVER) as v:
                with pool.If(v < n_over):
                    pool.wait_ge(m.tr_done, NE + STEPS)
                    pool.dma_start(m.index[:, 0:1], m.slot_token[bass.ds(v * SLOTS + NE * SLOTS, SLOTS), :])\
                        .then_inc(m.over_in, 16)
                    pool.wait_ge(m.over_in, v * 32 + 16)
                    alone(pool)
                    G.indirect_dma_start(m.xg[0:SLOTS, 0, :], None, m.xn_rows[:, :],
                                         bass.IndirectOffsetOnAxis(ap=m.index[:, 0:1], axis=0))\
                        .then_inc(m.over_in, 16)
                    pool.wait_ge(m.over_stored, v * 16 + 16)
                    alone(pool)
            for q in range(2):
                pool.wait_ge(m.y_stored[q], 8 * NE + 16)
            for n in range(2 * NT):
                k, t = n % 2, n // 2
                if n >= 4:
                    pool.wait_ge(m.moe_added, n - 3)
                G.indirect_dma_start(m.gathered[:, n % 4, :], None, m.y_rows[:, :],
                                     bass.IndirectOffsetOnAxis(ap=m.row_at[:, k * NT + t:k * NT + t + 1], axis=0))\
                    .then_inc(gather_in[n % 4], 16)

        def norm_act(act, m, ready):
            for t in range(NT):
                ready(act, t)
                nc.scalar.activation(m.rows[:, t, :], x[:, t, :], ACT.Square, accum_out=ssq[:, t:t + 1])\
                    .then_inc(sumsq, 1)
            act.wait_ge(rms, m.roots + 1)
            act.wait_ge(sumsq, m.tiles + NT)
            for t in range(NT):
                nc.scalar.activation(m.rows[:, t, :], x[:, t, :], ACT.Copy, scale=rstd[:, t:t + 1])\
                    .then_inc(scaled, 1)

        def norm_pool(pool, m, then):
            G = nc.gpsimd
            pool.wait_ge(sumsq, m.tiles + NT)
            then(G.tensor_scalar(rstd[:, 0:NT], ssq[:, 0:NT], 1.0 / D, EPS, ALU.mult, ALU.add))
            G.tensor_tensor(rstd[:, 0:NT], rstd[:, 0:NT], c("nhalf")[:, 0:NT], ALU.pow).then_inc(rms, 1)

        def router_sp(sp, m):
            for t in range(NT):
                sp.wait_ge(m.normed, t + 1)
                sp.dma_start(m.xn_rows[t * P:(t + 1) * P, :], m.rows[:, t, :]).then_inc(m.rows_stored, 16)

        def router_pe(pe, m, U, begin, end, transposes, wait_read):
            pe.wait_ge(m.normed, NT)
            for k in range(KC):
                transposes(("x2T", k), [m.rows[:, t, k * P:(k + 1) * P] for t in range(NT)])
            pe.wait_ge(m.router_in, 48)
            wait_read(pe, ("x2T", KC - 1))
            r = begin("router")
            w = NG + NE
            for t in range(NT):
                for k in range(KC):
                    last = nc.tensor.matmul(r[:, t * w:(t + 1) * w], m.xnT[:, k, t * P:(t + 1) * P], m.wr[:, k, :],
                                            start=(k == 0), stop=(k == KC - 1))
            end(last)
            pe.wait_ge(m.exp_in, 2)
            r = begin("ranks")
            chosen = at(arena, 3 * TILE + 3584, [NT, NE])
            for t in range(NT):
                for s in range(t + 1):
                    last = nc.tensor.matmul(r[:, t * NE:(t + 1) * NE], c("tri_lt") if s == t else c("ones"),
                                            chosen[:, s, :], start=(s == 0), stop=(s == t))
            for s in range(NT):
                last = nc.tensor.matmul(r[:, NT * NE:(NT + 1) * NE], c("ones"), chosen[:, s, :],
                                        start=(s == 0), stop=(s == NT - 1))
            end(last)

        def router_act(act, m):
            act.wait_ge(m.exp_in, 1)
            nc.scalar.activation(m.ework[0], m.ework[0], ACT.Exp).then_inc(m.exp_out, 1)
            act.wait_ge(m.exp_in, 2)
            nc.scalar.activation(m.ework[1], m.ework[1], ACT.Exp).then_inc(m.exp_out, 1)

        for m in moes:
            m.ework = (at(arena, 3 * TILE + 3400, [NT, NG]), at(arena, 3 * TILE + 3416, [NT]))

        def router_dve(dve, m, unit, read, then, wait_read):
            V = nc.vector
            at3 = [3 * TILE + 1408]

            def tmp(*shape):
                v = at(arena, at3[0], list(shape))
                at3[0] += int(np.prod(shape))
                assert at3[0] <= 3 * TILE + 3400
                return v

            dve.wait_ge(m.router_in, 48)
            for t in range(NT):
                dve.wait_ge(scaled, m.tiles + t + 1)
                V.tensor_tensor(m.rows[:, t, :], m.rows[:, t, :], m.gain, ALU.mult).then_inc(m.normed, 1)
            for k in range(KC):
                b = unit(("x2T", k))
                read(V.tensor_copy(m.xnT[:, k, :], b[:, :]))
            w = NG + NE
            logits = tmp(NT, w)
            b = unit("router")
            read(V.tensor_tensor(logits, b[:, 0:NT * w].rearrange("p (t w) -> p t w", w=w),
                                 m.br[:, None, :].broadcast_to([P, NT, w]), ALU.add))
            wait_read(dve, "router")
            gl, el = logits[:, :, 0:NG], logits[:, :, NG:w]

            def bc(v, n):
                return v[:, :, None].broadcast_to([P, NT, n])

            def first_max(values, n):
                best, hit, low = tmp(NT), tmp(NT, n), tmp(NT)
                then(V.tensor_reduce(best, values, AX.X, ALU.max))
                then(V.tensor_tensor(hit, values, bc(best, n), ALU.is_equal))
                then(V.tensor_tensor(hit, hit, c("iota_m")[:, None, 0:n].broadcast_to([P, NT, n]), ALU.mult))
                then(V.tensor_reduce(low, hit, AX.X, ALU.min))
                then(V.tensor_tensor(hit, hit, bc(low, n), ALU.is_equal))
                return best, hit

            gbest, ghit = first_max(gl, NG)
            V.tensor_tensor(m.ework[0], gl, bc(gbest, NG), ALU.subtract).then_inc(m.exp_in, 1)
            off = tmp(NT, NG)
            then(V.tensor_scalar(off, ghit, -NEG, NEG, ALU.mult, ALU.add))
            em = tmp(NT, NE)
            split = dict(g=NG, e=EPG)
            then(V.tensor_tensor(em.rearrange("p t (g e) -> p t g e", **split),
                                 el.rearrange("p t (g e) -> p t g e", **split),
                                 off[:, :, :, None].broadcast_to([P, NT, NG, EPG]), ALU.add))
            best1, hit1 = first_max(em, NE)
            then(V.scalar_tensor_tensor(em, hit1, 3 * NEG, em, ALU.mult, ALU.add))
            best2, hit2 = first_max(em, NE)
            chosen = at(arena, 3 * TILE + 3584, [NT, NE])
            then(V.tensor_tensor(chosen, hit1, hit2, ALU.add))
            V.tensor_tensor(m.ework[1], best2, best1, ALU.subtract).then_inc(m.exp_in, 1)
            dve.wait_ge(m.exp_out, 2)
            gsum, den = tmp(NT), tmp(NT)
            then(V.tensor_reduce(gsum, m.ework[0], AX.X, ALU.add))
            then(V.tensor_scalar(den, m.ework[1], 1.0, None, ALU.add))
            then(V.tensor_tensor(den, den, gsum, ALU.mult))
            then(V.reciprocal(m.gates[:, 0, :], den))
            then(V.tensor_tensor(m.gates[:, 1, :], m.gates[:, 0, :], m.ework[1], ALU.mult))
            rk = tmp(NT + 1, NE)
            b = unit("ranks")
            read(V.tensor_copy(rk, b[:, 0:(NT + 1) * NE].rearrange("p (t e) -> p t e", e=NE)))
            wait_read(dve, "ranks")
            ranks, counts = rk[:, 0:NT, :], rk[:, NT, :]
            more, upto_, before = tmp(NE), tmp(NE), tmp(NE)
            then(V.tensor_scalar(more, counts, float(SLOTS), None, ALU.is_gt))
            for n in range(2, SEQ // SLOTS):
                then(V.scalar_tensor_tensor(more, counts, float(n * SLOTS), more, ALU.is_gt, ALU.add))
            then(V.tensor_tensor_scan(upto_, c("ones")[:, 0:NE], more, 0.0, ALU.mult, ALU.add))
            then(V.tensor_tensor(before, upto_, more, ALU.subtract))
            then(V.tensor_scalar(before, before, float(SLOTS), float((NE - 1) * SLOTS), ALU.mult, ALU.add))
            isover, far = tmp(NT, NE), tmp(NT, NE)
            then(V.tensor_scalar(isover, ranks, float(SLOTS), None, ALU.is_ge))
            then(V.tensor_tensor(far, ranks, before[:, None, :].broadcast_to([P, NT, NE]), ALU.add))
            for (table, near_scale, iota) in ((m.slot_at, float(NE), "iota_e"), (m.row_at, 1.0, "iota_s")):
                near, pick = tmp(NT, NE), tmp(NT)
                then(V.tensor_scalar(near, ranks, near_scale, None, ALU.mult))
                then(V.tensor_tensor(near, near, c(iota)[:, None, :].broadcast_to([P, NT, NE]), ALU.add))
                d = tmp(NT, NE)
                then(V.tensor_tensor(d, far, near, ALU.subtract))
                then(V.tensor_tensor(d, d, isover, ALU.mult))
                then(V.tensor_tensor(near, near, d, ALU.add))
                for k, hit in ((0, hit1), (1, hit2)):
                    then(V.tensor_tensor(d, near, hit, ALU.mult))
                    then(V.tensor_reduce(pick, d, AX.X, ALU.add))
                    then(V.tensor_copy(table[:, k * NT:(k + 1) * NT], pick))
            owner, le = tmp(16), at(misc, 0, [16, NE])
            then(V.tensor_tensor(le, upto_[:, None, :].broadcast_to([P, 16, NE]),
                                 c("iota_e")[:, 0:16, None].broadcast_to([P, 16, NE]), ALU.is_le))
            then(V.tensor_reduce(owner, le, AX.X, ALU.add))
            then(V.tensor_scalar(owner, owner, float(NE - 1), None, ALU.min))
            then(V.tensor_copy(m.over[:, 1:16], owner[:, 0:15]))
            V.tensor_copy(m.over[:, 0:1], upto_[:, NE - 1:NE]).then_inc(m.routed, 1)

        def moe_gates_0(sp):
            def gate(b, j, i):
                place = {0: 0, 1: 1, 2: 4, 3: 5}[j] if i == 0 else 2 if j < 2 else 5
                if place <= 3:
                    sp.wait_ge(psum_filled, U.filled(("wb", KC - 1)))
                else:
                    sp.wait_ge(psum_filled, U.filled(("wo", place - 4, NT - 1)))
            return gate

        U2 = second_block_units()
        n_stream2 = {name: n for n, name in enumerate(STREAM2)}
        psum_filled2 = sem("psum_filled2")
        read_by2 = {"act": sem("bank_read2_act"), "dve": sem("bank_read2_dve")}
        weights2 = [sem(f"weights2_{i}") for i in range(RING)]
        block2_in = sem("block2_in")
        meta_cleared = sem("meta_cleared"); meta_in = sem("meta_in")
        x_normed = sem("x_normed")
        lb_out = sem("lb_out"); lb_exp = sem("lb_exp")
        decay_ready = sem("decay_ready"); last_ready = sem("last_ready"); keys_ready = sem("keys_ready")
        z_ready = sem("z_ready"); log_ready = sem("log_ready"); sp_ready = sem("sp_ready")
        weight_ready = sem("weight_ready"); carried = sem("carried"); log_f_ready = sem("log_f_ready")
        diff_ready = sem("diff_ready"); diff_exp = sem("diff_exp"); level_ready = sem("level_ready")
        kd_exp = sem("kd_exp"); kd_ready = sem("kd_ready"); q_exp = sem("q_exp"); q_ready = sem("q_ready")
        scores_ready = sem("scores_ready"); states_ready = sem("states_ready")
        squares_ready = sem("squares_ready"); heads_normed = sem("heads_normed")
        result = sem("result")

        base2 = 5376
        hT = at(arena, 0, [KC, L2])
        xs2 = at(arena, base2, [NT2, D])
        hv = at(arena, base2, [NT2, HGH * HD])
        sbv = at(arena, base2 + 2560, [NT2, SBH * SBD])
        sbq = at(arena, base2 + 5120, [4, SEQ])
        sbk = at(arena, base2 + 7168, [4, L2])
        hq = at(arena, base2 + 9728, [HGH, SEQ])
        hk = at(arena, base2 + 11776, [HGH, L2])
        bc = at(arena, base2 + 14336, [HGH, L2])
        hgate = at(arena, base2 + 16896, [NT, HGH * HD])
        mixed = at(arena, base2 + 18944, [NT, D])
        assert base2 + 18944 + NT * D <= 7 * TILE
        mixedT = at(arena, 0, [KC, SEQ])
        zw = [at(arena, i * STICK, [STICK]) for i in range(3)]
        sps = [ring[0][:, i * STICK:(i + 1) * STICK] for i in range(2)]
        diff = at(arena, 0, [2, SEQ]); qE = at(arena, 1024, [2, SEQ]); kE = at(arena, 2048, [2, SEQ])
        hsc = at(arena, 3072, [2, SEQ]); qexp = at(arena, 4096, [2, SEQ])
        kd = at(ring[0], 0, [2, SEQ]); kdR = at(ring[0], 1024, [2, SEQ])
        states = at(ring[0], 2048, [2, NT, P])
        squares = at(arena, 0, [NT, D])
        sb_gain = at(misc, 0, [512]); hg_gain = at(misc, 512, [512])
        gf = at(misc, 1024, [D])
        meta = at(misc, 2048, [D])
        chunk_decay = sb("chunk_decay", [P, HGH, NT2])
        gmix = sb("gmix", [P, KC])
        lbl = sb("lbl", [P, 2, HGH]); lb = sb("lb", [P, HGH]); oml = sb("oml", [P, HGH]); lbm = sb("lbm", [P, HGH])

        def last_unit2(name):
            if name in ("sbq", "hq"):
                return (name, 3)
            if name in ("sbk", "hf"):
                return name + "_meta"
            if name in ("sbv", "hi"):
                return (name, NT2 - 1)
            return (name, NT - 1) if name == "hg" else ("wo2", int(name[-1]), NT - 1)

        def wait_read2(eng, key):
            who, reads = U2.read_count(key)
            eng.wait_ge(read_by2[who], reads)

        block = ctx.enter_context(nc.Block())

        def wait_read(eng, key):
            who, reads = U.read_count(key)
            eng.wait_ge(read_by[who], reads)

        linked = {"dve": 0, "act": 0, "pool": 0}

        def link(name, eng, step, ins):
            linked[name] += 1
            ins.then_inc(step, 1)
            eng.wait_ge(step, linked[name])

        @block.sync
        def _(sp):
            sp.dma_start(x[:, :, :], x_in.rearrange("(t p) d -> p t d", p=P)).then_inc(x_in_s, 16)
            sp.dma_start(cst[:, :], consts_in).then_inc(consts_in_s, 16)
            sp.dma_start(g1[:, :], g1_in).then_inc(small_in, 16)
            sp.dma_start(pos_i[:, :], pos_in).then_inc(small_in, 16)
            sp.dma_start(kiwi_w[:, :, :], kiwi_in.rearrange("p (k c) -> p k c", c=72)).then_inc(small_in, 16)
            sp.dma_start(sgu_w[:, :, :], sguw_in.rearrange("g t s -> t g s")).then_inc(sgu_in, 16)
            sp.dma_start(sgu_b[:, :, :], sgub_in[None, :, :].broadcast_to([P, GROUPS, P])).then_inc(sgu_in, 16)
            sp.dma_start(sgu_g[:, :], sgug_in.broadcast_to([P, D])).then_inc(sgu_in, 16)
            sp.wait_ge(ids_ready, 3)
            for m in moes:
                sp.dma_start(m.slot_token.rearrange("(p n) o -> p (n o)", p=P), no_token[:, :])\
                    .then_inc(m.table_cleared, 16)
                for n in range((OVER + 1) * SLOTS // P):
                    row = NE * SLOTS + n * P
                    sp.dma_start(m.y_rows[row:row + P, :], zeros).then_inc(m.rows_cleared, 16)
            for n in range(len(STREAM1)):
                if n >= RING:
                    sp.wait_ge(psum_filled, U.filled(last_unit(STREAM1[n - RING])))
                sp.dma_start(ring[n % RING][:, :], stream_a[n, :, :]).then_inc(weights[n % RING], 16)
            m = moes[0]
            sp.wait_ge(psum_filled, U.filled(("wo", 1, NT - 1)))
            sp.dma_start(m.gain, m.inputs[0].broadcast_to([P, D])).then_inc(m.router_in, 16)
            sp.dma_start(m.wr, m.inputs[1].rearrange("p (k c) -> p k c", k=KC)).then_inc(m.router_in, 16)
            sp.dma_start(m.br, m.inputs[2].broadcast_to([P, NG + NE])).then_inc(m.router_in, 16)
            router_sp(sp, m)
            moe_sp(sp, m, moe_gates_0(sp))

            sp.wait_ge(m.routed, 1)
            sp.dma_start(sb_gain, sbg_in.broadcast_to([P, 512])).then_inc(block2_in, 16)
            sp.dma_start(hg_gain, hgg_in.broadcast_to([P, 512])).then_inc(block2_in, 16)
            sp.dma_start(gf, gf_in.broadcast_to([P, D])).then_inc(block2_in, 16)
            sp.dma_start(gmix[:, :], gmix_in).then_inc(block2_in, 16)
            sp.dma_start(lbl[:, :, :], lb_in.rearrange("p (r h) -> p r h", r=2)).then_inc(block2_in, 16)
            sp.wait_ge(meta_cleared, 1)
            sp.dma_start(meta[P - META:P, :], meta_in_dram).then_inc(meta_in, 16)
            sp.wait_ge(m.y_done, 2 * NE)
            for n in range(len(STREAM2)):
                if n >= RING:
                    sp.wait_ge(psum_filled2, U2.filled(last_unit2(STREAM2[n - RING])))
                sp.dma_start(ring[n % RING][:, :], stream_b[n, :, :]).then_inc(weights2[n % RING], 16)
            m = moes[1]
            sp.wait_ge(psum_filled2, U2.filled(("wo2", 1, NT - 1)))
            sp.dma_start(m.gain, m.inputs[0].broadcast_to([P, D])).then_inc(m.router_in, 16)
            sp.dma_start(m.wr, m.inputs[1].rearrange("p (k c) -> p k c", k=KC)).then_inc(m.router_in, 16)
            sp.dma_start(m.br, m.inputs[2].broadcast_to([P, NG + NE])).then_inc(m.router_in, 16)
            router_sp(sp, m)
            moe_sp(sp, m, lambda b, j, i: None)
            sp.wait_ge(m.routed, 1)
            sp.dma_start(gf, gfin_in.broadcast_to([P, D])).then_inc(block2_in, 16)
            for t in range(NT):
                sp.wait_ge(result, t + 1)
                sp.dma_start(out[0, t * P:(t + 1) * P, :], x[:, t, :]).then_inc(stored, 16)
            sp.wait_ge(stored, 16 * NT)

        @block.tensor
        def _(pe):
            def begin(key, w=512):
                who, reads = U.read_before(key)
                if who:
                    pe.wait_ge(read_by[who], reads)
                return bank[U.bank(key)]

            def end(ins):
                ins.then_inc(psum_filled, 1)

            def weight(name):
                n = n_stream[name]
                pe.wait_ge(weights[n % RING], 16 * (n // RING + 1))
                return ring[n % RING][:, :].rearrange("p (k c) -> p k c", c=512)

            def transposes(key, sources):
                b = begin(key)
                for j, s in enumerate(sources):
                    last = nc.tensor.transpose(b[:, j * P:(j + 1) * P], s, c("ident"))
                end(last)

            def rows_product(prefix, name, left, prior=None):
                w = weight(name)
                for t in range(NT):
                    b = begin((*prefix, t))
                    for k in range(KC):
                        last = nc.tensor.matmul(b[:, :], left[:, k, t * P:(t + 1) * P], w[:, k, :],
                                                start=(k == 0), stop=(k == KC - 1))
                    end(last)

            def columns_product(prefix, name, n, right):
                w = weight(name)
                for m in range(4):
                    b = begin((prefix, 4 * n + m))
                    for k in range(KC):
                        last = nc.tensor.matmul(b[:, :], w[:, k, m * P:(m + 1) * P], right[:, k, :],
                                                start=(k == 0), stop=(k == KC - 1))
                    end(last)

            pe.wait_ge(consts_in_s, 16)
            pe.wait_ge(scaled, NT)
            for k in range(KC):
                transposes(("xT", k), [xs[:, t, k * P:(k + 1) * P] for t in range(NT)])
            wait_read(pe, ("xT", KC - 1))
            rows_product(("qi",), "qi", xnT)
            pe.wait_ge(small_in, 48)
            b = begin("kiwi")
            for t in range(NT):
                for k in range(KC):
                    last = nc.tensor.matmul(b[:, t * 72:(t + 1) * 72], xnT[:, k, t * P:(t + 1) * P],
                                            kiwi_w[:, k, :], start=(k == 0), stop=(k == KC - 1))
            end(last)
            for t in range(NT):
                pe.wait_ge(rotated, t + 1)
                transposes(("qiT", t), [rot[:, t, j * P:(j + 1) * P] for j in range(4)])
            wait_read(pe, "kiwi")
            transposes("kiT", [kirot[:, t, :] for t in range(NT)])
            wait_read(pe, "kiT")
            for t in range(1, NT):
                for h in range(IH):
                    b = begin(("idx", t, h))
                    half = slice(ID * (h % 2), ID * (h % 2) + ID)
                    end(nc.tensor.matmul(b[:, 0:(t + 1) * P], qiT[half, h // 2, t * P:(t + 1) * P],
                                         kiT[half, 0:(t + 1) * P], start=True, stop=True))
            for n in range(2):
                rows_product(("sv", n), f"sv{n}", xnT)
            for n in range(2):
                columns_product("su", f"su{n}", n, xnT)
            for n in range(2):
                columns_product("ga", f"ga{n}", n, xnT)
            pe.wait_ge(sgu_in, 48)
            for n in range(2):
                transposes(("wT", n), [sgu_w[:, 4 * n + j, :] for j in range(4)])
            wait_read(pe, ("wT", 1))
            pe.wait_ge(vn_scaled, NT)
            for g in range(GROUPS):
                b = begin(("mix", g))
                for t in range(NT):
                    last = nc.tensor.matmul(b[:, t * P:(t + 1) * P], vn[:, t, g * P:(g + 1) * P], wT[:, g, :],
                                            start=True, stop=True)
                end(last)
            pe.wait_ge(gated, GROUPS)
            for n in range(2):
                columns_product("wa", f"wa{n}", n, suT)
            for n in range(5):
                if n < 4:
                    rows_product(("qk", n), ["q0", "q1", "k0", "k1"][n], xnT)
                if n >= 1:
                    for t in range(NT):
                        pe.wait_ge(rotated, 4 + 4 * (n - 1) + t + 1)
                        transposes(("qkT", n - 1, t), [rot[:, t, j * P:(j + 1) * P] for j in range(4)])
            for n in range(2):
                rows_product(("v", n), f"v{n}", xnT)
            wait_read(pe, ("qkT", 3, NT - 1))
            for h in range(HEADS + 1):
                if h < HEADS:
                    for t in range(NT):
                        b = begin(("S", h, t))
                        end(nc.tensor.matmul(b[:, 0:(t + 1) * P], qT[:, h, t * P:(t + 1) * P],
                                             kT[:, h, 0:(t + 1) * P], start=True, stop=True))
                if h >= 1:
                    g = h - 1
                    for t in range(NT):
                        pe.wait_ge(probs_ready, g * NT + t + 1)
                        transposes(("T", g, t), [probs[g % 2][:, CAUSAL_AT[t] + s * P:CAUSAL_AT[t] + (s + 1) * P]
                                                 for s in range(t + 1)])
                    b = begin(("O", g))
                    wait_read(pe, ("v", 1, NT - 1))
                    wait_read(pe, ("T", g, NT - 1))
                    for s in range(NT):
                        last = nc.tensor.matmul(b[:, s * P:SEQ], v_rows[:, s, g * HD:(g + 1) * HD],
                                                pT[:, s, s * P:SEQ], start=(s == 0), stop=(s == NT - 1))
                    end(last)
            for n in range(2):
                columns_product("gb", f"gb{n}", n, xnT)
            wait_read(pe, ("O", HEADS - 1))
            for n in range(2):
                columns_product("wb", f"wb{n}", n, yT)
            pe.wait_ge(merged, KC)
            for n in range(2):
                rows_product(("wo", n), f"wo{n}", gT)
            m = moes[0]
            router_pe(pe, m, U, begin, end, transposes, wait_read)
            for who in ("act", "dve"):
                pe.wait_ge(read_by[who], U.reader.count(who))
            moe_pe(pe, m)

            pe.wait_ge(m.y_free_act, NE + 1)
            pe.wait_ge(m.y_free_dve, NE + 1)

            def begin2(key):
                who, reads = U2.read_before(key)
                if who:
                    pe.wait_ge(read_by2[who], reads)
                return bank[U2.bank(key)]

            def end2(ins):
                ins.then_inc(psum_filled2, 1)

            def transposes2(key, sources):
                b = begin2(key)
                for j, s in enumerate(sources):
                    last_ = nc.tensor.transpose(b[:, j * P:(j + 1) * P], s, c("ident"))
                end2(last_)

            def weight2(name):
                n = n_stream2[name]
                pe.wait_ge(weights2[n % RING], 16 * (n // RING + 1))
                return ring[n % RING][:, :].rearrange("p (k c) -> p k c", c=512)

            def rows2(name, left, tiles, first=0, prefix=None):
                w = weight2(name)
                for t in range(tiles):
                    b = begin2((*(prefix or (name,)), t))
                    for k in range(KC):
                        last_ = nc.tensor.matmul(b[:, :], left[:, k, (first + t) * P:(first + t + 1) * P], w[:, k, :],
                                                 start=(k == 0), stop=(k == KC - 1))
                    end2(last_)

            def columns2(name, meta_too):
                w = weight2(name)
                for m_ in range(4):
                    b = begin2((name, m_))
                    for k in range(KC):
                        last_ = nc.tensor.matmul(b[:, :], w[:, k, m_ * P:(m_ + 1) * P], hT[:, k, P:L2],
                                                 start=(k == 0), stop=(k == KC - 1))
                    end2(last_)
                if meta_too:
                    b = begin2(name + "_meta")
                    for m_ in range(4):
                        for k in range(KC):
                            last_ = nc.tensor.matmul(b[:, m_ * P:(m_ + 1) * P], w[:, k, m_ * P:(m_ + 1) * P],
                                                     hT[:, k, 0:P], start=(k == 0), stop=(k == KC - 1))
                    end2(last_)

            pe.wait_ge(scaled, TILES_BEFORE["in2"] + NT2)
            for n in range(2):
                transposes2(("metaT", n), [xs2[:, 0, (4 * n + j) * P:(4 * n + j + 1) * P] for j in range(4)])
            for k in range(KC):
                transposes2(("hT", k), [xs2[:, 1 + t, k * P:(k + 1) * P] for t in range(NT)])
            wait_read2(pe, ("hT", KC - 1))
            columns2("sbq", False)
            columns2("sbk", True)
            rows2("sbv", hT, NT2)
            rows2("hi", hT, NT2)
            columns2("hq", False)
            rows2("hg", hT, NT, first=1)
            columns2("hf", True)
            for h in range(SBH + 2):
                if h < SBH:
                    half = slice(SBD * (h % 2), SBD * (h % 2) + SBD)
                    for s in range(NT2):
                        b = begin2(("Z", h, s))
                        end2(nc.tensor.matmul(b[:, 0:STICK_W[s]], sbk[half, h // 2, s * P:(s + 1) * P],
                                              sbq[half, h // 2, FIRST_T[s] * P:SEQ], start=True, stop=True))
                if 1 <= h <= SBH:
                    g = h - 1
                    pe.wait_ge(sp_ready, h)
                    for s in range(NT2):
                        b = begin2(("R", g, s))
                        for s2 in range(s, NT2):
                            col = (FIRST_T[s2] - FIRST_T[s]) * P
                            last_ = nc.tensor.matmul(b[:, col:STICK_W[s]], c("tri_ge") if s2 == s else c("ones"),
                                                     sps[g % 2][:, STICK_AT[s2]:STICK_AT[s2] + STICK_W[s2]],
                                                     start=(s2 == s), stop=(s2 == NT2 - 1))
                        end2(last_)
                if h >= 2:
                    g = h - 2
                    pe.wait_ge(weight_ready, g + 1)
                    b = begin2(("SO", g))
                    for t in range(NT):
                        for s in range(t + 2):
                            a = STICK_AT[s] + (t - FIRST_T[s]) * P
                            last_ = nc.tensor.matmul(b[:, t * SBD:(t + 1) * SBD], zw[g % 3][:, a:a + P],
                                                     sbv[:, s, g * SBD:(g + 1) * SBD], start=(s == 0), stop=(s == t + 1))
                    end2(last_)

            def head_out(g):
                pe.wait_ge(scores_ready, g + 1)
                pe.wait_ge(states_ready, g + 1)
                pe.wait_ge(q_ready, g + 1)
                b = begin2(("HO", g))
                for t in range(NT):
                    nc.tensor.matmul(b[:, t * P:(t + 1) * P], hsc[:, g % 2, t * P:(t + 1) * P],
                                     hv[:, t + 1, g * HD:(g + 1) * HD], start=True, stop=False)
                    last_ = nc.tensor.matmul(b[:, t * P:(t + 1) * P], qexp[:, g % 2, t * P:(t + 1) * P],
                                             states[:, g % 2, t, :], start=False, stop=True)
                end2(last_)

            for h in range(HGH):
                for lv in range(LEVELS):
                    if lv == 0:
                        pe.wait_ge(kd_ready, h + 1)
                        transposes2(("KT", h), [kd[:, h % 2, t * P:(t + 1) * P] for t in range(NT)])
                        b = begin2(("DG", h))
                        for t in range(NT):
                            last_ = nc.tensor.matmul(b[:, t * P:(t + 1) * P], hk[:, h, (t + 1) * P:(t + 2) * P],
                                                     hq[:, h, t * P:(t + 1) * P], start=True, stop=True)
                        end2(last_)
                    n = h * LEVELS + lv
                    pe.wait_ge(level_ready, n + 1)
                    b = begin2(("L", h, lv))
                    for t in range(NT):
                        last_ = nc.tensor.matmul(b[:, t * P:(t + 1) * P], kE[:, n % 2, t * P:(t + 1) * P],
                                                 qE[:, n % 2, t * P:(t + 1) * P], start=True, stop=True)
                    end2(last_)
                    if lv == 2:
                        wait_read2(pe, ("KT", h))
                        b = begin2(("KV", h))
                        for t in range(NT):
                            last_ = nc.tensor.matmul(b[:, t * P:(t + 1) * P], kdR[:, h % 2, t * P:(t + 1) * P],
                                                     hv[:, t, h * HD:(h + 1) * HD], start=True, stop=True)
                        end2(last_)
                    if lv == 1 and h >= 1:
                        head_out(h - 1)
            head_out(HGH - 1)
            pe.wait_ge(heads_normed, NT)
            for k in range(KC):
                transposes2(("mT", k), [mixed[:, t, k * P:(k + 1) * P] for t in range(NT)])
            wait_read2(pe, ("mT", KC - 1))
            for n in range(2):
                rows2(f"wo2_{n}", mixedT, NT, prefix=("wo2", n))
            m = moes[1]
            router_pe(pe, m, U2, begin2, end2, transposes2, wait_read2)
            for who in ("act", "dve"):
                pe.wait_ge(read_by2[who], U2.reader.count(who))
            moe_pe(pe, m)

        @block.scalar
        def _(act):
            def unit(key):
                act.wait_ge(psum_filled, U.filled(key))
                return bank[U.bank(key)]

            def read(ins):
                ins.then_inc(read_by["act"], 1)

            act.wait_ge(x_in_s, 16)
            for t in range(NT):
                nc.scalar.activation(xs[:, t, :], x[:, t, :], ACT.Square, accum_out=ssq[:, t:t + 1])\
                    .then_inc(sumsq, 1)
            act.wait_ge(rms, 1)
            act.wait_ge(sumsq, NT)
            for t in range(NT):
                nc.scalar.activation(xs[:, t, :], x[:, t, :], ACT.Copy, scale=rstd[:, t:t + 1]).then_inc(scaled, 1)
            act.wait_ge(angles_ready, 2)
            nc.scalar.activation(cos[:, :, :], trig[:, 0, :].rearrange("p (t f) -> p t f", t=NT), ACT.Sin)\
                .then_inc(trig_ready, 1)
            nc.scalar.activation(sin[:, :, :], trig[:, 1, :].rearrange("p (t f) -> p t f", t=NT), ACT.Sin)\
                .then_inc(trig_ready, 1)
            for t in range(NT):
                b = unit(("qiT", t))
                read(nc.scalar.copy(qiT[:, :, t * P:(t + 1) * P], b[:, :].rearrange("p (j q) -> p j q", q=P)))
            b = unit("kiT")
            read(nc.scalar.copy(kiT[:, :], b[:, :]))
            n = 0
            for t in range(1, NT):
                for h in range(IH):
                    b = unit(("idx", t, h))
                    if n >= 3:
                        act.wait_ge(rel_used, n - 2)
                    read(nc.scalar.activation(rel[:, n % 3, 0:(t + 1) * P], b[:, 0:(t + 1) * P], ACT.Relu))
                    n += 1
            for n in range(2):
                for t in range(NT):
                    b = unit(("sv", n, t))
                    read(nc.scalar.activation(vn[:, t, n * 512:(n + 1) * 512], b[:, :], ACT.Gelu_apprx_tanh))
            for m in range(KC):
                b = unit(("su", m))
                read(nc.scalar.activation(suT[:, m, :], b[:, :], ACT.Gelu_apprx_tanh))
            for m in moes:
                act.wait_ge(m.rows_cleared, (OVER + 1) * SLOTS // P * 16)
            for m in range(KC):
                b = unit(("ga", m))
                read(nc.scalar.activation(gT[:, m, :], b[:, :], ACT.Sigmoid))
            for n in range(4):
                dst = qT if n < 2 else kT
                for t in range(NT):
                    b = unit(("qkT", n, t))
                    h = 4 * (n % 2)
                    read(nc.scalar.copy(dst[:, h:h + 4, t * P:(t + 1) * P],
                                        b[:, :].rearrange("p (j q) -> p j q", q=P)))
            for n in range(2):
                for t in range(NT):
                    b = unit(("v", n, t))
                    read(nc.scalar.copy(v_rows[:, t, n * 512:(n + 1) * 512], b[:, :]))
            for h in range(HEADS):
                for t in range(NT):
                    act.wait_ge(logits_ready, h + 1)
                    p = probs[h % 2][:, CAUSAL_AT[t]:CAUSAL_AT[t + 1]]
                    nc.scalar.activation(p, p, ACT.Exp, bias=nm[:, h, t:t + 1], scale=HD ** -0.5,
                                         accum_out=sums[:, h, t:t + 1]).then_inc(exp_ready, 1)
                for t in range(NT):
                    b = unit(("T", h, t))
                    if t == 0 and h >= 1:
                        act.wait_ge(psum_filled, U.filled(("O", h - 1)))
                    read(nc.scalar.copy(pT[:, 0:t + 1, t * P:(t + 1) * P],
                                        b[:, 0:(t + 1) * P].rearrange("p (j q) -> p j q", q=P)))
                b = unit(("O", h))
                read(nc.scalar.copy(yT[:, h, :], b[:, :]))
            for m in range(KC):
                b = unit(("gb", m))
                read(nc.scalar.activation(gbT[:, m, :], b[:, :], ACT.Sigmoid))
            m = moes[0]
            norm_act(act, m, lambda e, t: wait_read(e, ("wo", 1, t)))
            router_act(act, m)
            moe_act(act, m)

            def squares_of(t):
                return at(arena, 3 * TILE + t * D, [D])

            A = nc.scalar
            for t in range(NT):
                act.wait_ge(m.moe_added, 2 * t + 2)
                A.activation(squares_of(t), x[:, t, :], ACT.Square, accum_out=ssq[:, t:t + 1]).then_inc(sumsq, 1)
            act.wait_ge(rms, ROOTS_BEFORE["out1"] + 1)
            act.wait_ge(sumsq, TILES_BEFORE["out1"] + NT)
            for t in range(NT):
                A.activation(x[:, t, :], x[:, t, :], ACT.Copy, scale=rstd[:, t:t + 1]).then_inc(scaled, 1)
            act.wait_ge(meta_in, 16)
            A.activation(squares_of(0), meta, ACT.Square, accum_out=ssq[:, 4:5]).then_inc(sumsq, 1)
            for t in range(NT):
                act.wait_ge(x_normed, t + 1)
                A.activation(squares_of(1 + t), x[:, t, :], ACT.Square, accum_out=ssq[:, 5 + t:6 + t]).then_inc(sumsq, 1)
            act.wait_ge(rms, ROOTS_BEFORE["in2"] + 1)
            A.activation(xs2[:, 0, :], meta, ACT.Copy, scale=rstd[:, 4:5]).then_inc(scaled, 1)
            for t in range(NT):
                A.activation(xs2[:, 1 + t, :], x[:, t, :], ACT.Copy, scale=rstd[:, 5 + t:6 + t]).then_inc(scaled, 1)
            act.wait_ge(lb_out, 1)
            A.activation(lbl[:, :, :], lbl[:, :, :], ACT.Exp).then_inc(lb_exp, 1)

            def unit2(key):
                act.wait_ge(psum_filled2, U2.filled(key))
                return bank[U2.bank(key)]

            def read2(ins):
                ins.then_inc(read_by2["act"], 1)

            for m_ in range(4):
                b = unit2(("sbq", m_))
                read2(A.copy(sbq[:, m_, :], b[:, :]))
            for m_ in range(4):
                b = unit2(("sbk", m_))
                read2(A.copy(sbk[:, m_, P:L2], b[:, :]))
            b = unit2("sbk_meta")
            read2(A.copy(sbk[:, :, 0:P], b[:, :].rearrange("p (m q) -> p m q", q=P)))
            for name, dst in (("sbv", sbv), ("hi", hv)):
                for t in range(NT2):
                    b = unit2((name, t))
                    read2(A.copy(dst[:, t, :], b[:, :]))
            for m_ in range(4):
                b = unit2(("hq", m_))
                read2(A.activation(hq[:, m_, :], b[:, :], ACT.Silu))
            for t in range(NT):
                b = unit2(("hg", t))
                read2(A.activation(hgate[:, t, :], b[:, :], ACT.Silu))
            for m_ in range(4):
                b = unit2(("hf", m_))
                A.activation(bc[:, m_, P:L2], b[:, :], ACT.Sigmoid)
                read2(A.activation(hk[:, m_, P:L2], b[:, :], ACT.Sigmoid, scale=-1.0))
            b = unit2("hf_meta")
            bv = b[:, :].rearrange("p (m q) -> p m q", q=P)
            A.activation(bc[:, :, 0:P], bv, ACT.Sigmoid)
            read2(A.activation(hk[:, :, 0:P], bv, ACT.Sigmoid, scale=-1.0))
            act.wait_ge(decay_ready, 1)
            wait_read2(act, "hf_meta")
            for h in range(HGH):
                A.activation(bc[:, h, :], bc[:, h, :], ACT.Ln, bias=lb[:, h:h + 1], scale=oml[:, h:h + 1])\
                    .then_inc(log_f_ready, 1)
            for h in range(SBH + 2):
                if h < SBH:
                    act.wait_ge(z_ready, h + 1)
                    v = sps[h % 2]
                    A.activation(v, v, ACT.Exp, scale=-1.0).then_inc(act_step, 1)
                    act.wait_ge(act_step, h + 1)
                    A.activation(v, v, ACT.Ln, bias=1.0).then_inc(log_ready, 1)
                if 1 <= h <= SBH:
                    g = h - 1
                    wait_read2(act, ("R", g, NT2 - 1))
                    A.activation(zw[g % 3], zw[g % 3], ACT.Exp).then_inc(weight_ready, 1)
                if h >= 2:
                    g = h - 2
                    b = unit2(("SO", g))
                    read2(A.copy(mixed[:, :, g * SBD:(g + 1) * SBD],
                                 b[:, 0:NT * SBD].rearrange("p (t d) -> p t d", d=SBD)))
            act.wait_ge(carried, HGH * NT2)
            A.activation(chunk_decay[:, :, :], bc[:, :, P - 1:L2:P], ACT.Exp).then_inc(last_ready, 1)

            def level_exp(n):
                act.wait_ge(diff_ready, n + 1)
                A.activation(diff[:, n % 2, :], diff[:, n % 2, :], ACT.Exp).then_inc(diff_exp, 1)

            def head_exps(h):
                if h >= 2:
                    act.wait_ge(psum_filled2, U2.filled(("HO", h - 2)))
                for t in range(NT):
                    ins = A.activation(kd[:, h % 2, t * P:(t + 1) * P], bc[:, h, t * P:(t + 1) * P], ACT.Exp,
                                       bias=bc[:, h, (t + 1) * P - 1:(t + 1) * P], scale=-1.0)
                ins.then_inc(kd_exp, 1)
                A.activation(qexp[:, h % 2, :], bc[:, h, P:L2], ACT.Exp).then_inc(q_exp, 1)

            def head_copy(h):
                b = unit2(("HO", h))
                read2(A.copy(mixed[:, :, 512 + h * HD:512 + (h + 1) * HD],
                             b[:, :].rearrange("p (t d) -> p t d", d=HD)))

            head_exps(0)
            level_exp(0)
            for h in range(HGH):
                for lv in range(LEVELS):
                    n = h * LEVELS + lv
                    if lv == LEVELS - 1 and h + 1 < HGH:
                        head_exps(h + 1)
                    if n + 1 < HGH * LEVELS:
                        level_exp(n + 1)
                    if lv == 0:
                        b = unit2(("KT", h))
                        read2(A.copy(kdR[:, h % 2, :], b[:, :]))
                    if lv == 1 and h >= 1:
                        head_copy(h - 1)
            head_copy(HGH - 1)
            for k in range(KC):
                b = unit2(("mT", k))
                read2(A.copy(mixedT[:, k, :], b[:, :]))
            m = moes[1]
            norm_act(act, m, lambda e, t: wait_read2(e, ("wo2", 1, t)))
            router_act(act, m)
            moe_act(act, m)
            for t in range(NT):
                act.wait_ge(m.moe_added, 2 * t + 2)
                A.activation(squares_of(t), x[:, t, :], ACT.Square, accum_out=ssq[:, t:t + 1])\
                    .then_inc(sumsq, 1)
            act.wait_ge(rms, ROOTS_BEFORE["out2"] + 1)
            act.wait_ge(sumsq, TILES_BEFORE["out2"] + NT)
            for t in range(NT):
                A.activation(x[:, t, :], x[:, t, :], ACT.Copy, scale=rstd[:, t:t + 1]).then_inc(scaled, 1)

        @block.vector
        def _(dve):
            def unit(key):
                dve.wait_ge(psum_filled, U.filled(key))
                return bank[U.bank(key)]

            def read(ins):
                ins.then_inc(read_by["dve"], 1)

            def then(ins):
                link("dve", dve, dve_step, ins)

            V = nc.vector
            dve.wait_ge(small_in, 48)
            dve.wait_ge(consts_in_s, 16)
            then(V.tensor_copy(pos_f[:, :], pos_i[:, :]))
            ang, turns = trig[:, 2, :], trig[:, 3, :]
            for t in range(NT):
                then(V.tensor_scalar(ang[:, t * 64:(t + 1) * 64], c("invf"), pos_f[:, t:t + 1], None, ALU.mult))
            two_pi = 2 * np.pi
            c1 = float(np.float32(6.28125))
            c2 = float(np.float32(np.round((two_pi - c1) * 2 ** 21) / 2 ** 21))
            c3 = float(np.float32(two_pi - c1 - c2))
            magic = 1.5 * 2.0 ** 23
            for j, quarter in ((0, 0.25), (1, 0.0)):
                r = trig[:, j, :]
                then(V.tensor_scalar(turns, ang, 1.0 / two_pi, quarter, ALU.mult, ALU.add))
                then(V.tensor_scalar(turns, turns, magic, None, ALU.add))
                then(V.tensor_scalar(turns, turns, -magic, None, ALU.add))
                then(V.scalar_tensor_tensor(r, turns, -c1, ang, ALU.mult, ALU.add))
                then(V.scalar_tensor_tensor(r, turns, -c2, r, ALU.mult, ALU.add))
                then(V.scalar_tensor_tensor(r, turns, -c3, r, ALU.mult, ALU.add))
                then(V.tensor_scalar(r, r, float(np.pi / 2) if j == 0 else 0.0, 3.1415925, ALU.add, ALU.min))
                V.tensor_scalar(r, r, -3.1415925, None, ALU.max).then_inc(angles_ready, 1)
            for k in range(KC):
                b = unit(("xT", k))
                read(V.tensor_scalar(xnT[:, k, :], b[:, :], g1[:, k:k + 1], None, ALU.mult))

            rotations = 0

            def rope_unit(key, t, heads, width):
                nonlocal rotations
                b = unit(key)
                if rotations >= 2:
                    dve.wait_ge(rotated, rotations - 1)
                step = HD // width
                shape = [P, 2 * heads, width // 2]
                src = b[:, :].rearrange("p (a f) -> p a f", f=width // 2)
                for table, dst in ((cos, rot_a), (sin, rot_b)):
                    row = table[:, t, 0:HD // 2:step][:, None, :].broadcast_to(shape)
                    last = V.tensor_tensor(dst[:, rotations % 2, :].rearrange("p (a f) -> p a f", f=width // 2),
                                           src, row, ALU.mult)
                read(last)
                rotations += 1

            dve.wait_ge(trig_ready, 2)
            for t in range(NT):
                rope_unit(("qi", t), t, IH, ID)
            b = unit("kiwi")
            kv = b[:, 0:288].rearrange("p (t c) -> p t c", c=72)
            shape = [P, NT, ID // 2]
            x1, x2 = kv[:, :, 0:32], kv[:, :, 32:64]
            cs, sn = cos[:, :, 0:64:2], sin[:, :, 0:64:2]
            then(V.tensor_copy(wi[:, :, :], kv[:, :, 64:72]))
            for dup in (0, 64):
                tmp = at(misc, 0, [NT, 32])
                tmp2 = at(misc, 128, [NT, 32])
                then(V.tensor_tensor(tmp, x1, cs, ALU.mult))
                then(V.tensor_tensor(tmp2, x2, sn, ALU.mult))
                then(V.tensor_tensor(kirot[:, :, dup:dup + 32], tmp, tmp2, ALU.subtract))
                then(V.tensor_tensor(tmp, x2, cs, ALU.mult))
                then(V.tensor_tensor(tmp2, x1, sn, ALU.mult))
                last = V.tensor_tensor(kirot[:, :, dup + 32:dup + 64], tmp, tmp2, ALU.add)
                if dup == 0:
                    then(last)
            read(last)
            n = 0
            for t in range(1, NT):
                s = scores[:, SCORE_AT[t]:SCORE_AT[t] + (t + 1) * P]
                for h in range(IH):
                    wait_read(dve, ("idx", t, h))
                    r = rel[:, n % 3, 0:(t + 1) * P]
                    if h == 0:
                        ins = V.tensor_scalar(s, r, wi[:, t, 0:1], None, ALU.mult)
                    else:
                        dve.wait_ge(rel_used, n)
                        ins = V.scalar_tensor_tensor(s, r, wi[:, t, h:h + 1], s, ALU.mult, ALU.add)
                    ins.then_inc(rel_used, 1)
                    n += 1
            dve.wait_ge(rel_used, n)
            for t in range(1, NT):
                s = scores[:, SCORE_AT[t]:SCORE_AT[t] + (t + 1) * P]
                then(V.tensor_tensor(s[:, t * P:(t + 1) * P], s[:, t * P:(t + 1) * P], c("causal"), ALU.add))
                for _ in range(TOPK // 8):
                    then(V.max(top8[:, :], s))
                    then(V.match_replace(s, top8[:, :], s, TAKEN))
                then(V.tensor_scalar(s, s, -2.0e38, NEG, ALU.is_gt, ALU.mult))
            wait_read(dve, ("sv", 1, NT - 1))
            for t in range(NT):
                for n in range(2):
                    then(V.bn_stats(bn6[:, t, n, :], vn[:, t, n * 512:(n + 1) * 512]))
                V.bn_aggr(bn2[:, t, :], bn6[:, t, :, :]).then_inc(var_ready, 1)
            dve.wait_ge(rms, 2)
            for t in range(NT):
                V.tensor_scalar(vn[:, t, :], vn[:, t, :], bn2[:, t, 0:1], rstd[:, 4 + t:5 + t],
                                ALU.subtract, ALU.mult).then_inc(vn_ready, 1)
            for n in range(2):
                b = unit(("wT", n))
                read(V.tensor_tensor(wT[:, 4 * n:4 * n + 4, :], b[:, :].rearrange("p (g t) -> p g t", t=P),
                                     c("le")[:, None, :].broadcast_to([P, 4, P]), ALU.mult))
            wait_read(dve, ("su", KC - 1))
            sgu_mixed = at(misc, 0, [2, 512])
            for g in range(GROUPS):
                b = unit(("mix", g))
                m = sgu_mixed[:, g % 2, :]
                ins = V.tensor_tensor(m.rearrange("p (t q) -> p t q", q=P), b[:, :].rearrange("p (t q) -> p t q", q=P),
                                      sgu_b[:, g, :][:, None, :].broadcast_to([P, NT, P]), ALU.add)
                read(ins)
                wait_read(dve, ("mix", g))
                V.tensor_tensor(suT[:, g, :], suT[:, g, :], m, ALU.mult).then_inc(gated, 1)
            wait_read(dve, ("ga", KC - 1))
            for m in range(KC):
                b = unit(("wa", m))
                read(V.tensor_tensor(gT[:, m, :], gT[:, m, :], b[:, :], ALU.mult))
            for n in range(4):
                for t in range(NT):
                    rope_unit(("qk", n, t), t, 4, HD)
            for h in range(HEADS + 1):
                if h < HEADS:
                    for t in range(NT):
                        b = unit(("S", h, t))
                        if h >= 2 and t == 0:
                            dve.wait_ge(psum_filled, U.filled(("T", h - 2, NT - 1)))
                        w = (t + 1) * P
                        mask = c("causal") if t == 0 else scores[:, SCORE_AT[t]:SCORE_AT[t] + w]
                        p = probs[h % 2][:, CAUSAL_AT[t]:CAUSAL_AT[t + 1]]
                        ins = V.tensor_tensor_reduce(out=p, in0=b[:, 0:w], in1=mask, scale=1.0, scalar=-3.0e38,
                                                     op0=ALU.add, op1=ALU.max, accum_out=mx[:, h, t:t + 1])
                        read(ins)
                    wait_read(dve, ("S", h, NT - 1))
                    V.tensor_scalar(nm[:, h, :], mx[:, h, :], -(HD ** -0.5), None, ALU.mult)\
                        .then_inc(logits_ready, 1)
                if h >= 1:
                    g = h - 1
                    dve.wait_ge(exp_ready, (g + 1) * NT)
                    then(V.reciprocal(inv[:, g, :], sums[:, g, :]))
                    for t in range(NT):
                        p = probs[g % 2][:, CAUSAL_AT[t]:CAUSAL_AT[t + 1]]
                        V.tensor_scalar(p, p, inv[:, g, t:t + 1], None, ALU.mult).then_inc(probs_ready, 1)
            for m in range(KC):
                b = unit(("wb", m))
                wait_read(dve, ("gb", m))
                ins = V.tensor_tensor(gbT[:, m, :], gbT[:, m, :], b[:, :], ALU.mult)
                read(ins)
                wait_read(dve, ("wb", m))
                V.tensor_tensor(gT[:, m, :], gT[:, m, :], gbT[:, m, :], ALU.add).then_inc(merged, 1)
            for n in range(2):
                for t in range(NT):
                    b = unit(("wo", n, t))
                    xv = x[:, t, n * 512:(n + 1) * 512]
                    read(V.tensor_tensor(xv, xv, b[:, :], ALU.add))
            m = moes[0]
            router_dve(dve, m, unit, read, then, wait_read)
            moe_dve(dve, m, then)

            dve.wait_ge(block2_in, 16 * 5)
            for t in range(NT):
                dve.wait_ge(scaled, TILES_BEFORE["out1"] + t + 1)
                V.tensor_tensor(x[:, t, :], x[:, t, :], gf, ALU.mult).then_inc(x_normed, 1)
            then(V.tensor_tensor(lbm[:, :], lbl[:, 0, :], lbl[:, 1, :], ALU.max))
            V.tensor_tensor(lbl[:, :, :], lbl[:, :, :], lbm[:, None, :].broadcast_to([P, 2, HGH]), ALU.subtract)\
                .then_inc(lb_out, 1)

            def unit2(key):
                dve.wait_ge(psum_filled2, U2.filled(key))
                return bank[U2.bank(key)]

            def read2(ins):
                ins.then_inc(read_by2["dve"], 1)

            for n in range(2):
                b = unit2(("metaT", n))
                gm = gmix[:, 4 * n:4 * n + 4][:, :, None].broadcast_to([P, 4, P])
                read2(V.tensor_tensor(hT[:, 4 * n:4 * n + 4, 0:P], b[:, :].rearrange("p (k q) -> p k q", q=P), gm,
                                      ALU.mult))
            for k in range(KC):
                b = unit2(("hT", k))
                read2(V.tensor_scalar(hT[:, k, P:L2], b[:, :], gmix[:, k:k + 1], None, ALU.mult))
            dve.wait_ge(lb_exp, 1)
            then(V.tensor_tensor(lbm[:, :], lbl[:, 0, :], lbl[:, 1, :], ALU.add))
            then(V.reciprocal(lbm[:, :], lbm[:, :]))
            then(V.tensor_tensor(lb[:, :], lbl[:, 0, :], lbm[:, :], ALU.mult))
            V.tensor_scalar(oml[:, :], lb[:, :], -1.0, 1.0, ALU.mult, ALU.add).then_inc(decay_ready, 1)
            dve.wait_ge(decay_ready, 1)
            wait_read2(dve, "hf_meta")
            for h in range(HGH):
                then(V.tensor_scalar(hk[:, h, :], hk[:, h, :], oml[:, h:h + 1], None, ALU.mult))
            V.memset(hk[:, :, 0:P - META], 0.0).then_inc(keys_ready, 1)
            for h in range(HGH):
                dve.wait_ge(log_f_ready, h + 1)
                for t in range(NT2):
                    v = bc[:, h, t * P:(t + 1) * P]
                    V.tensor_tensor_scan(v, c("ones"), v, 0.0, ALU.mult, ALU.add).then_inc(carried, 1)
            scale = SBD ** -0.5
            for h in range(SBH + 1):
                if h < SBH:
                    z, v = zw[h % 3], sps[h % 2]
                    if h >= 3:
                        dve.wait_ge(psum_filled2, U2.filled(("SO", h - 3)))
                    for s in range(NT2):
                        b = unit2(("Z", h, s))
                        zs = z[:, STICK_AT[s]:STICK_AT[s] + STICK_W[s]]
                        if s == 0:
                            ins = V.tensor_scalar(zs, b[:, :], scale, c("pad_rows"), ALU.mult, ALU.add)
                        else:
                            ins = V.scalar_tensor_tensor(zs[:, 0:P], b[:, 0:P], scale, c("strict"), ALU.mult, ALU.add)
                            if STICK_W[s] > P:
                                ins = V.tensor_scalar(zs[:, P:], b[:, P:STICK_W[s]], scale, None, ALU.mult)
                        read2(ins)
                    wait_read2(dve, ("Z", h, NT2 - 1))
                    V.scalar_tensor_tensor(v, z, -1.0, z, ALU.mult, ALU.max).then_inc(z_ready, 1)
                if h >= 1:
                    g = h - 1
                    for s in range(NT2):
                        b = unit2(("R", g, s))
                        zs = zw[g % 3][:, STICK_AT[s]:STICK_AT[s] + STICK_W[s]]
                        read2(V.tensor_tensor(zs, zs, b[:, 0:STICK_W[s]], ALU.subtract))
                if h < SBH:
                    dve.wait_ge(log_ready, h + 1)
                    V.scalar_tensor_tensor(v, z, 0.0, v, ALU.max, ALU.add).then_inc(sp_ready, 1)
            dve.wait_ge(psum_filled2, U2.filled(("SO", SBH - 1)))
            dve.wait_ge(carried, HGH * NT2)
            then(V.memset(qE[:, :, :], 0.0))
            then(V.memset(kE[:, :, :], 0.0))

            def halves(v, half):
                return v.rearrange("p (b two i) -> p b two i", two=2, i=half)

            def level_diff(n):
                h, lv = divmod(n, LEVELS)
                half = P >> (lv + 1)
                src, dst = halves(bc[:, h, P:L2], half), halves(diff[:, n % 2, :], half)
                if n >= 2:
                    dve.wait_ge(level_ready, n - 1)
                ref = src[:, :, 0, half - 1:half].broadcast_to([P, SEQ // (2 * half), half])
                V.tensor_tensor(dst[:, :, 1, :], src[:, :, 1, :], ref, ALU.subtract)
                V.tensor_tensor(dst[:, :, 0, :], ref, src[:, :, 0, :], ALU.subtract).then_inc(diff_ready, 1)

            def level_products(n):
                h, lv = divmod(n, LEVELS)
                half = P >> (lv + 1)
                dve.wait_ge(diff_exp, n + 1)
                e = halves(diff[:, n % 2, :], half)
                V.tensor_tensor(halves(qE[:, n % 2, :], half)[:, :, 1, :], e[:, :, 1, :],
                                halves(hq[:, h, :], half)[:, :, 1, :], ALU.mult)
                V.tensor_tensor(halves(kE[:, n % 2, :], half)[:, :, 0, :], e[:, :, 0, :],
                                halves(hk[:, h, P:L2], half)[:, :, 0, :], ALU.mult).then_inc(level_ready, 1)

            def level_mask(i):
                a = CONST_COLS["levels"][0] + i * P
                return cst[:, a:a + P][:, None, :].broadcast_to([P, NT, P])

            def level_read(n):
                h, lv = divmod(n, LEVELS)
                s = hsc[:, h % 2, :].rearrange("p (t q) -> p t q", q=P)
                if lv == 0:
                    if h >= 2:
                        dve.wait_ge(psum_filled2, U2.filled(("HO", h - 2)))
                    b = unit2(("DG", h))
                    read2(V.tensor_tensor(s, b[:, :].rearrange("p (t q) -> p t q", q=P), level_mask(LEVELS), ALU.mult))
                    wait_read2(dve, ("DG", h))
                b = unit2(("L", h, lv))
                read2(V.copy_predicated(s, level_mask(lv).bitcast(U32), b[:, :].rearrange("p (t q) -> p t q", q=P)))
                wait_read2(dve, ("L", h, lv))
                if lv == 2:
                    b = unit2(("KV", h))
                    st = states[:, h % 2, :, :]
                    then(V.tensor_copy(st[:, 0, :], b[:, 0:P]))
                    for t in range(1, NT):
                        ins = V.scalar_tensor_tensor(st[:, t, :], st[:, t - 1, :], chunk_decay[:, h, t:t + 1],
                                                     b[:, t * P:(t + 1) * P], ALU.mult, ALU.add)
                        if t < NT - 1:
                            then(ins)
                    read2(ins)
                    wait_read2(dve, ("KV", h))
                    dve.sem_inc(states_ready, 1)
                if lv == LEVELS - 1:
                    dve.sem_inc(scores_ready, 1)

            def head_products(h):
                dve.wait_ge(kd_exp, h + 1)
                V.tensor_tensor(kd[:, h % 2, :], kd[:, h % 2, :], hk[:, h, 0:SEQ], ALU.mult).then_inc(kd_ready, 1)
                dve.wait_ge(q_exp, h + 1)
                V.tensor_tensor(qexp[:, h % 2, :], qexp[:, h % 2, :], hq[:, h, :], ALU.mult).then_inc(q_ready, 1)

            dve.wait_ge(last_ready, 1)
            dve.wait_ge(keys_ready, 1)
            level_diff(0)
            head_products(0)
            for n in range(HGH * LEVELS):
                if n + 1 < HGH * LEVELS:
                    level_diff(n + 1)
                level_products(n)
                if n >= 1:
                    level_read(n - 1)
                if n % LEVELS == LEVELS - 1 and n // LEVELS + 1 < HGH:
                    head_products(n // LEVELS + 1)
            level_read(HGH * LEVELS - 1)
            wait_read2(dve, ("HO", HGH - 1))
            for t in range(NT):
                then(V.tensor_tensor(squares[:, t, :], mixed[:, t, :], mixed[:, t, :], ALU.mult))
            V.tensor_reduce(rstd[:, 0:32].rearrange("p (t h) -> p t h", h=8),
                            squares[:, :, 0:512].rearrange("p t (h d) -> p t h d", d=SBD), AX.X, ALU.add)\
                .then_inc(squares_ready, 1)
            V.tensor_reduce(rstd[:, 32:48].rearrange("p (t h) -> p t h", h=4),
                            squares[:, :, 512:1024].rearrange("p t (h d) -> p t h d", d=HD), AX.X, ALU.add)\
                .then_inc(squares_ready, 1)
            dve.wait_ge(rms, ROOTS_BEFORE["heads"] + 1)
            for t in range(NT):
                for lo, wd, r0 in ((0, SBD, 8 * t), (512, HD, 32 + 4 * t)):
                    n_ = 512 // wd
                    v = mixed[:, t, lo:lo + 512].rearrange("p (h d) -> p h d", d=wd)
                    ins = V.tensor_tensor(v, v, rstd[:, r0:r0 + n_][:, :, None].broadcast_to([P, n_, wd]), ALU.mult)
                    if lo == 512:
                        then(ins)
                        ins = V.tensor_tensor(mixed[:, t, 512:], mixed[:, t, 512:], hgate[:, t, :], ALU.mult)
                    then(ins)
                V.tensor_tensor(mixed[:, t, :], mixed[:, t, :], misc[:, 0:D], ALU.mult).then_inc(heads_normed, 1)
            for n in range(2):
                for t in range(NT):
                    b = unit2(("wo2", n, t))
                    xv = x[:, t, n * 512:(n + 1) * 512]
                    read2(V.tensor_tensor(xv, xv, b[:, :], ALU.add))
            m = moes[1]
            router_dve(dve, m, unit2, read2, then, wait_read2)
            moe_dve(dve, m, then)
            dve.wait_ge(block2_in, 16 * 6)
            for t in range(NT):
                dve.wait_ge(scaled, TILES_BEFORE["out2"] + t + 1)
                V.tensor_tensor(x[:, t, :], x[:, t, :], gf, ALU.mult).then_inc(result, 1)

        @block.gpsimd
        def _(pool):
            def then(ins):
                link("pool", pool, pool_step, ins)

            G = nc.gpsimd
            G.memset(no_token[:, :], 0).then_inc(ids_ready, 1)
            G.memset(zeros, 0.0).then_inc(ids_ready, 1)
            G.iota(token_id[:, :], pattern=[[P, NT]], base=0, channel_multiplier=1).then_inc(ids_ready, 1)
            pool.wait_ge(consts_in_s, 16)
            pool.wait_ge(sumsq, NT)
            then(G.tensor_scalar(rstd[:, 0:4], ssq[:, 0:4], 1.0 / D, EPS, ALU.mult, ALU.add))
            G.tensor_tensor(rstd[:, 0:4], rstd[:, 0:4], c("nhalf")[:, 0:4], ALU.pow).then_inc(rms, 1)
            rotations = 0

            def add_halves(key, slot, heads, width):
                nonlocal rotations
                wait_read(pool, key)
                pattern = dict(two=2, f=width // 2)
                a = rot_a[:, rotations % 2, :].rearrange("p (h two f) -> p h two f", **pattern)
                s = rot_b[:, rotations % 2, :].rearrange("p (h two f) -> p h two f", **pattern)
                o = rot[:, slot, :].rearrange("p (h two f) -> p h two f", **pattern)
                if rotations >= 8:
                    pool.wait_ge(psum_filled, U.filled(("qkT", (rotations - 8) // 4, slot)))
                elif rotations >= 4:
                    pool.wait_ge(psum_filled, U.filled(("qiT", slot)))
                then(G.tensor_tensor(o[:, :, 0, :], a[:, :, 0, :], s[:, :, 1, :], ALU.subtract))
                G.tensor_tensor(o[:, :, 1, :], a[:, :, 1, :], s[:, :, 0, :], ALU.add).then_inc(rotated, 1)
                rotations += 1

            for t in range(NT):
                add_halves(("qi", t), t, IH, ID)
            pool.wait_ge(var_ready, NT)
            then(G.tensor_scalar(rstd[:, 4:8], bn2[:, :, 1], EPS, None, ALU.add))
            G.tensor_tensor(rstd[:, 4:8], rstd[:, 4:8], c("nhalf")[:, 0:4], ALU.pow).then_inc(rms, 1)
            pool.wait_ge(sgu_in, 48)
            for t in range(NT):
                pool.wait_ge(vn_ready, t + 1)
                G.tensor_tensor(vn[:, t, :], vn[:, t, :], sgu_g[:, :], ALU.mult).then_inc(vn_scaled, 1)
            for n in range(4):
                for t in range(NT):
                    add_halves(("qk", n, t), t, 4, HD)
            m = moes[0]
            norm_pool(pool, m, then)
            moe_pool(pool, m)

            def inverse_rms(dst, n, width, ready):
                then(G.tensor_scalar(dst, dst if n is None else n, 1.0 / width, EPS, ALU.mult, ALU.add))
                G.tensor_tensor(dst, dst, c("nhalf")[:, 0:dst.shape[1]], ALU.pow).then_inc(ready, 1)

            G.memset(meta, 0.0).then_inc(meta_cleared, 1)
            pool.wait_ge(sumsq, TILES_BEFORE["out1"] + NT)
            inverse_rms(rstd[:, 0:4], ssq[:, 0:4], D, rms)
            pool.wait_ge(sumsq, TILES_BEFORE["in2"] + NT2)
            pool.wait_ge(scaled, TILES_BEFORE["out1"] + NT)
            inverse_rms(rstd[:, 4:9], ssq[:, 4:9], D, rms)
            pool.wait_ge(squares_ready, 2)
            then(G.tensor_scalar(rstd[:, 0:32], rstd[:, 0:32], 1.0 / SBD, EPS, ALU.mult, ALU.add))
            then(G.tensor_scalar(rstd[:, 32:48], rstd[:, 32:48], 1.0 / HD, EPS, ALU.mult, ALU.add))
            G.tensor_tensor(rstd[:, :], rstd[:, :], c("nhalf"), ALU.pow).then_inc(rms, 1)
            m = moes[1]
            norm_pool(pool, m, then)
            moe_pool(pool, m)
            pool.wait_ge(sumsq, TILES_BEFORE["out2"] + NT)
            inverse_rms(rstd[:, 0:4], ssq[:, 0:4], D, rms)


def kernel(**inputs):
    import concourse.bacc as bacc
    from concourse.bass_utils import run_bass_kernel_spmd as run

    def a(name):
        return np.asarray(inputs[name])

    def chunks(w):
        return w.reshape(w.shape[0] // P, P, w.shape[1]).transpose(1, 0, 2).reshape(P, -1)

    def experts(w):
        e, k, n = w.shape
        return w.reshape(e, k // P, P, n).transpose(0, 2, 1, 3).reshape(e, P, -1)

    def column(v):
        return v.reshape(-1, P).T

    w_in = a("w_in")[0]
    widths = [("q", 1024), ("k", 1024), ("v", 1024), ("qi", 512), ("ki", 64), ("wi", 8), ("su", 1024), ("sv", 1024),
              ("ga", 1024), ("gb", 1024)]
    parts, start = {}, 0
    for name, width in widths:
        parts[name] = w_in[:, start:start + width]
        start += width
    parts["wa"], parts["wb"], parts["wo"] = a("w_branch_a")[0], a("w_branch_b")[0], a("w_out")[0]

    def tile(name):
        if name == "qi":
            return chunks(parts["qi"])
        n = int(name[-1])
        return chunks(parts[name[:-1]][:, n * 512:(n + 1) * 512])

    w_in2 = a("w_in_2")[0]
    order2 = ["sbq", "sbk", "sbv", "hq", "hf", "hi", "hg"]
    parts2 = {name: w_in2[:, n * 512:(n + 1) * 512] for n, name in enumerate(order2)}
    for n in range(2):
        parts2[f"wo2_{n}"] = a("w_out_2")[0][:, n * 512:(n + 1) * 512]

    arrays = {
        "x": a("x")[0],
        "positions": a("positions")[0].reshape(NT, P).T,
        "constants": CONSTANTS,
        "norm1": column(a("norm1_g")[0]),
        "stream_a": np.stack([tile(name) for name in STREAM1]),
        "kiwi": chunks(np.concatenate([parts["ki"], parts["wi"]], axis=1)),
        "sgu_norm": a("sgu_norm_g"),
        "sgu_w": a("sgu_w")[0],
        "sgu_b": a("sgu_b")[0],
        "norm2": a("norm2_g"),
        "router": chunks(np.concatenate([a("w_router_group")[0], a("w_router_expert")[0]], axis=1)),
        "router_b": np.concatenate([a("b_router_group"), a("b_router_expert")], axis=1),
        "expert_in": experts(a("w_expert_in")[0]),
        "expert_out": experts(a("w_expert_out")[0]),
        "meta": a("meta_tokens_2"),
        "lb": a("lb_logits_2").reshape(2, HGH, P).transpose(2, 0, 1).reshape(P, 2 * HGH),
        "mix_norm": column(a("g_mix_2")[0]),
        "stream_b": np.stack([chunks(parts2[name]) for name in STREAM2]),
        "sb_gain": a("sb_gain_2"),
        "hg_gain": a("hg_gain_2"),
        "ffn_norm": a("g_ffn_2"),
        "router2": chunks(np.concatenate([a("w_router_group_2")[0], a("w_router_expert_2")[0]], axis=1)),
        "router2_b": np.concatenate([a("b_router_group_2"), a("b_router_expert_2")], axis=1),
        "expert_gate": experts(a("w_expert_gate_2")[0]),
        "expert_up": experts(a("w_expert_up_2")[0]),
        "expert_down": experts(a("w_expert_down_2")[0]),
        "final_norm2": a("g_final_2").reshape(1, D),
        "final_norm1": a("norm_f_g").reshape(1, D),
    }
    arrays = {"in_" + name: np.ascontiguousarray(v) for name, v in arrays.items()}
    nc = bacc.Bacc("TRN2", target_bir_lowering=False, num_devices=1)
    args = [nc.dram_tensor(name, v.shape, mybir.dt.from_np(v.dtype), kind="ExternalInput").ap()
            for name, v in arrays.items()]
    args.append(nc.dram_tensor("out_0", (1, SEQ, D), F32, kind="ExternalOutput").ap())
    build(nc, *args)
    r = run(nc, [arrays], core_ids=[0])
    return r.results[0]["out_0"]
```

```python
import concourse.bass as bass
from concourse import mybir
from contextlib import ExitStack
import numpy as np

F32 = mybir.dt.float32
F32R = mybir.dt.float32r
I32 = mybir.dt.int32
U32 = mybir.dt.uint32
ALU = mybir.AluOpType
ACT = mybir.ActivationFunctionType
AX = mybir.AxisListType

P = 128
D = 1024
SEQ = 512
NT = SEQ // P
KC = D // P
HEADS, HD = 8, 128
IH, ID = 8, 64
TOPK = 128
GROUPS = 8
NG, EPG = 4, 8
NE = NG * EPG
SLOTS = 64
OVER = 2 * SEQ // SLOTS - 1
CLEARS_A_BLOCK = (OVER + 1) * SLOTS // P
CLEARS = 8
EPS = 1e-6
NEG = -1.0e30
TAKEN = -3.0e38
NT2 = NT + 1
L2 = NT2 * P
META = 16
SBH, SBD = 8, 64
HGH = 4
LEVELS = 7
BANKS = 8
RING = 3
TILE = 4096
HALF_TILE = TILE // 2

CONST_COLS = {}


def constant_table():
    parts = []

    def put(name, a):
        a = np.broadcast_to(np.asarray(a, np.float32), (P, a.shape[-1]))
        start = sum(q.shape[1] for q in parts)
        CONST_COLS[name] = (start, start + a.shape[1])
        parts.append(a)

    i = np.arange(P)
    row, col = i[:, None], i[None, :]
    put("ident", (row == col) * 1.0)
    put("ones", np.ones((P, P)))
    put("tri_ge", (row >= col) * 1.0)
    put("tri_lt", (row < col) * 1.0)
    put("le", (row <= col) * 1.0)
    put("causal", np.where(col <= row, 0.0, NEG))
    put("strict", np.where(row < col, 0.0, NEG))
    put("pad_rows", np.where(row >= P - META, 0.0, NEG)[:, :1])
    put("invf", 10000.0 ** (-np.arange(0, HD, 2, dtype=np.float32) / np.float32(HD))[None, :])
    put("iota_m", (np.arange(NE) - 99.0)[None, :])
    put("iota_e", np.arange(NE)[None, :])
    put("iota_slot", np.arange(SLOTS)[None, :])
    put("token", i[:, None] + P * np.arange(NT)[None, :])
    put("iota_p", i[:, None])
    put("nhalf", np.full((1, 48), -0.5))
    levels = []
    for lv in range(LEVELS):
        h = P >> (lv + 1)
        same = (row // (2 * h)) == (col // (2 * h))
        levels.append((same & ((row // h) % 2 == 0) & ((col // h) % 2 == 1)) * 1.0)
    levels.append((row == col) * 1.0)
    put("levels", np.concatenate(levels, axis=1))
    return np.ascontiguousarray(np.concatenate(parts, axis=1).astype(np.float32))


CONSTANTS = constant_table()


class Units:

    def __init__(self):
        self.index, self.reader = {}, []

    def add(self, key, reader):
        assert key not in self.index, key
        self.index[key] = len(self.reader)
        self.reader.append(reader)

    def bank(self, key):
        return self.index[key] % BANKS

    def filled(self, key):
        return self.index[key] + 1

    def read_count(self, key):
        i = self.index[key]
        who = self.reader[i]
        return who, self.reader[:i + 1].count(who)

    def read_before(self, key):
        old = self.index[key] - BANKS
        if old < 0:
            return None, 0
        who = self.reader[old]
        return who, self.reader[:old + 1].count(who)


def attention_widths():
    starts = [0]
    for t in range(NT):
        starts.append(starts[-1] + (t + 1) * P)
    return starts


CAUSAL_AT = attention_widths()
CAUSAL = CAUSAL_AT[-1]
SCORE_AT = [None] + [a - P for a in CAUSAL_AT[1:NT]]

STREAM1 = (["qi", "sv0", "sv1", "su0", "su1", "ga0", "ga1", "wa0", "wa1", "q0", "q1", "k0", "k1", "v0", "v1",
            "gb0", "gb1", "wb0", "wb1", "wo0", "wo1"])
STREAM2 = ["sbq", "sbk", "sbv", "hi", "hq", "hg", "hf", "wo2_0", "wo2_1"]


def first_block_units():
    u = Units()
    for k in range(KC):
        u.add(("xT", k), "dve")
    for t in range(NT):
        u.add(("qi", t), "dve")
    u.add("kiwi", "dve")
    for t in range(NT):
        u.add(("qiT", t), "act")
    u.add("kiT", "act")
    for t in range(1, NT):
        for h in range(IH):
            u.add(("idx", t, h), "act")
    for n in range(2):
        for t in range(NT):
            u.add(("sv", n, t), "act")
    for m in range(KC):
        u.add(("su", m), "act")
    for m in range(4):
        u.add(("ga", m), "act")
    for n in range(2):
        u.add(("wT", n), "dve")
    for g in range(GROUPS):
        u.add(("mix", g), "dve")
    for m in range(4, KC):
        u.add(("ga", m), "act")
    for m in range(KC):
        u.add(("wa", m), "dve")
    for n in range(5):
        if n < 4:
            for t in range(NT):
                u.add(("qk", n, t), "dve")
        if n >= 1:
            for t in range(NT):
                u.add(("qkT", n - 1, t), "act")
    for n in range(2):
        for t in range(NT):
            u.add(("v", n, t), "act")
    for h in range(HEADS + 2):
        if h < HEADS:
            for t in range(NT):
                u.add(("S", h, t), "dve")
        if h >= 2:
            for t in range(NT):
                u.add(("T", h - 2, t), "act")
            u.add(("O", h - 2), "act")
    for m in range(KC):
        u.add(("gb", m), "act")
    for m in range(KC):
        u.add(("wb", m), "dve")
    for n in range(2):
        for t in range(NT):
            u.add(("wo", n, t), "dve")
    for t in range(NT):
        for half in range(2):
            u.add(("x2T", t, half), "act")
    u.add("router", "dve")
    u.add("ranks", "dve")
    u.add("slots", "dve")
    return u


FIRST_T = [max(s, 1) - 1 for s in range(NT2)]
STICK_W = [SEQ - P * f for f in FIRST_T]
STICK_AT = [sum(STICK_W[:s]) for s in range(NT2)]
STICK = sum(STICK_W)


def second_block_units():
    u = Units()
    for n in range(2):
        u.add(("metaT", n), "dve")
    for t in range(NT):
        for half in range(2):
            u.add(("hT", t, half), "dve")
    for m in range(4):
        u.add(("sbq", m), "act")
    for m in range(4):
        u.add(("sbk", m), "act")
    u.add("sbk_meta", "act")
    for t in range(NT2):
        u.add(("sbv", t), "act")
    for t in range(NT2):
        u.add(("hi", t), "act")
    for m in range(4):
        u.add(("hq", m), "act")
    for t in range(NT):
        u.add(("hg", t), "act")
    for m in range(4):
        u.add(("hf", m), "act")
    u.add("hf_meta", "act")
    for h in range(SBH + 2):
        if h < SBH:
            for s in range(NT2):
                u.add(("Z", h, s), "dve")
        if 1 <= h <= SBH:
            for s in range(NT2):
                u.add(("R", h - 1, s), "dve")
        if h >= 2:
            u.add(("SO", h - 2), "act")
    for h in range(HGH):
        for lv in range(LEVELS):
            if lv == 0:
                u.add(("KT", h), "act")
                u.add(("DG", h), "dve")
            u.add(("L", h, lv), "dve")
            if lv == 2:
                u.add(("KV", h), "dve")
            if lv == 1 and h >= 1:
                u.add(("HO", h - 1), "act")
    u.add(("HO", HGH - 1), "act")
    for k in range(KC):
        u.add(("mT", k), "dve")
    for n in range(2):
        for t in range(NT):
            u.add(("wo2", n, t), "dve")
    for t in range(NT):
        for half in range(2):
            u.add(("x2T", t, half), "act")
    u.add("router", "dve")
    u.add("ranks", "dve")
    u.add("slots", "dve")
    return u


def build(nc, x_in, pos_in, consts_in, g1_in, stream_a, kiwi_in, sgug_in, sguw_in, sgub_in, g2_in, wr_in, br_in,
          we_in, we_out, meta_in_dram, lb_in, gmix_in, stream_b, sbg_in, hgg_in, gffn_in, wr2_in, br2_in,
          wg2_in, wu2_in, wd2_in, gfin_in, gf_in, out, upto=99):
    ctx = ExitStack()
    with ctx:
        def sb(name, shape, dt=F32):
            return ctx.enter_context(nc.sbuf_tensor(name, shape, dt))

        def sem(name):
            return ctx.enter_context(nc.semaphore(name))

        def dram(name, shape, dt=F32):
            return nc.dram_tensor(name, shape, dt, kind="Internal").ap()

        bank = [ctx.enter_context(nc.psum_tensor(f"bank{i}", [P, 512], F32)) for i in range(BANKS)]

        cst = sb("cst", [P, CONSTANTS.shape[1]])

        def sb_and_place(name, shape):
            place = -(-nc.sbuf_base // 32) * 32
            return sb(name, shape), place

        def part(name, place, start, shape):
            t_ = nc.alloc_sbuf_tensor_at(name, [P, *shape], F32R, offset=place + 4 * start)
            return t_[:, :, :]

        x, x_place = sb_and_place("resid", [P, NT, D])
        x_flat = x[:, :, :].rearrange("p t d -> p (t d)")
        ring, ring_place = zip(*[sb_and_place(f"ring{i}", [P, TILE]) for i in range(RING)])
        arena, arena_place = sb_and_place("arena", [P, 7 * TILE])
        misc, misc_place = sb_and_place("misc", [P, 4096])

        def c(name, rows=P):
            a, b = CONST_COLS[name]
            return cst[0:rows, a:b]

        def at(base, start, shape, dt=F32):
            size = int(np.prod(shape))
            v = base[:, start:start + size]
            if dt is not F32:
                v = v.bitcast(dt)
            if len(shape) == 2:
                v = v.rearrange("p (a b) -> p a b", b=shape[1])
            if len(shape) == 3:
                v = v.rearrange("p (a b c) -> p a b c", b=shape[1], c=shape[2])
            return v

        def big(n, shape):
            return at(arena, n * TILE, shape)

        xnT = big(0, [KC, SEQ])
        xs = big(1, [NT, D])
        vn = big(1, [NT, D])
        suT = big(2, [KC, SEQ])
        gT = big(3, [KC, SEQ])
        sgu_w = at(arena, 4 * TILE, [GROUPS, P])
        wT = at(arena, 4 * TILE + 1024, [GROUPS, P])
        sgu_b = at(arena, 4 * TILE + 2048, [GROUPS, P])
        sgu_g = at(arena, 4 * TILE + 3072, [D])
        scores = at(arena, 5 * TILE, [CAUSAL - P])
        qiT = at(arena, 5 * TILE + 1152, [IH // 2, SEQ])
        kiT = at(arena, 5 * TILE + 3200, [SEQ])
        pT = at(arena, 5 * TILE + 1152, [NT, SEQ])
        rot_a = at(arena, 6 * TILE, [2, 512])
        rot_b = at(arena, 6 * TILE + 1024, [2, 512])
        rot = at(arena, 6 * TILE + 2048, [4, 512])
        yT = big(6, [KC, SEQ])
        qT = big(1, [HEADS, SEQ])
        kT = big(2, [HEADS, SEQ])
        v_rows = big(4, [NT, D])
        gbT = big(1, [KC, SEQ])
        zeros = at(arena, 3 * TILE, [D])
        xn_parts = (part("xn_high", arena_place, 0, [KC, SEQ]), part("xn_low", x_place, 0, [KC, SEQ]))
        su_parts = (part("su_high", arena_place, 2 * TILE, [KC, SEQ]), part("su_low", arena_place, 6 * TILE, [KC, SEQ]))
        y_parts = (part("y_high", arena_place, 2 * TILE, [KC, SEQ]), part("y_low", arena_place, 6 * TILE, [KC, SEQ]))
        g_parts = (part("g_high", arena_place, 0, [KC, SEQ]), part("g_low", arena_place, 3 * TILE, [KC, SEQ]))
        ring_raw = [r_[:, 0:HALF_TILE] for r_ in ring]
        ring_parts = [(part(f"ring{i}_high", r_, HALF_TILE, [KC // 2, 512]), part(f"ring{i}_low", r_, 0, [KC // 2, 512])) 
                      for i, r_ in enumerate(ring_place)]
        rel = at(misc, 0, [3, 512])
        probs = [at(misc, i * CAUSAL, [CAUSAL]) for i in range(3)]
        cos = at(misc, 2560, [NT, HD // 2])
        sin = at(misc, 2816, [NT, HD // 2])
        trig = at(misc, 0, [4, NT * HD // 2])
        kirot = at(misc, 3072, [NT, P])
        kiwi_w = at(arena, 2 * TILE, [KC, 72])
        kiwi_parts = (part("kiwi_high", arena_place, 2 * TILE + KC * 72, [KC, 72]), part("kiwi_low", arena_place, 2 * TILE, [KC, 72]))
        wi = sb("wi", [P, NT, IH])
        g1 = sb("g1", [P, KC])
        pos_i = sb("pos_i", [P, NT], I32)
        pos_f = sb("pos_f", [P, NT])
        ssq = sb("ssq", [P, 16])
        rstd = sb("rstd", [P, 48])
        top8 = sb("top8", [P, 8])
        bn6 = sb("bn6", [P, NT, 2, 6])
        bn2 = sb("bn2", [P, NT, 2])
        mx = sb("mx", [P, HEADS, NT])
        nm = sb("nm", [P, HEADS, NT])
        sums = sb("sums", [P, HEADS, NT])
        inv = sb("inv", [P, HEADS, NT])

        U = first_block_units()
        def last_unit(name):
            kind, n = (name[:-1], int(name[-1])) if name[-1].isdigit() else (name, 0)
            if kind == "qi":
                return ("qi", NT - 1)
            if kind in ("q", "k"):
                return ("qk", n + 2 * (kind == "k"), NT - 1)
            if kind in ("sv", "v", "wo"):
                return (kind, n, NT - 1)
            return (kind, 4 * n + 3)

        n_stream = {name: n for n, name in enumerate(STREAM1)}

        psum_filled = sem("psum_filled")
        read_by = {"act": sem("bank_read_act"), "dve": sem("bank_read_dve")}
        weights = [sem(f"weights{i}") for i in range(RING)]
        weights_split = sem("weights_split")
        half_used = sem("half_used")
        kiwi_split = sem("kiwi_split")
        
        consts_in_s = sem("consts_in"); x_in_s = sem("x_in_s"); small_in = sem("small_in"); sgu_in = sem("sgu_in")
        dve_step = sem("dve_step"); act_step = sem("act_step"); pool_step = sem("pool_step")
        sumsq = sem("sumsq"); rms = sem("rms"); scaled = sem("scaled")
        TILES_BEFORE = {"in": 0, "moe0": 4, "between": 8, "moe1": 17, "out2": 21}
        ROOTS_BEFORE = {"in": 0, "sgu": 1, "moe0": 2, "between": 6, "heads": 15, "moe1": 16, "out2": 20}
        BETWEEN = ["meta", "out0", "out1", "in0", "out2", "in1", "out3", "in2", "in3"]
        BETWEEN_COLUMN = {"meta": 4, **{f"out{t}": t for t in range(NT)}, **{f"in{t}": 5 + t for t in range(NT)}}
        
        angles_ready = sem("angles_ready"); trig_ready = sem("trig_ready")
        rotated = sem("rotated"); 
        
        rel_used = sem("rel_used")
        var_ready = sem("var_ready"); vn_ready = sem("vn_ready")
        vn_scaled = sem("vn_scaled")
        
        gated = sem("gated"); y_split = sem("y_split")
        logits_ready = sem("logits_ready"); exp_ready = sem("exp_ready"); probs_ready = sem("probs_ready")
        
        merged = sem("merged"); 
        stored = sem("stored")

        token_id = sb("token_id", [P, NT], I32)
        no_token = sb("no_token", [P, (NE + OVER + 1) * SLOTS // P], I32)
        ids_ready = sem("ids_ready")
        waits_passed = sem("waits_passed")

        def alone(eng):
            eng.sem_inc(waits_passed, 1)

        gather_in = [sem(f"gather_in{j}") for j in range(4)]

        STEPS = 4
        xg_in = [sem(f"xg_in{j}") for j in range(STEPS)]

        routed = sem("routed"); router_in = sem("router_in"); exp_in = sem("exp_in"); exp_out = sem("exp_out")

        class Moe:

            def __init__(self, b, f_chunks, depth):
                self.b, self.F, self.depth = b, f_chunks, depth
                self.xg_base = b * 16 * (NE // STEPS)
                self.tiles, self.roots = TILES_BEFORE[f"moe{b}"], ROOTS_BEFORE[f"moe{b}"]
                self.tr_done = sem(f"tr_done{b}")
                self.h_done = sem(f"h_done{b}")
                self.y_done = sem(f"y_done{b}")
                self.xgT_ready = sem(f"xgT_ready{b}")
                self.sg_ready = sem(f"sg_ready{b}")
                self.act_ready = sem(f"act_ready{b}")
                self.y_free_act = sem(f"y_free_act{b}")
                self.y_free_dve = sem(f"y_free_dve{b}")
                self.rows_stored = sem(f"rows_stored{b}")
                self.slots_written = sem(f"slots_written{b}")
                self.over_stored = sem(f"over_stored{b}")
                self.over_in = sem(f"over_in{b}")
                self.over_tr = sem(f"over_tr{b}")
                self.over_h = sem(f"over_h{b}")
                self.over_y = sem(f"over_y{b}")
                self.over_xgT = sem(f"over_xgT{b}")
                self.over_sg = sem(f"over_sg{b}")
                self.over_act = sem(f"over_act{b}")
                self.over_y_act = sem(f"over_y_act{b}")
                self.over_y_dve = sem(f"over_y_dve{b}")
                self.table_cleared = sem(f"table_cleared{b}")
                self.rows_cleared = sem(f"rows_cleared{b}")
                self.moe_added = sem(f"moe_added{b}")
                self.index_copied = sem(f"index_copied{b}")
                self.normed = sem(f"normed{b}")
                self.y_stored = [sem(f"y_stored{b}_{j}") for j in range(2)]
                slots = [big(4 + i, [TILE]) for i in range(3)] + [r[:, :] for r in ring]
                if b == 0:
                    half = TILE // 2
                    self.places = [(slots[(0, 1, 3, 4)[j]], slots[(2, 2, 5, 5)[j]][:, (j % 2) * half:(j % 2 + 1) * half])
                                   for j in range(4)]
                else:
                    self.places = [tuple(slots[3 * j:3 * j + 3]) for j in range(2)]
                self.sources = (we_in, we_out) if b == 0 else (wg2_in, wu2_in, wd2_in)
                self.tile_in = [[sem(f"tile_in{b}_{j}_{i}") for i in range(len(self.places[0]))] for j in range(depth)]
                self.over_tile = [sem(f"over_tile{b}_{i}") for i in range(len(self.places[0]))]
                self.slot_token = dram(f"slot_token{b}", [(NE + OVER + 1) * SLOTS, 1], I32)
                self.xn_rows = dram(f"xn_rows{b}", [SEQ, D])
                self.y_rows = dram(f"y_rows{b}", [(NE + OVER + 1) * SLOTS, D])
                self.xg = big(1, [STEPS, D])
                self.xgT = at(arena, 2048, [2, KC, SLOTS])
                self.sg = at(arena, 3072, [2, 4 * SLOTS])
                self.actT = at(arena, 3584, [2, 4, SLOTS])
                self.y = at(arena, 0, [2, D])
                self.rows = big(1, [NT, D])
                self.xnT = big(2, [KC, SEQ])
                self.gathered = big(2, [4, D])
                self.gain = at(misc, 2048, [D])
                self.wr = at(misc, 3072, [KC, NG + NE])
                self.br = at(misc, 3360, [NG + NE])
                self.inputs = (g2_in, wr_in, br_in) if b == 0 else (gffn_in, wr2_in, br2_in)
                self.gates = sb(f"gates{b}", [P, 2, NT])
                self.slot_at = sb(f"slot_at{b}", [P, 2 * NT], I32)
                self.row_at = sb(f"row_at{b}", [P, 2 * NT], I32)
                self.over = sb(f"over{b}", [P, 16], I32)
                self.table = sb(f"table{b}", [SLOTS, NE], I32)
                self.index = sb(f"index{b}", [SLOTS, STEPS], I32)

            def tile_value(self, it, j):
                return it * (16 * STEPS // self.depth) + 16 * (j // self.depth + 1)

        moes = [Moe(0, 2, 4), Moe(1, 4, 2)]

        def moe_gate_up(pe, m, j, parity, done):
            for part in range(2):
                h = bank[2 + 2 * part + parity]
                if part == 1 and m.b == 1:
                    moe_wait(pe, m, j, 1)
                for f in range(m.F):
                    col = f * SLOTS
                    for k in range(KC):
                        if m.b == 0:
                            w = m.places[j % m.depth][0][:, k * 512 + (part * m.F + f) * P:k * 512 + (part * m.F + f + 1) * P]
                        else:
                            w = m.places[j % m.depth][part][:, k * 512 + f * P:k * 512 + (f + 1) * P]
                        last = nc.tensor.matmul(h[:, col:col + SLOTS], w, m.xgT[:, parity, k, :],
                                                start=(k == 0), stop=(k == KC - 1))
                last.then_inc(done, 1)

        def moe_down(m, j, parity, done):
            w = m.places[j % m.depth][-1]
            for n in range(2):
                for f in range(m.F):
                    last = nc.tensor.matmul(bank[6 + n][0:SLOTS, :], m.actT[:, parity, f, :],
                                            w[:, f * D + n * 512:f * D + n * 512 + 512],
                                            start=(f == 0), stop=(f == m.F - 1))
                last.then_inc(done, 1)

        def moe_transposes(m, j, done):
            for k in range(KC):
                last = nc.tensor.transpose(bank[j % 2][:, k * SLOTS:(k + 1) * SLOTS],
                                           m.xg[0:SLOTS, j, k * P:(k + 1) * P], c("ident", SLOTS)[:, 0:SLOTS])
            last.then_inc(done, 1)

        moe_expect = {}

        def moe_wait(pe, m, j, i):
            pe.wait_ge(*moe_expect[m.b, j, i])

        def moe_load(sp, m, e, j, i):
            src = m.sources[i][bass.ds(e, 1), :, :].rearrange("e p c -> p (e c)") if not isinstance(e, int) \
                else m.sources[i][e, :, :]
            sp.dma_start(m.places[j][i], src).then_inc(m.tile_in[j][i], 16)

        def router_inputs_sp(sp, m):
            sp.dma_start(m.gain, m.inputs[0].broadcast_to([P, D])).then_inc(router_in, 16)
            sp.dma_start(m.wr, m.inputs[1].rearrange("p (k c) -> p k c", k=KC)).then_inc(router_in, 16)
            sp.dma_start(m.br, m.inputs[2].broadcast_to([P, NG + NE])).then_inc(router_in, 16)

        def moe_sp(sp, m):
            n_tiles = len(m.places[0])
            with sp.Fori(0, NE // m.depth - 1) as it:
                for j in range(m.depth):
                    for i in range(n_tiles):
                        done = m.y_done if i == n_tiles - 1 else m.h_done
                        gate_only = m.b == 1 and i == 0
                        sp.wait_ge(done, it * (2 * m.depth) + (2 * j + (1 if gate_only else 2)))
                        moe_load(sp, m, it * m.depth + (m.depth + j), j, i)
            alone(sp)
            n_over = sp.value_load(m.over[0:1, 0:1], min_val=0, max_val=OVER)
            with sp.Fori(0, OVER) as v:
                with sp.If(v < n_over):
                    sp.wait_ge(m.y_done, 2 * NE)
                    e = sp.value_load(m.over[0:1, bass.ds(v + 1, 1)], min_val=0, max_val=NE - 1)
                    for i in range(n_tiles):
                        src = m.sources[i][bass.ds(e, 1), :, :].rearrange("e p c -> p (e c)")
                        sp.dma_start(m.places[0][i], src).then_inc(m.over_tile[i], 16)
                    sp.wait_ge(m.over_y_act, v + 1)
                    sp.wait_ge(m.over_y_dve, v + 1)
                    sp.dma_start(m.y_rows[bass.ds(v * SLOTS + NE * SLOTS, SLOTS), :], m.y[0:SLOTS, 0, :])\
                        .then_inc(m.over_stored, 16)
                    sp.wait_ge(m.over_stored, v * 16 + 16)
                    alone(sp)

        def moe_pe(pe, m):
            pe.sem_inc(m.tr_done, STEPS)
            pe.wait_ge(xg_in[0], m.xg_base + 16)
            moe_transposes(m, 0, m.tr_done)

            def experts(it, is_last):
                for j in range(STEPS):
                    q = j % 2
                    pe.wait_ge(m.tile_in[j % m.depth][0], m.tile_value(it, j))
                    moe_expect[m.b, j, 1] = (m.tile_in[j % m.depth][1], m.tile_value(it, j))
                    pe.wait_ge(m.xgT_ready, it * STEPS + (j + 1))
                    moe_gate_up(pe, m, j, q, m.h_done)
                    if not (is_last and j == STEPS - 1):
                        pe.wait_ge(xg_in[(j + 1) % STEPS], it * 16 + (m.xg_base + 16 * (1 + (j + 1) // STEPS)))
                        alone(pe)
                        moe_transposes(m, (j + 1) % STEPS, m.tr_done)
                    pe.wait_ge(m.tile_in[j % m.depth][-1], m.tile_value(it, j))
                    pe.wait_ge(m.act_ready, it * STEPS + (j + 1))
                    pe.wait_ge(m.y_free_act, it * STEPS + (j + 1))
                    pe.wait_ge(m.y_free_dve, it * STEPS + (j + 1))
                    moe_down(m, j, q, m.y_done)

            with pe.Fori(0, NE // STEPS - 1) as it:
                experts(it, False)
            experts(NE // STEPS - 1, True)
            n_over = pe.value_load(m.over[0:1, 0:1], min_val=0, max_val=OVER)
            with pe.Fori(0, OVER) as v:
                with pe.If(v < n_over):
                    pe.wait_ge(m.y_free_act, NE + 1)
                    pe.wait_ge(m.y_free_dve, NE + 1)
                    pe.wait_ge(m.over_in, v * 32 + 32)
                    alone(pe)
                    moe_transposes(m, 0, m.over_tr)
                    pe.wait_ge(m.over_tile[0], v * 16 + 16)
                    moe_expect[m.b, 0, 1] = (m.over_tile[1], v * 16 + 16)
                    pe.wait_ge(m.over_xgT, v + 1)
                    moe_gate_up(pe, m, 0, 0, m.over_h)
                    pe.wait_ge(m.over_tile[-1], v * 16 + 16)
                    pe.wait_ge(m.over_act, v + 1)
                    moe_down(m, 0, 0, m.over_y)
                    pe.wait_ge(m.over_y_act, v + 1)
                    pe.wait_ge(m.over_y_dve, v + 1)
                    alone(pe)

        def moe_act(act, m):
            w = m.F * SLOTS
            act.sem_inc(m.y_free_act, 1)
            for q in range(2):
                act.sem_inc(m.y_stored[q], 16)
            with act.Fori(0, NE // STEPS) as it:
                for j in range(STEPS):
                    q = j % 2
                    act.wait_ge(m.h_done, it * (2 * STEPS) + (2 * j + 1))
                    nc.scalar.activation(m.sg[:, q, 0:w], bank[2 + q][:, 0:w], ACT.Silu).then_inc(m.sg_ready, 1)
                    act.wait_ge(m.y_done, it * (2 * STEPS) + (2 * j + 1))
                    act.wait_ge(m.y_stored[q], it * (8 * STEPS) + 16 * (j // 2 + 1))
                    nc.scalar.copy(m.y[0:SLOTS, q, 0:512], bank[6][0:SLOTS, :]).then_inc(m.y_free_act, 1)
                    act.wait_ge(m.y_free_act, it * STEPS + (j + 2))
                    act.wait_ge(m.y_free_dve, it * STEPS + (j + 2))
                    act.dma_start(m.y_rows[bass.ds(it * (STEPS * SLOTS) + j * SLOTS, SLOTS), :],
                                  m.y[0:SLOTS, q, :]).then_inc(m.y_stored[q], 16)
            n_over = act.value_load(m.over[0:1, 0:1], min_val=0, max_val=OVER)
            with act.Fori(0, OVER) as v:
                with act.If(v < n_over):
                    act.wait_ge(m.y_stored[0], 8 * NE + 16)
                    act.wait_ge(m.over_h, v * 2 + 1)
                    nc.scalar.activation(m.sg[:, 0, 0:w], bank[2][:, 0:w], ACT.Silu).then_inc(m.over_sg, 1)
                    act.wait_ge(m.over_y, v * 2 + 1)
                    nc.scalar.copy(m.y[0:SLOTS, 0, 0:512], bank[6][0:SLOTS, :]).then_inc(m.over_y_act, 1)
                    act.wait_ge(m.over_stored, v * 16 + 16)
                    alone(act)

        def moe_dve(dve, m, after):
            V, w = nc.vector, m.F * SLOTS
            dve.sem_inc(m.y_free_dve, 1)

            def hidden(q, ready):
                V.tensor_tensor(m.actT[:, q, 0:m.F, :].rearrange("p f s -> p (f s)"), m.sg[:, q, 0:w],
                                bank[4 + q][:, 0:w], ALU.mult).then_inc(ready, 1)

            def tokens(e, q):
                dve.wait_ge(m.tr_done, e)
                V.tensor_copy(m.xgT[:, q, :, :].rearrange("p k s -> p (k s)"), bank[q][:, :])\
                    .then_inc(m.xgT_ready, 1)

            def experts(it, is_last):
                for j in range(STEPS):
                    q = j % 2
                    dve.wait_ge(m.h_done, it * (2 * STEPS) + (2 * j + 2))
                    dve.wait_ge(m.sg_ready, it * STEPS + (j + 1))
                    hidden(q, m.act_ready)
                    if not (is_last and j == STEPS - 1):
                        tokens(it * STEPS + (STEPS + j + 2), 1 - q)
                    dve.wait_ge(m.y_done, it * (2 * STEPS) + (2 * j + 2))
                    dve.wait_ge(m.y_stored[q], it * (8 * STEPS) + 16 * (j // 2 + 1))
                    V.tensor_copy(m.y[0:SLOTS, q, 512:1024], bank[7][0:SLOTS, :]).then_inc(m.y_free_dve, 1)

            tokens(STEPS + 1, 0)
            with dve.Fori(0, NE // STEPS - 1) as it:
                experts(it, False)
            experts(NE // STEPS - 1, True)
            n_over = dve.value_load(m.over[0:1, 0:1], min_val=0, max_val=OVER)
            with dve.Fori(0, OVER) as v:
                with dve.If(v < n_over):
                    dve.wait_ge(m.y_stored[0], 8 * NE + 16)
                    dve.wait_ge(m.over_tr, v + 1)
                    V.tensor_copy(m.xgT[:, 0, :, :].rearrange("p k s -> p (k s)"), bank[0][:, :])\
                        .then_inc(m.over_xgT, 1)
                    dve.wait_ge(m.over_h, v * 2 + 2)
                    dve.wait_ge(m.over_sg, v + 1)
                    hidden(0, m.over_act)
                    dve.wait_ge(m.over_y, v * 2 + 2)
                    V.tensor_copy(m.y[0:SLOTS, 0, 512:1024], bank[7][0:SLOTS, :]).then_inc(m.over_y_dve, 1)
                    dve.wait_ge(m.over_stored, v * 16 + 16)
                    alone(dve)
            for n in range(2 * NT):
                k, t = n % 2, n // 2
                dve.wait_ge(gather_in[n % 4], 16 * (n // 4 + 1) + 32 * m.b)
                if k == 1:
                    dve.wait_ge(m.moe_added, n)
                V.scalar_tensor_tensor(x[:, t, :], m.gathered[:, n % 4, :], m.gates[:, k, t:t + 1], x[:, t, :],
                                       ALU.mult, ALU.add).then_inc(m.moe_added, 1)
                if k == 1:
                    after(t)

        def moe_pool(pool, m, before_overflow, after_gather):
            G = nc.gpsimd
            pool.wait_ge(routed, 2 * m.b + 1)
            pool.wait_ge(m.rows_stored, 16 * NT)
            with pool.Fori(0, NE // STEPS) as it:
                for j in range(STEPS):
                    pool.wait_ge(m.tr_done, it * STEPS + (j + 1))
                    G.tensor_copy(m.index[:, j:j + 1], m.table[:, bass.ds(it * STEPS + j, 1)])\
                        .then_inc(m.index_copied, 1)
                    pool.wait_ge(m.index_copied, it * STEPS + (j + 1))
                    alone(pool)
                    G.indirect_dma_start(m.xg[0:SLOTS, j, :], None, m.xn_rows[:, :],
                                         bass.IndirectOffsetOnAxis(ap=m.index[:, j:j + 1], axis=0))\
                        .then_inc(xg_in[j], 16)
            pool.wait_ge(routed, 2 * m.b + 2)
            pool.wait_ge(m.table_cleared, 16)
            for n in range(2 * NT):
                G.indirect_dma_start(m.slot_token[:, :], bass.IndirectOffsetOnAxis(ap=m.slot_at[:, n:n + 1], axis=0),
                                     token_id[:, n % NT:n % NT + 1], None).then_inc(m.slots_written, 16)
            before_overflow()
            pool.wait_ge(m.slots_written, 16 * 2 * NT)
            n_over = pool.value_load(m.over[0:1, 0:1], min_val=0, max_val=OVER)
            with pool.Fori(0, OVER) as v:
                with pool.If(v < n_over):
                    pool.wait_ge(m.tr_done, NE + STEPS)
                    pool.dma_start(m.index[:, 0:1], m.slot_token[bass.ds(v * SLOTS + NE * SLOTS, SLOTS), :])\
                        .then_inc(m.over_in, 16)
                    pool.wait_ge(m.over_in, v * 32 + 16)
                    alone(pool)
                    G.indirect_dma_start(m.xg[0:SLOTS, 0, :], None, m.xn_rows[:, :],
                                         bass.IndirectOffsetOnAxis(ap=m.index[:, 0:1], axis=0))\
                        .then_inc(m.over_in, 16)
                    pool.wait_ge(m.over_stored, v * 16 + 16)
                    alone(pool)
            for q in range(2):
                pool.wait_ge(m.y_stored[q], 8 * NE + 16)
            for n in range(2 * NT):
                k, t = n % 2, n // 2
                if n >= 4:
                    pool.wait_ge(m.moe_added, n - 3)
                G.indirect_dma_start(m.gathered[:, n % 4, :], None, m.y_rows[:, :],
                                     bass.IndirectOffsetOnAxis(ap=m.row_at[:, k * NT + t:k * NT + t + 1], axis=0))\
                    .then_inc(gather_in[n % 4], 16)
                after_gather(n)

        def norm_act(act, m, ready):
            for t in range(NT):
                ready(act, t)
                nc.scalar.activation(m.rows[:, t, :], x[:, t, :], ACT.Square, accum_out=ssq[:, t:t + 1])\
                    .then_inc(sumsq, 1)

        def inverse_rms(pool, column, squares, then):
            G, v = nc.gpsimd, rstd[:, column:column + 1]
            pool.wait_ge(sumsq, squares)
            then(G.tensor_scalar(v, ssq[:, column:column + 1], 1.0 / D, EPS, ALU.mult, ALU.add))
            G.tensor_tensor(v, v, c("nhalf")[:, 0:1], ALU.pow).then_inc(rms, 1)

        def norm_pool(pool, m, then):
            for t in range(NT):
                inverse_rms(pool, t, m.tiles + t + 1, then)

        def norm_dve(dve, m, t):
            if t == 0:
                dve.wait_ge(router_in, 48 * m.b + 48)
            dve.wait_ge(rms, m.roots + t + 1)
            nc.vector.scalar_tensor_tensor(m.rows[:, t, :], x[:, t, :], rstd[:, t:t + 1], m.gain, ALU.mult, ALU.mult)\
                .then_inc(m.normed, 1)

        def router_sp(sp, m):
            for t in range(NT):
                sp.wait_ge(m.normed, t + 1)
                sp.dma_start(m.xn_rows[t * P:(t + 1) * P, :], m.rows[:, t, :]).then_inc(m.rows_stored, 16)

        def router_pe(pe, m, U, begin, end, transposes, wait_read):
            w = NG + NE
            for t in range(NT + 1):
                if t < NT:
                    pe.wait_ge(m.normed, t + 1)
                    for half in range(2):
                        transposes(("x2T", t, half), [m.rows[:, t, k * P:(k + 1) * P]
                                                      for k in range(4 * half, 4 * half + 4)])
                if t == 1:
                    wait_read(pe, ("x2T", 0, 1))
                    r = begin("router")
                if t >= 1:
                    s = t - 1
                    wait_read(pe, ("x2T", s, 1))
                    for k in range(KC):
                        last = nc.tensor.matmul(r[:, s * w:(s + 1) * w], m.xnT[:, k, s * P:(s + 1) * P], m.wr[:, k, :],
                                                start=(k == 0), stop=(k == KC - 1))
            end(last)
            pe.wait_ge(exp_in, 3 * m.b + 2)
            r = begin("ranks")
            chosen = at(arena, 3 * TILE + 3584, [NT, NE])
            for t in range(NT):
                for s in range(t + 1):
                    last = nc.tensor.matmul(r[:, t * NE:(t + 1) * NE], c("tri_lt") if s == t else c("ones"),
                                            chosen[:, s, :], start=(s == 0), stop=(s == t))
            for s in range(NT):
                last = nc.tensor.matmul(r[:, NT * NE:(NT + 1) * NE], c("ones"), chosen[:, s, :],
                                        start=(s == 0), stop=(s == NT - 1))
            end(last)
            r = begin("slots")
            pe.wait_ge(exp_in, 3 * m.b + 3)
            for n in range(2 * NT):
                last = nc.tensor.matmul(r[0:SLOTS, 0:NE], m.in_slot[:, n, :], m.tagged[:, n, :],
                                        start=(n == 0), stop=(n == 2 * NT - 1))
            end(last)

        def router_act(act, m, unit, read):
            for t in range(NT):
                for half in range(2):
                    b = unit(("x2T", t, half))
                    read(nc.scalar.copy(m.xnT[:, 4 * half:4 * half + 4, t * P:(t + 1) * P],
                                        b[:, :].rearrange("p (k q) -> p k q", q=P)))
            act.wait_ge(exp_in, 3 * m.b + 1)
            nc.scalar.activation(m.ework[0], m.ework[0], ACT.Exp).then_inc(exp_out, 1)
            act.wait_ge(exp_in, 3 * m.b + 2)
            nc.scalar.activation(m.ework[1], m.ework[1], ACT.Exp).then_inc(exp_out, 1)

        for m in moes:
            m.in_slot = at(arena, 3 * TILE, [2 * NT, SLOTS])
            m.tagged = at(arena, 3 * TILE + 2 * NT * SLOTS, [2 * NT, NE])
            m.ework = (at(arena, 3 * TILE + 3400, [NT, NG]), at(arena, 3 * TILE + 3416, [NT]))

        def router_dve(dve, m, unit, read, then, wait_read):
            V = nc.vector
            at3 = [3 * TILE + 2 * NT * (SLOTS + NE)]

            def tmp(*shape):
                v = at(arena, at3[0], list(shape))
                at3[0] += int(np.prod(shape))
                assert at3[0] <= 3 * TILE + 3400
                return v

            w = NG + NE
            logits = tmp(NT, w)
            b = unit("router")
            read(V.tensor_tensor(logits, b[:, 0:NT * w].rearrange("p (t w) -> p t w", w=w),
                                 m.br[:, None, :].broadcast_to([P, NT, w]), ALU.add))
            wait_read(dve, "router")
            gl, el = logits[:, :, 0:NG], logits[:, :, NG:w]

            def bc(v, n):
                return v[:, :, None].broadcast_to([P, NT, n])

            def first_max(values, n, hit):
                best, low = tmp(NT), tmp(NT)
                then(V.tensor_reduce(best, values, AX.X, ALU.max))
                then(V.tensor_tensor(hit, values, bc(best, n), ALU.is_equal))
                then(V.tensor_tensor(hit, hit, c("iota_m")[:, None, 0:n].broadcast_to([P, NT, n]), ALU.mult))
                then(V.tensor_reduce(low, hit, AX.X, ALU.min))
                then(V.tensor_tensor(hit, hit, bc(low, n), ALU.is_equal))
                return best, hit

            hits = tmp(2 * NT, NE)
            gbest, ghit = first_max(gl, NG, tmp(NT, NG))
            V.tensor_tensor(m.ework[0], gl, bc(gbest, NG), ALU.subtract).then_inc(exp_in, 1)
            off = tmp(NT, NG)
            then(V.tensor_scalar(off, ghit, -NEG, NEG, ALU.mult, ALU.add))
            em = tmp(NT, NE)
            split = dict(g=NG, e=EPG)
            then(V.tensor_tensor(em.rearrange("p t (g e) -> p t g e", **split),
                                 el.rearrange("p t (g e) -> p t g e", **split),
                                 off[:, :, :, None].broadcast_to([P, NT, NG, EPG]), ALU.add))
            best1, hit1 = first_max(em, NE, hits[:, 0:NT, :])
            then(V.scalar_tensor_tensor(em, hit1, 3 * NEG, em, ALU.mult, ALU.add))
            best2, hit2 = first_max(em, NE, hits[:, NT:, :])
            chosen = at(arena, 3 * TILE + 3584, [NT, NE])
            then(V.tensor_tensor(chosen, hit1, hit2, ALU.add))
            V.tensor_tensor(m.ework[1], best2, best1, ALU.subtract).then_inc(exp_in, 1)
            dve.wait_ge(exp_out, 2 * m.b + 2)
            gsum, den = tmp(NT), tmp(NT)
            then(V.tensor_reduce(gsum, m.ework[0], AX.X, ALU.add))
            then(V.tensor_scalar(den, m.ework[1], 1.0, None, ALU.add))
            then(V.tensor_tensor(den, den, gsum, ALU.mult))
            then(V.reciprocal(m.gates[:, 0, :], den))
            then(V.tensor_tensor(m.gates[:, 1, :], m.gates[:, 0, :], m.ework[1], ALU.mult))
            by_choice = dict(k=2, t=NT)
            hits4 = hits.rearrange("p (k t) e -> p k t e", **by_choice)
            masked, expert = tmp(2 * NT, NE), tmp(2 * NT)
            masked4 = masked.rearrange("p (k t) e -> p k t e", **by_choice)
            then(V.tensor_tensor(masked, hits, c("iota_e")[:, None, :].broadcast_to([P, 2 * NT, NE]), ALU.mult))
            then(V.tensor_reduce(expert, masked, AX.X, ALU.add))
            then(V.tensor_tensor(m.tagged.rearrange("p (k t) e -> p k t e", **by_choice), hits4,
                                 c("token")[:, None, :, None].broadcast_to([P, 2, NT, NE]), ALU.mult))
            rk = tmp(NT + 1, NE)
            b = unit("ranks")
            read(V.tensor_copy(rk, b[:, 0:(NT + 1) * NE].rearrange("p (t e) -> p t e", e=NE)))
            wait_read(dve, "ranks")
            ranks, counts = rk[:, 0:NT, :], rk[:, NT, :]
            rank = tmp(2 * NT)
            then(V.tensor_tensor(masked4, hits4, ranks[:, None, :, :].broadcast_to([P, 2, NT, NE]), ALU.mult))
            then(V.tensor_reduce(rank, masked, AX.X, ALU.add))
            V.tensor_tensor(m.in_slot, c("iota_slot")[:, None, :].broadcast_to([P, 2 * NT, SLOTS]),
                            rank[:, :, None].broadcast_to([P, 2 * NT, SLOTS]), ALU.is_equal).then_inc(exp_in, 1)
            b = unit("slots")
            read(V.tensor_copy(m.table[:, :], b[0:SLOTS, 0:NE]))
            wait_read(dve, "slots")
            dve.sem_inc(routed, 1)
            more, upto_, before = tmp(NE), tmp(NE), tmp(NE)
            then(V.tensor_scalar(more, counts, float(SLOTS), None, ALU.is_gt))
            for n in range(2, SEQ // SLOTS):
                then(V.scalar_tensor_tensor(more, counts, float(n * SLOTS), more, ALU.is_gt, ALU.add))
            then(V.tensor_tensor_scan(upto_, c("ones")[:, 0:NE], more, 0.0, ALU.mult, ALU.add))
            then(V.tensor_tensor(before, upto_, more, ALU.subtract))
            then(V.tensor_scalar(before, before, float(SLOTS), float((NE - 1) * SLOTS), ALU.mult, ALU.add))
            isover, far, near = tmp(2 * NT), tmp(2 * NT), tmp(2 * NT)
            then(V.tensor_tensor(masked, hits, before[:, None, :].broadcast_to([P, 2 * NT, NE]), ALU.mult))
            then(V.tensor_reduce(far, masked, AX.X, ALU.add))
            then(V.tensor_tensor(far, far, rank, ALU.add))
            then(V.tensor_scalar(isover, rank, float(SLOTS), None, ALU.is_ge))
            for table, scale, a_, b_ in ((m.slot_at, float(NE), rank, expert), (m.row_at, float(SLOTS), expert, rank)):
                then(V.scalar_tensor_tensor(near, a_, scale, b_, ALU.mult, ALU.add))
                d = tmp(2 * NT)
                then(V.tensor_tensor(d, far, near, ALU.subtract))
                then(V.tensor_tensor(d, d, isover, ALU.mult))
                then(V.tensor_tensor(near, near, d, ALU.add))
                then(V.tensor_copy(table[:, :], near))
            owner, le = tmp(16), at(misc, 0, [16, NE])
            then(V.tensor_tensor(le, upto_[:, None, :].broadcast_to([P, 16, NE]),
                                 c("iota_e")[:, 0:16, None].broadcast_to([P, 16, NE]), ALU.is_le))
            then(V.tensor_reduce(owner, le, AX.X, ALU.add))
            then(V.tensor_scalar(owner, owner, float(NE - 1), None, ALU.min))
            then(V.tensor_copy(m.over[:, 1:16], owner[:, 0:15]))
            V.tensor_copy(m.over[:, 0:1], upto_[:, NE - 1:NE]).then_inc(routed, 1)

        U2 = second_block_units()
        n_stream2 = {name: n for n, name in enumerate(STREAM2)}
        psum_filled2 = sem("psum_filled2")
        read_by2 = {"act": sem("bank_read2_act"), "dve": sem("bank_read2_dve")}
        block2_in = sem("block2_in")
        meta_cleared = sem("meta_cleared"); meta_in = sem("meta_in")
        x_normed = sem("x_normed")
        lb_out = sem("lb_out"); lb_exp = sem("lb_exp")
        decay_ready = sem("decay_ready"); last_ready = sem("last_ready"); keys_ready = sem("keys_ready")
        z_ready = sem("z_ready"); log_ready = sem("log_ready"); sp_ready = sem("sp_ready")
        weight_ready = sem("weight_ready"); carried = sem("carried"); log_f_ready = sem("log_f_ready")
        diff_ready = sem("diff_ready"); diff_exp = sem("diff_exp"); level_ready = sem("level_ready")
        kd_exp = sem("kd_exp"); kd_ready = sem("kd_ready"); q_exp = sem("q_exp"); q_ready = sem("q_ready")
        scores_ready = sem("scores_ready"); states_ready = sem("states_ready")
        squared = sem("squared"); squares_ready = sem("squares_ready"); heads_normed = sem("heads_normed")
        result = sem("result")
        high_ready = sem("high_ready")

        base2 = 5376
        hT_parts = (part("hT_high", arena_place, 0, [KC, SEQ]), part("hT_low", arena_place, base2 + 18944, [KC, SEQ]))
        hT_meta = (part("hT_meta_high", arena_place, TILE, [KC, P]), part("hT_meta_low", misc_place, 3072, [KC, P]))
        resid_rows = dram("resid_rows", [SEQ, D])
        xs2 = at(arena, 18944, [NT2, D])
        hv = at(arena, base2, [NT2, HGH * HD])
        sbv = at(arena, base2 + 2560, [NT2, SBH * SBD])
        sbq = at(arena, base2 + 5120, [4, SEQ])
        sbk = at(arena, base2 + 7168, [4, L2])
        hq = at(arena, base2 + 9728, [HGH, SEQ])
        hk = at(arena, base2 + 11776, [HGH, L2])
        bc = at(arena, base2 + 14336, [HGH, L2])
        hgate = at(arena, base2 + 16896, [NT, HGH * HD])
        mixed = at(arena, base2 + 18944, [NT, D])
        assert base2 + 18944 + NT * D <= 7 * TILE
        mixed_parts = (part("mixed_high", arena_place, 0, [KC, SEQ]), part("mixed_low", arena_place, 3 * TILE, [KC, SEQ]))
        zw = [at(arena, i * STICK, [STICK]) for i in range(3)]
        sps = [x_flat[:, i * STICK:(i + 1) * STICK] for i in range(2)]
        diff = at(arena, 0, [2, SEQ]); qE = at(arena, 1024, [2, SEQ]); kE = at(arena, 2048, [2, SEQ])
        hsc = at(arena, 3072, [2, SEQ]); qexp = at(arena, 4096, [2, SEQ])
        kd = at(x_flat, 0, [2, SEQ]); kdR = at(x_flat, 1024, [2, SEQ])
        states = at(x_flat, 2048, [2, NT, P])
        squares = at(arena, 0, [NT, HD])
        sb_gain = at(misc, 0, [512]); hg_gain = at(misc, 512, [512])
        gf = at(misc, 1024, [D])
        meta = at(misc, 2048, [D])
        chunk_decay = sb("chunk_decay", [P, HGH, NT2])
        gmix = at(arena, 3 * TILE + 3072, [D])
        lbl = sb("lbl", [P, 2, HGH]); lb = sb("lb", [P, HGH]); oml = sb("oml", [P, HGH]); lbm = sb("lbm", [P, HGH])

        def norm_pieces2():
            for n in range(2):
                yield ("metaT", n), [v[:, 4 * n:4 * n + 4, :] for v in hT_meta]
            for t in range(NT):
                for n in range(2):
                    yield ("hT", t, n), [v[:, 4 * n:4 * n + 4, t * P:(t + 1) * P] for v in hT_parts]

        def last_unit2(name):
            if name in ("sbq", "hq"):
                return (name, 3)
            if name in ("sbk", "hf"):
                return name + "_meta"
            if name in ("sbv", "hi"):
                return (name, NT2 - 1)
            return (name, NT - 1) if name == "hg" else ("wo2", int(name[-1]), NT - 1)

        def wait_read2(eng, key):
            who, reads = U2.read_count(key)
            eng.wait_ge(read_by2[who], reads)

        block = ctx.enter_context(nc.Block())

        def wait_read(eng, key):
            who, reads = U.read_count(key)
            eng.wait_ge(read_by[who], reads)

        linked = {"dve": 0, "act": 0, "pool": 0}

        def link(name, eng, step, ins):
            linked[name] += 1
            ins.then_inc(step, 1)
            eng.wait_ge(step, linked[name])

        @block.sync
        def _(sp):
            sp.dma_start(x[:, :, :], x_in.rearrange("(t p) d -> p t d", p=P)).then_inc(x_in_s, 16)
            sp.dma_start(cst[:, :], consts_in).then_inc(consts_in_s, 16)
            for n in range(2 * len(STREAM1)):
                if n >= RING:
                    old = n - RING
                    if old % 2 == 0:
                        sp.wait_ge(half_used, old // 2 + 1)
                    else:
                        sp.wait_ge(psum_filled, U.filled(last_unit(STREAM1[old // 2])))
                sp.dma_start(ring_raw[n % RING], stream_a[n // 2, :, (n % 2) * HALF_TILE:(n % 2 + 1) * HALF_TILE])\
                    .then_inc(weights[n % RING], 16)
                if n == 0:
                    sp.dma_start(g1[:, :], g1_in).then_inc(small_in, 16)
                    sp.dma_start(pos_i[:, :], pos_in).then_inc(small_in, 16)
                    sp.dma_start(kiwi_w[:, :, :], kiwi_in.rearrange("p (k c) -> p k c", c=72)).then_inc(small_in, 16)
                if n == RING:
                    sp.dma_start(sgu_w[:, :, :], sguw_in.rearrange("g t s -> t g s")).then_inc(sgu_in, 16)
                    sp.dma_start(sgu_b[:, :, :], sgub_in[None, :, :].broadcast_to([P, GROUPS, P])).then_inc(sgu_in, 16)
                    sp.dma_start(sgu_g[:, :], sgug_in.broadcast_to([P, D])).then_inc(sgu_in, 16)
                    sp.wait_ge(ids_ready, 3)
                    for m in moes:
                        sp.dma_start(m.slot_token.rearrange("(p n) o -> p (n o)", p=P), no_token[:, :])\
                            .then_inc(m.table_cleared, 16)
                if RING <= n < RING + CLEARS:
                    for i in range(2 * CLEARS_A_BLOCK // CLEARS):
                        k = (n - RING) * (2 * CLEARS_A_BLOCK // CLEARS) + i
                        m, row = moes[k // CLEARS_A_BLOCK], NE * SLOTS + k % CLEARS_A_BLOCK * P
                        sp.dma_start(m.y_rows[row:row + P, :], zeros).then_inc(m.rows_cleared, 16)
                if n == 2 * n_stream["wb1"]:
                    sp.wait_ge(psum_filled, U.filled(("gb", KC - 1)))
                    sp.dma_start(x[:, :, :], x_in.rearrange("(t p) d -> p t d", p=P)).then_inc(x_in_s, 16)
            m = moes[0]
            sp.wait_ge(psum_filled, U.filled(("wb", KC - 1)))
            router_inputs_sp(sp, m)
            for (j, i) in ((0, 0), (1, 0), (0, 1), (1, 1)):
                moe_load(sp, m, j, j, i)
            router_sp(sp, m)
            sp.wait_ge(psum_filled, U.filled(("wo", 1, NT - 1)))
            for (j, i) in ((2, 0), (3, 0), (2, 1), (3, 1)):
                moe_load(sp, m, j, j, i)
            moe_sp(sp, m)

            sp.wait_ge(routed, 2 * m.b + 2)
            sp.dma_start(sb_gain, sbg_in.broadcast_to([P, 512])).then_inc(block2_in, 16)
            sp.dma_start(hg_gain, hgg_in.broadcast_to([P, 512])).then_inc(block2_in, 16)
            sp.dma_start(gf, gf_in.broadcast_to([P, D])).then_inc(block2_in, 16)
            sp.dma_start(gmix, gmix_in.broadcast_to([P, D])).then_inc(block2_in, 16)
            sp.dma_start(lbl[:, :, :], lb_in.rearrange("p (r h) -> p r h", r=2)).then_inc(block2_in, 16)
            sp.wait_ge(meta_cleared, 1)
            sp.dma_start(meta[P - META:P, :], meta_in_dram).then_inc(meta_in, 16)
            sp.wait_ge(m.y_done, 2 * NE)
            first = 2 * len(STREAM1)
            for n in range(first, first + 2 * len(STREAM2)):
                old = n - RING
                if n == first + RING:
                    for t in range(NT):
                        sp.wait_ge(x_normed, t + 1)
                        sp.dma_start(resid_rows[t * P:(t + 1) * P, :], x[:, t, :]).then_inc(stored, 16)
                if n == first + 2 * len(STREAM2) - 1:
                    sp.wait_ge(psum_filled2, U2.filled(("HO", HGH - 1)))
                    sp.wait_ge(stored, 16 * NT)
                    sp.dma_start(x[:, :, :], resid_rows.rearrange("(t p) d -> p t d", p=P)).then_inc(x_in_s, 16)
                if n >= first + RING:
                    if old % 2 == 0:
                        sp.wait_ge(half_used, old // 2 + 1)
                    else:
                        sp.wait_ge(psum_filled2, U2.filled(last_unit2(STREAM2[(old - first) // 2])))
                half = slice((n % 2) * HALF_TILE, (n % 2 + 1) * HALF_TILE)
                sp.dma_start(ring_raw[n % RING], stream_b[(n - first) // 2, :, half]).then_inc(weights[n % RING], 16)
            m = moes[1]
            sp.wait_ge(psum_filled2, U2.filled(("mT", KC - 1)))
            router_inputs_sp(sp, m)
            for i in range(3):
                moe_load(sp, m, 0, 0, i)
            router_sp(sp, m)
            sp.wait_ge(psum_filled2, U2.filled(("wo2", 1, NT - 1)))
            for i in range(3):
                moe_load(sp, m, 1, 1, i)
            moe_sp(sp, m)
            sp.wait_ge(routed, 2 * m.b + 2)
            sp.dma_start(gf, gfin_in.broadcast_to([P, D])).then_inc(block2_in, 16)
            for t in range(NT):
                sp.wait_ge(result, t + 1)
                sp.dma_start(out[0, t * P:(t + 1) * P, :], x[:, t, :]).then_inc(stored, 16)
            sp.wait_ge(stored, 2 * 16 * NT)

        @block.tensor
        def _(pe):
            def begin(key, w=512):
                who, reads = U.read_before(key)
                if who:
                    pe.wait_ge(read_by[who], reads)
                return bank[U.bank(key)]

            def end(ins):
                ins.then_inc(psum_filled, 1)

            def transposes(key, sources):
                b = begin(key)
                for j, s in enumerate(sources):
                    last = nc.tensor.transpose(b[:, j * P:(j + 1) * P], s, c("ident"))
                end(last)

            def half_product(b, left, right, first, last):
                for k in range(KC // 2):
                    for i, (l_, r_) in enumerate(((0, 1), (1, 0), (0, 0))):
                        ins = nc.tensor.matmul(b, left(k)[l_], right(k)[r_], start=(first and k == 0 and i == 0),
                                               stop=(last and k == KC // 2 - 1 and i == 2))
                return ins

            def tile_product(n, pieces, left, right, begin, end):
                units = [key for key, _, _ in pieces]
                banks = {}
                for part in range(2):
                    pe.wait_ge(weights_split, 2 * n + part + 1)
                    w = ring_parts[(2 * n + part) % RING]
                    for i, (key, lo, hi) in enumerate(pieces):
                        starts = key not in banks
                        if starts:
                            banks[key] = begin(key)
                        ends = part == 1 and key not in units[i + 1:]
                        ins = half_product(banks[key][:, lo:hi], lambda k: left(w, part, i, k),
                                           lambda k: right(w, part, i, k), starts, ends)
                        if ends:
                            end(ins)
                    if part == 0:
                        ins.then_inc(half_used, 1)

            def rows_product(prefix, name, parts):
                tile_product(n_stream[name], [((*prefix, t), 0, 512) for t in range(NT)],
                             lambda w, part, t, k: [v[:, 4 * part + k, t * P:(t + 1) * P] for v in parts],
                             lambda w, part, t, k: [v[:, k, :] for v in w], begin, end)

            def columns_product(prefix, name, n, parts):
                tile_product(n_stream[name], [((prefix, 4 * n + m), 0, 512) for m in range(4)],
                             lambda w, part, m, k: [v[:, k, m * P:(m + 1) * P] for v in w],
                             lambda w, part, m, k: [v[:, 4 * part + k, :] for v in parts], begin, end)

            pe.wait_ge(consts_in_s, 16)
            pe.wait_ge(scaled, NT)
            for k in range(KC):
                transposes(("xT", k), [xs[:, t, k * P:(k + 1) * P] for t in range(NT)])
            wait_read(pe, ("xT", KC - 1))
            rows_product(("qi",), "qi", xn_parts)
            pe.wait_ge(kiwi_split, 1)
            b = begin("kiwi")
            for t in range(NT):
                for part in range(2):
                    last = half_product(b[:, t * 72:(t + 1) * 72],
                                        lambda k: [v[:, 4 * part + k, t * P:(t + 1) * P] for v in xn_parts],
                                        lambda k: [v[:, 4 * part + k, :] for v in kiwi_parts], part == 0, part == 1)
            end(last)
            for t in range(NT):
                pe.wait_ge(rotated, t + 1)
                transposes(("qiT", t), [rot[:, t, j * P:(j + 1) * P] for j in range(4)])
            wait_read(pe, "kiwi")
            transposes("kiT", [kirot[:, t, :] for t in range(NT)])
            wait_read(pe, "kiT")
            for t in range(1, NT):
                for h in range(IH):
                    b = begin(("idx", t, h))
                    half = slice(ID * (h % 2), ID * (h % 2) + ID)
                    end(nc.tensor.matmul(b[:, 0:(t + 1) * P], qiT[half, h // 2, t * P:(t + 1) * P],
                                         kiT[half, 0:(t + 1) * P], start=True, stop=True))
            for n in range(2):
                rows_product(("sv", n), f"sv{n}", xn_parts)
            for n in range(2):
                columns_product("su", f"su{n}", n, xn_parts)
            columns_product("ga", "ga0", 0, xn_parts)
            pe.wait_ge(sgu_in, 48)
            for n in range(2):
                transposes(("wT", n), [sgu_w[:, 4 * n + j, :] for j in range(4)])
            wait_read(pe, ("wT", 1))
            pe.wait_ge(vn_scaled, NT)
            for g in range(GROUPS):
                b = begin(("mix", g))
                for t in range(NT):
                    last = nc.tensor.matmul(b[:, t * P:(t + 1) * P], vn[:, t, g * P:(g + 1) * P], wT[:, g, :],
                                            start=True, stop=True)
                end(last)
            columns_product("ga", "ga1", 1, xn_parts)
            pe.wait_ge(gated, GROUPS)
            for n in range(2):
                columns_product("wa", f"wa{n}", n, su_parts)
            for n in range(5):
                if n < 4:
                    rows_product(("qk", n), ["q0", "q1", "k0", "k1"][n], xn_parts)
                if n >= 1:
                    for t in range(NT):
                        pe.wait_ge(rotated, 4 + 4 * (n - 1) + t + 1)
                        transposes(("qkT", n - 1, t), [rot[:, t, j * P:(j + 1) * P] for j in range(4)])
            for n in range(2):
                rows_product(("v", n), f"v{n}", xn_parts)
            wait_read(pe, ("qkT", 3, NT - 1))
            for h in range(HEADS + 2):
                if h < HEADS:
                    for t in range(NT):
                        b = begin(("S", h, t))
                        end(nc.tensor.matmul(b[:, 0:(t + 1) * P], qT[:, h, t * P:(t + 1) * P],
                                             kT[:, h, 0:(t + 1) * P], start=True, stop=True))
                if h >= 2:
                    g = h - 2
                    for t in range(NT):
                        pe.wait_ge(probs_ready, g * NT + t + 1)
                        transposes(("T", g, t), [probs[g % 3][:, CAUSAL_AT[t] + s * P:CAUSAL_AT[t] + (s + 1) * P]
                                                 for s in range(t + 1)])
                    b = begin(("O", g))
                    wait_read(pe, ("v", 1, NT - 1))
                    wait_read(pe, ("T", g, NT - 1))
                    for s in range(NT):
                        last = nc.tensor.matmul(b[:, s * P:SEQ], v_rows[:, s, g * HD:(g + 1) * HD],
                                                pT[:, s, s * P:SEQ], start=(s == 0), stop=(s == NT - 1))
                    end(last)
            for n in range(2):
                columns_product("gb", f"gb{n}", n, xn_parts)
            pe.wait_ge(y_split, HEADS)
            for n in range(2):
                columns_product("wb", f"wb{n}", n, y_parts)
            pe.wait_ge(merged, KC)
            for n in range(2):
                rows_product(("wo", n), f"wo{n}", g_parts)
            m = moes[0]
            router_pe(pe, m, U, begin, end, transposes, wait_read)
            for who in ("act", "dve"):
                pe.wait_ge(read_by[who], U.reader.count(who))
            moe_pe(pe, m)

            pe.wait_ge(m.y_free_act, NE + 1)
            pe.wait_ge(m.y_free_dve, NE + 1)

            def begin2(key):
                who, reads = U2.read_before(key)
                if who:
                    pe.wait_ge(read_by2[who], reads)
                return bank[U2.bank(key)]

            def end2(ins):
                ins.then_inc(psum_filled2, 1)

            def transposes2(key, sources):
                b = begin2(key)
                for j, s in enumerate(sources):
                    last_ = nc.tensor.transpose(b[:, j * P:(j + 1) * P], s, c("ident"))
                end2(last_)

            def rows2(name, parts, meta_parts=None, prefix=None):
                first = 0 if meta_parts else 1

                def tokens(w, part, i, k):
                    if first + i == 0:
                        return [v[:, 4 * part + k, :] for v in meta_parts]
                    t = first + i - 1
                    return [v[:, 4 * part + k, t * P:(t + 1) * P] for v in parts]

                tile_product(len(STREAM1) + n_stream2[name],
                             [((*(prefix or (name,)), i), 0, 512) for i in range(NT2 - first)],
                             tokens, lambda w, part, i, k: [v[:, k, :] for v in w], begin2, end2)

            def columns2(name, meta_too):
                pieces = [((name, m_), 0, 512) for m_ in range(4)]
                if meta_too:
                    pieces += [(name + "_meta", m_ * P, (m_ + 1) * P) for m_ in range(4)]
                tile_product(len(STREAM1) + n_stream2[name], pieces,
                             lambda w, part, i, k: [v[:, k, i % 4 * P:(i % 4 + 1) * P] for v in w],
                             lambda w, part, i, k: [v[:, 4 * part + k, :] for v in (hT_parts if i < 4 else hT_meta)],
                             begin2, end2)

            pe.wait_ge(scaled, NT + 1)
            for n in range(2):
                transposes2(("metaT", n), [xs2[:, 0, (4 * n + j) * P:(4 * n + j + 1) * P] for j in range(4)])
            for t in range(NT):
                pe.wait_ge(scaled, NT + 1 + t + 1)
                for half in range(2):
                    transposes2(("hT", t, half), [xs2[:, 1 + t, k * P:(k + 1) * P]
                                                  for k in range(4 * half, 4 * half + 4)])
            wait_read2(pe, ("hT", NT - 1, 1))
            columns2("sbq", False)
            columns2("sbk", True)
            rows2("sbv", hT_parts, hT_meta)
            rows2("hi", hT_parts, hT_meta)
            columns2("hq", False)
            rows2("hg", hT_parts)
            columns2("hf", True)
            for h in range(SBH + 2):
                if h < SBH:
                    half = slice(SBD * (h % 2), SBD * (h % 2) + SBD)
                    for s in range(NT2):
                        b = begin2(("Z", h, s))
                        end2(nc.tensor.matmul(b[:, 0:STICK_W[s]], sbk[half, h // 2, s * P:(s + 1) * P],
                                              sbq[half, h // 2, FIRST_T[s] * P:SEQ], start=True, stop=True))
                if 1 <= h <= SBH:
                    g = h - 1
                    pe.wait_ge(sp_ready, h)
                    for s in range(NT2):
                        b = begin2(("R", g, s))
                        for s2 in range(s, NT2):
                            col = (FIRST_T[s2] - FIRST_T[s]) * P
                            last_ = nc.tensor.matmul(b[:, col:STICK_W[s]], c("tri_ge") if s2 == s else c("ones"),
                                                     sps[g % 2][:, STICK_AT[s2]:STICK_AT[s2] + STICK_W[s2]],
                                                     start=(s2 == s), stop=(s2 == NT2 - 1))
                        end2(last_)
                if h >= 2:
                    g = h - 2
                    pe.wait_ge(weight_ready, g + 1)
                    b = begin2(("SO", g))
                    for t in range(NT):
                        for s in range(t + 2):
                            a = STICK_AT[s] + (t - FIRST_T[s]) * P
                            last_ = nc.tensor.matmul(b[:, t * SBD:(t + 1) * SBD], zw[g % 3][:, a:a + P],
                                                     sbv[:, s, g * SBD:(g + 1) * SBD], start=(s == 0), stop=(s == t + 1))
                    end2(last_)

            def head_out(g):
                pe.wait_ge(scores_ready, g + 1)
                pe.wait_ge(states_ready, g + 1)
                pe.wait_ge(q_ready, g + 1)
                b = begin2(("HO", g))
                for t in range(NT):
                    nc.tensor.matmul(b[:, t * P:(t + 1) * P], hsc[:, g % 2, t * P:(t + 1) * P],
                                     hv[:, t + 1, g * HD:(g + 1) * HD], start=True, stop=False)
                    last_ = nc.tensor.matmul(b[:, t * P:(t + 1) * P], qexp[:, g % 2, t * P:(t + 1) * P],
                                             states[:, g % 2, t, :], start=False, stop=True)
                end2(last_)

            for h in range(HGH):
                for lv in range(LEVELS):
                    if lv == 0:
                        pe.wait_ge(kd_ready, h + 1)
                        transposes2(("KT", h), [kd[:, h % 2, t * P:(t + 1) * P] for t in range(NT)])
                        b = begin2(("DG", h))
                        for t in range(NT):
                            last_ = nc.tensor.matmul(b[:, t * P:(t + 1) * P], hk[:, h, (t + 1) * P:(t + 2) * P],
                                                     hq[:, h, t * P:(t + 1) * P], start=True, stop=True)
                        end2(last_)
                    n = h * LEVELS + lv
                    pe.wait_ge(level_ready, n + 1)
                    b = begin2(("L", h, lv))
                    for t in range(NT):
                        last_ = nc.tensor.matmul(b[:, t * P:(t + 1) * P], kE[:, n % 2, t * P:(t + 1) * P],
                                                 qE[:, n % 2, t * P:(t + 1) * P], start=True, stop=True)
                    end2(last_)
                    if lv == 2:
                        wait_read2(pe, ("KT", h))
                        b = begin2(("KV", h))
                        for t in range(NT):
                            last_ = nc.tensor.matmul(b[:, t * P:(t + 1) * P], kdR[:, h % 2, t * P:(t + 1) * P],
                                                     hv[:, t, h * HD:(h + 1) * HD], start=True, stop=True)
                        end2(last_)
                    if lv == 1 and h >= 1:
                        head_out(h - 1)
            head_out(HGH - 1)
            pe.wait_ge(heads_normed, HGH + 1)
            for k in range(KC):
                transposes2(("mT", k), [mixed[:, t, k * P:(k + 1) * P] for t in range(NT)])
            wait_read2(pe, ("mT", KC - 1))
            for n in range(2):
                rows2(f"wo2_{n}", mixed_parts, prefix=("wo2", n))
            m = moes[1]
            router_pe(pe, m, U2, begin2, end2, transposes2, wait_read2)
            for who in ("act", "dve"):
                pe.wait_ge(read_by2[who], U2.reader.count(who))
            moe_pe(pe, m)

        @block.scalar
        def _(act):
            def unit(key):
                act.wait_ge(psum_filled, U.filled(key))
                return bank[U.bank(key)]

            def read(ins):
                ins.then_inc(read_by["act"], 1)

            act.wait_ge(x_in_s, 16)
            for t in range(NT):
                nc.scalar.activation(xs[:, t, :], x[:, t, :], ACT.Square, accum_out=ssq[:, t:t + 1])\
                    .then_inc(sumsq, 1)
            act.wait_ge(rms, 1)
            act.wait_ge(sumsq, NT)
            for t in range(NT):
                nc.scalar.activation(xs[:, t, :], x[:, t, :], ACT.Copy, scale=rstd[:, t:t + 1]).then_inc(scaled, 1)
            act.wait_ge(angles_ready, 2)
            nc.scalar.activation(cos[:, :, :], trig[:, 0, :].rearrange("p (t f) -> p t f", t=NT), ACT.Sin)\
                .then_inc(trig_ready, 1)
            nc.scalar.activation(sin[:, :, :], trig[:, 1, :].rearrange("p (t f) -> p t f", t=NT), ACT.Sin)\
                .then_inc(trig_ready, 1)
            for t in range(NT):
                b = unit(("qiT", t))
                read(nc.scalar.copy(qiT[:, :, t * P:(t + 1) * P], b[:, :].rearrange("p (j q) -> p j q", q=P)))
            b = unit("kiT")
            read(nc.scalar.copy(kiT[:, :], b[:, :]))
            n = 0
            for t in range(1, NT):
                for h in range(IH):
                    b = unit(("idx", t, h))
                    if n >= 3:
                        act.wait_ge(rel_used, n - 2)
                    read(nc.scalar.activation(rel[:, n % 3, 0:(t + 1) * P], b[:, 0:(t + 1) * P], ACT.Relu))
                    n += 1
            for n in range(2):
                for t in range(NT):
                    b = unit(("sv", n, t))
                    read(nc.scalar.activation(vn[:, t, n * 512:(n + 1) * 512], b[:, :], ACT.Gelu_apprx_tanh))
            for m in range(KC):
                b = unit(("su", m))
                read(nc.scalar.activation(suT[:, m, :], b[:, :], ACT.Gelu_apprx_tanh))
            for m in moes:
                act.wait_ge(m.rows_cleared, CLEARS_A_BLOCK * 16)
            for m in range(KC):
                b = unit(("ga", m))
                read(nc.scalar.activation(gT[:, m, :], b[:, :], ACT.Sigmoid))
            for n in range(4):
                dst = qT if n < 2 else kT
                for t in range(NT):
                    b = unit(("qkT", n, t))
                    h = 4 * (n % 2)
                    read(nc.scalar.copy(dst[:, h:h + 4, t * P:(t + 1) * P],
                                        b[:, :].rearrange("p (j q) -> p j q", q=P)))
            for n in range(2):
                for t in range(NT):
                    b = unit(("v", n, t))
                    read(nc.scalar.copy(v_rows[:, t, n * 512:(n + 1) * 512], b[:, :]))
            for h in range(HEADS + 1):
                if h < HEADS:
                    for t in range(NT):
                        act.wait_ge(logits_ready, h + 1)
                        p = probs[h % 3][:, CAUSAL_AT[t]:CAUSAL_AT[t + 1]]
                        nc.scalar.activation(p, p, ACT.Exp, bias=nm[:, h, t:t + 1], scale=HD ** -0.5,
                                             accum_out=sums[:, h, t:t + 1]).then_inc(exp_ready, 1)
                if h >= 1:
                    g = h - 1
                    for t in range(NT):
                        b = unit(("T", g, t))
                        if t == 0 and g >= 1:
                            act.wait_ge(psum_filled, U.filled(("O", g - 1)))
                        read(nc.scalar.copy(pT[:, 0:t + 1, t * P:(t + 1) * P],
                                            b[:, 0:(t + 1) * P].rearrange("p (j q) -> p j q", q=P)))
                    b = unit(("O", g))
                    read(nc.scalar.copy(yT[:, g, :], b[:, :]))
            for m in range(KC):
                b = unit(("gb", m))
                read(nc.scalar.activation(gbT[:, m, :], b[:, :], ACT.Sigmoid))
            m = moes[0]
            norm_act(act, m, lambda e, t: wait_read(e, ("wo", 1, t)))
            router_act(act, m, unit, read)
            moe_act(act, m)

            def squares_of(n):
                return at(arena, 4 * TILE + (n % 2) * D, [D])

            A = nc.scalar
            for n, what in enumerate(BETWEEN):
                t, col = (0 if what == "meta" else int(what[-1])), BETWEEN_COLUMN[what]
                if what == "meta":
                    act.wait_ge(meta_in, 16)
                    act.wait_ge(m.moe_added, 1)
                elif what[:-1] == "out":
                    act.wait_ge(m.moe_added, 2 * t + 2)
                else:
                    act.wait_ge(x_normed, t + 1)
                if n >= 2:
                    act.wait_ge(sumsq, TILES_BEFORE["between"] + n - 1)
                A.activation(squares_of(n), meta if what == "meta" else x[:, t, :], ACT.Square,
                             accum_out=ssq[:, col:col + 1]).then_inc(sumsq, 1)
            act.wait_ge(lb_out, 1)
            A.activation(lbl[:, :, :], lbl[:, :, :], ACT.Exp).then_inc(lb_exp, 1)

            def unit2(key):
                act.wait_ge(psum_filled2, U2.filled(key))
                return bank[U2.bank(key)]

            def read2(ins):
                ins.then_inc(read_by2["act"], 1)

            for key, parts in norm_pieces2():
                b = unit2(key)
                A.copy(parts[0], b[:, :].rearrange("p (k q) -> p k q", q=P)).then_inc(high_ready, 1)
            for m_ in range(4):
                b = unit2(("sbq", m_))
                read2(A.copy(sbq[:, m_, :], b[:, :]))
            for m_ in range(4):
                b = unit2(("sbk", m_))
                read2(A.copy(sbk[:, m_, P:L2], b[:, :]))
            b = unit2("sbk_meta")
            read2(A.copy(sbk[:, :, 0:P], b[:, :].rearrange("p (m q) -> p m q", q=P)))
            for name, dst in (("sbv", sbv), ("hi", hv)):
                for t in range(NT2):
                    b = unit2((name, t))
                    read2(A.copy(dst[:, t, :], b[:, :]))
            for m_ in range(4):
                b = unit2(("hq", m_))
                read2(A.activation(hq[:, m_, :], b[:, :], ACT.Silu))
            for t in range(NT):
                b = unit2(("hg", t))
                read2(A.activation(hgate[:, t, :], b[:, :], ACT.Silu))
            for m_ in range(4):
                b = unit2(("hf", m_))
                A.activation(bc[:, m_, P:L2], b[:, :], ACT.Sigmoid)
                read2(A.activation(hk[:, m_, P:L2], b[:, :], ACT.Sigmoid, scale=-1.0))
            b = unit2("hf_meta")
            bv = b[:, :].rearrange("p (m q) -> p m q", q=P)
            A.activation(bc[:, :, 0:P], bv, ACT.Sigmoid)
            read2(A.activation(hk[:, :, 0:P], bv, ACT.Sigmoid, scale=-1.0))
            act.wait_ge(decay_ready, 1)
            wait_read2(act, "hf_meta")
            for h in range(HGH):
                A.activation(bc[:, h, :], bc[:, h, :], ACT.Ln, bias=lb[:, h:h + 1], scale=oml[:, h:h + 1])\
                    .then_inc(log_f_ready, 1)
            for h in range(SBH + 2):
                if h < SBH:
                    act.wait_ge(z_ready, h + 1)
                    v = sps[h % 2]
                    A.activation(v, v, ACT.Exp, scale=-1.0).then_inc(act_step, 1)
                    act.wait_ge(act_step, h + 1)
                    A.activation(v, v, ACT.Ln, bias=1.0).then_inc(log_ready, 1)
                if 1 <= h <= SBH:
                    g = h - 1
                    wait_read2(act, ("R", g, NT2 - 1))
                    A.activation(zw[g % 3], zw[g % 3], ACT.Exp).then_inc(weight_ready, 1)
                if h >= 2:
                    g = h - 2
                    b = unit2(("SO", g))
                    read2(A.copy(mixed[:, :, g * SBD:(g + 1) * SBD],
                                 b[:, 0:NT * SBD].rearrange("p (t d) -> p t d", d=SBD)))
            act.wait_ge(carried, HGH * NT2)
            A.activation(chunk_decay[:, :, :], bc[:, :, P - 1:L2:P], ACT.Exp).then_inc(last_ready, 1)

            def level_exp(n):
                act.wait_ge(diff_ready, n + 1)
                A.activation(diff[:, n % 2, :], diff[:, n % 2, :], ACT.Exp).then_inc(diff_exp, 1)

            def head_exps(h):
                if h >= 2:
                    act.wait_ge(psum_filled2, U2.filled(("HO", h - 2)))
                for t in range(NT):
                    ins = A.activation(kd[:, h % 2, t * P:(t + 1) * P], bc[:, h, t * P:(t + 1) * P], ACT.Exp,
                                       bias=bc[:, h, (t + 1) * P - 1:(t + 1) * P], scale=-1.0)
                ins.then_inc(kd_exp, 1)
                A.activation(qexp[:, h % 2, :], bc[:, h, P:L2], ACT.Exp).then_inc(q_exp, 1)

            def head_copy(h):
                b = unit2(("HO", h))
                read2(A.copy(mixed[:, :, 512 + h * HD:512 + (h + 1) * HD],
                             b[:, :].rearrange("p (t d) -> p t d", d=HD)))

            head_exps(0)
            level_exp(0)
            for h in range(HGH):
                for lv in range(LEVELS):
                    n = h * LEVELS + lv
                    if lv == LEVELS - 1 and h + 1 < HGH:
                        head_exps(h + 1)
                    if n + 1 < HGH * LEVELS:
                        level_exp(n + 1)
                    if lv == 0:
                        b = unit2(("KT", h))
                        read2(A.copy(kdR[:, h % 2, :], b[:, :]))
                    if lv == 1 and h >= 1:
                        head_copy(h - 1)
            head_copy(HGH - 1)
            for k in range(KC):
                b = unit2(("mT", k))
                A.copy(mixed_parts[0][:, k, :], b[:, :]).then_inc(high_ready, 1)
            m = moes[1]
            norm_act(act, m, lambda e, t: wait_read2(e, ("wo2", 1, t)))
            router_act(act, m, unit2, read2)
            moe_act(act, m)
            for t in range(NT):
                act.wait_ge(m.moe_added, 2 * t + 2)
                if t >= 2:
                    act.wait_ge(sumsq, TILES_BEFORE["out2"] + t - 1)
                A.activation(squares_of(t), x[:, t, :], ACT.Square, accum_out=ssq[:, t:t + 1]).then_inc(sumsq, 1)

        @block.vector
        def _(dve):
            def unit(key):
                dve.wait_ge(psum_filled, U.filled(key))
                return bank[U.bank(key)]

            def read(ins):
                ins.then_inc(read_by["dve"], 1)

            def then(ins):
                link("dve", dve, dve_step, ins)

            V = nc.vector
            n_split = 0

            def residual_and_norm(dve, m, name, unit, read):
                for n in range(2):
                    for t in range(NT):
                        b = unit((name, n, t))
                        xv = x[:, t, n * 512:(n + 1) * 512]
                        read(V.tensor_tensor(xv, xv, b[:, :], ALU.add))
                        if n == 1 and t >= 1:
                            norm_dve(dve, m, t - 1)
                norm_dve(dve, m, NT - 1)

            def split_weights(upto):
                nonlocal n_split
                while n_split < upto:
                    n = n_split
                    dve.wait_ge(weights[n % RING], 16 * (n // RING + 1))
                    hi, lo = (v.rearrange("p k c -> p (k c)") for v in ring_parts[n % RING])
                    then(V.tensor_copy(hi, ring_raw[n % RING]))
                    V.tensor_tensor(lo, ring_raw[n % RING], hi.bitcast(F32), ALU.subtract).then_inc(weights_split, 1)
                    n_split += 1

            dve.wait_ge(small_in, 48)
            split_weights(1)
            for k in range(KC):
                b = unit(("xT", k))
                then(V.tensor_scalar(xn_parts[0][:, k, :], b[:, :], g1[:, k:k + 1], None, ALU.mult))
                read(V.scalar_tensor_tensor(xn_parts[1][:, k, :], b[:, :], g1[:, k:k + 1],
                                            xn_parts[0][:, k, :].bitcast(F32), ALU.mult, ALU.subtract))
            split_weights(3)
            dve.wait_ge(small_in, 48)
            dve.wait_ge(consts_in_s, 16)
            then(V.tensor_copy(pos_f[:, :], pos_i[:, :]))
            ang, turns = trig[:, 2, :], trig[:, 3, :]
            for t in range(NT):
                then(V.tensor_scalar(ang[:, t * 64:(t + 1) * 64], c("invf"), pos_f[:, t:t + 1], None, ALU.mult))
            two_pi = 2 * np.pi
            c1 = float(np.float32(6.28125))
            c2 = float(np.float32(np.round((two_pi - c1) * 2 ** 21) / 2 ** 21))
            c3 = float(np.float32(two_pi - c1 - c2))
            magic = 1.5 * 2.0 ** 23
            for j, quarter in ((0, 0.25), (1, 0.0)):
                r = trig[:, j, :]
                then(V.tensor_scalar(turns, ang, 1.0 / two_pi, quarter, ALU.mult, ALU.add))
                then(V.tensor_scalar(turns, turns, magic, None, ALU.add))
                then(V.tensor_scalar(turns, turns, -magic, None, ALU.add))
                then(V.scalar_tensor_tensor(r, turns, -c1, ang, ALU.mult, ALU.add))
                then(V.scalar_tensor_tensor(r, turns, -c2, r, ALU.mult, ALU.add))
                then(V.scalar_tensor_tensor(r, turns, -c3, r, ALU.mult, ALU.add))
                then(V.tensor_scalar(r, r, float(np.pi / 2) if j == 0 else 0.0, 3.1415925, ALU.add, ALU.min))
                V.tensor_scalar(r, r, -3.1415925, None, ALU.max).then_inc(angles_ready, 1)
            kv_ = kiwi_w.rearrange("p k c -> p (k c)")
            hi, lo = (v.rearrange("p k c -> p (k c)") for v in kiwi_parts)
            then(V.tensor_copy(hi, kv_))
            V.tensor_tensor(lo, kv_, hi.bitcast(F32), ALU.subtract).then_inc(kiwi_split, 1)

            rotations = 0

            def rope_unit(key, t, heads, width):
                nonlocal rotations
                b = unit(key)
                if rotations >= 2:
                    dve.wait_ge(rotated, rotations - 1)
                step = HD // width
                shape = [P, 2 * heads, width // 2]
                src = b[:, :].rearrange("p (a f) -> p a f", f=width // 2)
                for table, dst in ((cos, rot_a), (sin, rot_b)):
                    row = table[:, t, 0:HD // 2:step][:, None, :].broadcast_to(shape)
                    last = V.tensor_tensor(dst[:, rotations % 2, :].rearrange("p (a f) -> p a f", f=width // 2),
                                           src, row, ALU.mult)
                read(last)
                rotations += 1

            dve.wait_ge(trig_ready, 2)
            split_weights(4)
            for t in range(NT):
                rope_unit(("qi", t), t, IH, ID)
            split_weights(5)
            b = unit("kiwi")
            kv = b[:, 0:288].rearrange("p (t c) -> p t c", c=72)
            shape = [P, NT, ID // 2]
            x1, x2 = kv[:, :, 0:32], kv[:, :, 32:64]
            cs, sn = cos[:, :, 0:64:2], sin[:, :, 0:64:2]
            then(V.tensor_copy(wi[:, :, :], kv[:, :, 64:72]))
            for dup in (0, 64):
                tmp = at(misc, 0, [NT, 32])
                tmp2 = at(misc, 128, [NT, 32])
                then(V.tensor_tensor(tmp, x1, cs, ALU.mult))
                then(V.tensor_tensor(tmp2, x2, sn, ALU.mult))
                then(V.tensor_tensor(kirot[:, :, dup:dup + 32], tmp, tmp2, ALU.subtract))
                then(V.tensor_tensor(tmp, x2, cs, ALU.mult))
                then(V.tensor_tensor(tmp2, x1, sn, ALU.mult))
                last = V.tensor_tensor(kirot[:, :, dup + 32:dup + 64], tmp, tmp2, ALU.add)
                if dup == 0:
                    then(last)
            read(last)
            n = 0
            for t in range(1, NT):
                s = scores[:, SCORE_AT[t]:SCORE_AT[t] + (t + 1) * P]
                for h in range(IH):
                    wait_read(dve, ("idx", t, h))
                    r = rel[:, n % 3, 0:(t + 1) * P]
                    if h == 0:
                        ins = V.tensor_scalar(s, r, wi[:, t, 0:1], None, ALU.mult)
                    else:
                        dve.wait_ge(rel_used, n)
                        ins = V.scalar_tensor_tensor(s, r, wi[:, t, h:h + 1], s, ALU.mult, ALU.add)
                    ins.then_inc(rel_used, 1)
                    n += 1
            dve.wait_ge(rel_used, n)
            for t in range(1, NT):
                s = scores[:, SCORE_AT[t]:SCORE_AT[t] + (t + 1) * P]
                then(V.tensor_tensor(s[:, t * P:(t + 1) * P], s[:, t * P:(t + 1) * P], c("causal"), ALU.add))
                for i in range(TOPK // 8):
                    if i % 8 == 7:
                        split_weights(n_split + 1)
                    then(V.max(top8[:, :], s))
                    then(V.match_replace(s, top8[:, :], s, TAKEN))
                then(V.tensor_scalar(s, s, -2.0e38, NEG, ALU.is_gt, ALU.mult))
            wait_read(dve, ("sv", 1, NT - 1))
            for t in range(NT):
                for n in range(2):
                    then(V.bn_stats(bn6[:, t, n, :], vn[:, t, n * 512:(n + 1) * 512]))
                V.bn_aggr(bn2[:, t, :], bn6[:, t, :, :]).then_inc(var_ready, 1)
            dve.wait_ge(rms, 2)
            for t in range(NT):
                V.tensor_scalar(vn[:, t, :], vn[:, t, :], bn2[:, t, 0:1], rstd[:, 4 + t:5 + t],
                                ALU.subtract, ALU.mult).then_inc(vn_ready, 1)
            split_weights(2 * n_stream["ga1"] + 2)
            for n in range(2):
                b = unit(("wT", n))
                read(V.tensor_tensor(wT[:, 4 * n:4 * n + 4, :], b[:, :].rearrange("p (g t) -> p g t", t=P),
                                     c("le")[:, None, :].broadcast_to([P, 4, P]), ALU.mult))
            split_weights(2 * n_stream["wa0"] + 1)
            wait_read(dve, ("su", KC - 1))
            sgu_mixed = at(misc, 0, [2, 512])
            for g in range(GROUPS):
                b = unit(("mix", g))
                m = sgu_mixed[:, g % 2, :]
                ins = V.tensor_tensor(m.rearrange("p (t q) -> p t q", q=P), b[:, :].rearrange("p (t q) -> p t q", q=P),
                                      sgu_b[:, g, :][:, None, :].broadcast_to([P, NT, P]), ALU.add)
                read(ins)
                wait_read(dve, ("mix", g))
                then(V.tensor_tensor(m, suT[:, g, :], m, ALU.mult))
                then(V.tensor_copy(su_parts[0][:, g, :], m))
                V.tensor_tensor(su_parts[1][:, g, :], m, su_parts[0][:, g, :].bitcast(F32), ALU.subtract)\
                    .then_inc(gated, 1)
            split_weights(2 * n_stream["wa0"] + 3)
            wait_read(dve, ("ga", KC - 1))
            for m in range(KC):
                if m % 4 == 0:
                    split_weights(2 * (n_stream["wa0"] + m // 4) + 4)
                b = unit(("wa", m))
                read(V.tensor_tensor(gT[:, m, :], gT[:, m, :], b[:, :], ALU.mult))
            for n in range(4):
                split_weights(2 * (n_stream["q0"] + n) + 4)
                for t in range(NT):
                    rope_unit(("qk", n, t), t, 4, HD)
            split_weights(2 * n_stream["v1"] + 5)
            for h in range(HEADS + 1):
                if h < HEADS:
                    for t in range(NT):
                        b = unit(("S", h, t))
                        if h >= 3 and t == 0:
                            dve.wait_ge(psum_filled, U.filled(("T", h - 3, NT - 1)))
                        w = (t + 1) * P
                        mask = c("causal") if t == 0 else scores[:, SCORE_AT[t]:SCORE_AT[t] + w]
                        p = probs[h % 3][:, CAUSAL_AT[t]:CAUSAL_AT[t + 1]]
                        ins = V.tensor_tensor_reduce(out=p, in0=b[:, 0:w], in1=mask, scale=1.0, scalar=-3.0e38,
                                                     op0=ALU.add, op1=ALU.max, accum_out=mx[:, h, t:t + 1])
                        read(ins)
                    wait_read(dve, ("S", h, NT - 1))
                    V.tensor_scalar(nm[:, h, :], mx[:, h, :], -(HD ** -0.5), None, ALU.mult)\
                        .then_inc(logits_ready, 1)
                if h >= 1:
                    g = h - 1
                    dve.wait_ge(exp_ready, (g + 1) * NT)
                    then(V.reciprocal(inv[:, g, :], sums[:, g, :]))
                    for t in range(NT):
                        p = probs[g % 3][:, CAUSAL_AT[t]:CAUSAL_AT[t + 1]]
                        V.tensor_scalar(p, p, inv[:, g, t:t + 1], None, ALU.mult).then_inc(probs_ready, 1)
            split_weights(2 * n_stream["gb0"] + 3)
            wait_read(dve, ("O", HEADS - 1))
            for h in range(HEADS):
                then(V.tensor_copy(y_parts[0][:, h, :], yT[:, h, :]))
                V.tensor_tensor(y_parts[1][:, h, :], yT[:, h, :], y_parts[0][:, h, :].bitcast(F32), ALU.subtract)\
                    .then_inc(y_split, 1)
            split_weights(2 * n_stream["gb1"] + 4)
            for m in range(KC):
                if m % 4 == 0:
                    split_weights(2 * (n_stream["wb0"] + m // 4) + 4)
                b = unit(("wb", m))
                wait_read(dve, ("gb", m))
                ins = V.tensor_tensor(gbT[:, m, :], gbT[:, m, :], b[:, :], ALU.mult)
                read(ins)
                wait_read(dve, ("wb", m))
                then(V.tensor_tensor(gT[:, m, :], gT[:, m, :], gbT[:, m, :], ALU.add))
                then(V.tensor_copy(g_parts[0][:, m, :], gT[:, m, :]))
                V.tensor_tensor(g_parts[1][:, m, :], gT[:, m, :], g_parts[0][:, m, :].bitcast(F32), ALU.subtract)\
                    .then_inc(merged, 1)
            split_weights(2 * len(STREAM1))
            dve.wait_ge(x_in_s, 32)
            residual_and_norm(dve, moes[0], "wo", unit, read)
            m = moes[0]
            router_dve(dve, m, unit, read, then, wait_read)

            def normed_by(what, gain, dst, src, ready):
                col = BETWEEN_COLUMN[what]
                dve.wait_ge(rms, ROOTS_BEFORE["between"] + BETWEEN.index(what) + 1)
                V.scalar_tensor_tensor(dst, src, rstd[:, col:col + 1], gain, ALU.mult, ALU.mult).then_inc(ready, 1)

            def between(t):
                if t == 0:
                    dve.wait_ge(block2_in, 16 * 5)
                    normed_by("meta", gmix, xs2[:, 0, :], meta, scaled)
                if 1 <= t <= NT:
                    normed_by(f"out{t - 1}", gf, x[:, t - 1, :], x[:, t - 1, :], x_normed)
                if 2 <= t:
                    normed_by(f"in{t - 2}", gmix, xs2[:, t - 1, :], x[:, t - 2, :], scaled)

            moe_dve(dve, m, between)

            between(NT)
            between(NT + 1)
            then(V.tensor_tensor(lbm[:, :], lbl[:, 0, :], lbl[:, 1, :], ALU.max))
            V.tensor_tensor(lbl[:, :, :], lbl[:, :, :], lbm[:, None, :].broadcast_to([P, 2, HGH]), ALU.subtract)\
                .then_inc(lb_out, 1)

            def unit2(key):
                dve.wait_ge(psum_filled2, U2.filled(key))
                return bank[U2.bank(key)]

            def read2(ins):
                ins.then_inc(read_by2["dve"], 1)

            for i, (key, parts) in enumerate(norm_pieces2()):
                dve.wait_ge(high_ready, i + 1)
                b = unit2(key)
                read2(V.tensor_tensor(parts[1], b[:, :].rearrange("p (k q) -> p k q", q=P), parts[0].bitcast(F32),
                                      ALU.subtract))
                if i == 1:
                    split_weights(2 * len(STREAM1) + 1)
            split_weights(2 * len(STREAM1) + 4)
            dve.wait_ge(lb_exp, 1)
            then(V.tensor_tensor(lbm[:, :], lbl[:, 0, :], lbl[:, 1, :], ALU.add))
            then(V.reciprocal(lbm[:, :], lbm[:, :]))
            then(V.tensor_tensor(lb[:, :], lbl[:, 0, :], lbm[:, :], ALU.mult))
            V.tensor_scalar(oml[:, :], lb[:, :], -1.0, 1.0, ALU.mult, ALU.add).then_inc(decay_ready, 1)
            dve.wait_ge(decay_ready, 1)
            split_weights(2 * (len(STREAM1) + len(STREAM2)) - 1)
            wait_read2(dve, "hf_meta")

            def keys():
                for h in range(HGH):
                    then(V.tensor_scalar(hk[:, h, :], hk[:, h, :], oml[:, h:h + 1], None, ALU.mult))
                V.memset(hk[:, :, 0:P - META], 0.0).then_inc(keys_ready, 1)

            def running_decay(h):
                dve.wait_ge(log_f_ready, h + 1)
                for t in range(NT2):
                    v = bc[:, h, t * P:(t + 1) * P]
                    V.tensor_tensor_scan(v, c("ones"), v, 0.0, ALU.mult, ALU.add).then_inc(carried, 1)

            scale = SBD ** -0.5
            dve.wait_ge(stored, 16 * NT)
            for h in range(SBH + 1):
                if h < SBH:
                    z, v = zw[h % 3], sps[h % 2]
                    if h >= 3:
                        dve.wait_ge(psum_filled2, U2.filled(("SO", h - 3)))
                    for s in range(NT2):
                        b = unit2(("Z", h, s))
                        zs = z[:, STICK_AT[s]:STICK_AT[s] + STICK_W[s]]
                        if s == 0:
                            ins = V.tensor_scalar(zs, b[:, :], scale, c("pad_rows"), ALU.mult, ALU.add)
                        else:
                            ins = V.scalar_tensor_tensor(zs[:, 0:P], b[:, 0:P], scale, c("strict"), ALU.mult, ALU.add)
                            if STICK_W[s] > P:
                                ins = V.tensor_scalar(zs[:, P:], b[:, P:STICK_W[s]], scale, None, ALU.mult)
                        read2(ins)
                    wait_read2(dve, ("Z", h, NT2 - 1))
                    V.scalar_tensor_tensor(v, z, -1.0, z, ALU.mult, ALU.max).then_inc(z_ready, 1)
                if h >= 1:
                    g = h - 1
                    for s in range(NT2):
                        b = unit2(("R", g, s))
                        zs = zw[g % 3][:, STICK_AT[s]:STICK_AT[s] + STICK_W[s]]
                        read2(V.tensor_tensor(zs, zs, b[:, 0:STICK_W[s]], ALU.subtract))
                if h < SBH:
                    dve.wait_ge(log_ready, h + 1)
                    V.scalar_tensor_tensor(v, z, 0.0, v, ALU.max, ALU.add).then_inc(sp_ready, 1)
                if h < HGH:
                    running_decay(h)
                if h == HGH:
                    keys()
            dve.wait_ge(psum_filled2, U2.filled(("SO", SBH - 1)))
            dve.wait_ge(carried, HGH * NT2)
            then(V.memset(qE[:, :, :], 0.0))
            then(V.memset(kE[:, :, :], 0.0))

            def halves(v, half):
                return v.rearrange("p (b two i) -> p b two i", two=2, i=half)

            def level_diff(n):
                h, lv = divmod(n, LEVELS)
                half = P >> (lv + 1)
                src, dst = halves(bc[:, h, P:L2], half), halves(diff[:, n % 2, :], half)
                if n >= 2:
                    dve.wait_ge(level_ready, n - 1)
                ref = src[:, :, 0, half - 1:half].broadcast_to([P, SEQ // (2 * half), half])
                V.tensor_tensor(dst[:, :, 1, :], src[:, :, 1, :], ref, ALU.subtract)
                V.tensor_tensor(dst[:, :, 0, :], ref, src[:, :, 0, :], ALU.subtract).then_inc(diff_ready, 1)

            def level_products(n):
                h, lv = divmod(n, LEVELS)
                half = P >> (lv + 1)
                dve.wait_ge(diff_exp, n + 1)
                e = halves(diff[:, n % 2, :], half)
                V.tensor_tensor(halves(qE[:, n % 2, :], half)[:, :, 1, :], e[:, :, 1, :],
                                halves(hq[:, h, :], half)[:, :, 1, :], ALU.mult)
                V.tensor_tensor(halves(kE[:, n % 2, :], half)[:, :, 0, :], e[:, :, 0, :],
                                halves(hk[:, h, P:L2], half)[:, :, 0, :], ALU.mult).then_inc(level_ready, 1)

            def level_mask(i):
                a = CONST_COLS["levels"][0] + i * P
                return cst[:, a:a + P][:, None, :].broadcast_to([P, NT, P])

            def level_read(n):
                h, lv = divmod(n, LEVELS)
                s = hsc[:, h % 2, :].rearrange("p (t q) -> p t q", q=P)
                if lv == 0:
                    if h >= 2:
                        dve.wait_ge(psum_filled2, U2.filled(("HO", h - 2)))
                    b = unit2(("DG", h))
                    read2(V.tensor_tensor(s, b[:, :].rearrange("p (t q) -> p t q", q=P), level_mask(LEVELS), ALU.mult))
                    wait_read2(dve, ("DG", h))
                b = unit2(("L", h, lv))
                read2(V.copy_predicated(s, level_mask(lv).bitcast(U32), b[:, :].rearrange("p (t q) -> p t q", q=P)))
                wait_read2(dve, ("L", h, lv))
                if lv == 2:
                    b = unit2(("KV", h))
                    st = states[:, h % 2, :, :]
                    then(V.tensor_copy(st[:, 0, :], b[:, 0:P]))
                    for t in range(1, NT):
                        ins = V.scalar_tensor_tensor(st[:, t, :], st[:, t - 1, :], chunk_decay[:, h, t:t + 1],
                                                     b[:, t * P:(t + 1) * P], ALU.mult, ALU.add)
                        if t < NT - 1:
                            then(ins)
                    read2(ins)
                    wait_read2(dve, ("KV", h))
                    dve.sem_inc(states_ready, 1)
                if lv == LEVELS - 1:
                    dve.sem_inc(scores_ready, 1)

            def head_products(h):
                dve.wait_ge(kd_exp, h + 1)
                V.tensor_tensor(kd[:, h % 2, :], kd[:, h % 2, :], hk[:, h, 0:SEQ], ALU.mult).then_inc(kd_ready, 1)
                dve.wait_ge(q_exp, h + 1)
                V.tensor_tensor(qexp[:, h % 2, :], qexp[:, h % 2, :], hq[:, h, :], ALU.mult).then_inc(q_ready, 1)

            dve.wait_ge(last_ready, 1)
            dve.wait_ge(keys_ready, 1)
            level_diff(0)
            head_products(0)
            for n in range(HGH * LEVELS):
                if n + 1 < HGH * LEVELS:
                    level_diff(n + 1)
                level_products(n)
                if n >= 1:
                    level_read(n - 1)
                if n % LEVELS == LEVELS - 1 and n // LEVELS + 1 < HGH:
                    head_products(n // LEVELS + 1)
                if n == 4:
                    dve.wait_ge(squared, 1)
                    V.tensor_reduce(rstd[:, 0:32].rearrange("p (t h) -> p t h", h=SBH),
                                    at(misc, 1024, [NT, 512]).rearrange("p t (h d) -> p t h d", d=SBD), AX.X, ALU.add)\
                        .then_inc(squares_ready, 1)
                if n // LEVELS >= 1 and n % LEVELS == 5:
                    g = n // LEVELS - 1
                    dve.wait_ge(squared, g + 2)
                    V.tensor_reduce(rstd[:, 32 + 4 * g:36 + 4 * g], at(misc, 1024, [NT, HD]), AX.X, ALU.add)\
                        .then_inc(squares_ready, 1)
            level_read(HGH * LEVELS - 1)
            g = HGH - 1
            wait_read2(dve, ("HO", g))
            v, root = mixed[:, :, 512 + g * HD:], rstd[:, 32 + 4 * g:36 + 4 * g]
            then(V.tensor_tensor(squares, v, v, ALU.mult))
            V.tensor_reduce(root, squares, AX.X, ALU.add).then_inc(squares_ready, 1)
            dve.wait_ge(rms, ROOTS_BEFORE["heads"] + 1)
            then(V.tensor_tensor(v, v, root[:, :, None].broadcast_to([P, NT, HD]), ALU.mult))
            dve.wait_ge(heads_normed, HGH)
            V.tensor_tensor(v, v, hgate[:, :, g * HD:], ALU.mult).then_inc(heads_normed, 1)
            for k in range(KC):
                dve.wait_ge(high_ready, 2 + 2 * NT + k + 1)
                b = unit2(("mT", k))
                hi, lo = (v[:, k, :] for v in mixed_parts)
                read2(V.tensor_tensor(lo, b[:, :], hi.bitcast(F32), ALU.subtract))
            split_weights(2 * (len(STREAM1) + len(STREAM2)))
            dve.wait_ge(x_in_s, 48)
            residual_and_norm(dve, moes[1], "wo2", unit2, read2)
            m = moes[1]
            router_dve(dve, m, unit2, read2, then, wait_read2)

            def last_norm(t):
                if t == 0:
                    dve.wait_ge(block2_in, 16 * 6)
                else:
                    dve.wait_ge(rms, ROOTS_BEFORE["out2"] + t)
                    V.scalar_tensor_tensor(x[:, t - 1, :], x[:, t - 1, :], rstd[:, t - 1:t], gf, ALU.mult, ALU.mult)\
                        .then_inc(result, 1)

            moe_dve(dve, m, last_norm)
            last_norm(NT)

        @block.gpsimd
        def _(pool):
            def then(ins):
                link("pool", pool, pool_step, ins)

            G = nc.gpsimd
            G.memset(no_token[:, :], 0).then_inc(ids_ready, 1)
            G.memset(zeros, 0.0).then_inc(ids_ready, 1)
            G.iota(token_id[:, :], pattern=[[P, NT]], base=0, channel_multiplier=1).then_inc(ids_ready, 1)
            pool.wait_ge(consts_in_s, 16)
            pool.wait_ge(sumsq, NT)
            then(G.tensor_scalar(rstd[:, 0:4], ssq[:, 0:4], 1.0 / D, EPS, ALU.mult, ALU.add))
            G.tensor_tensor(rstd[:, 0:4], rstd[:, 0:4], c("nhalf")[:, 0:4], ALU.pow).then_inc(rms, 1)
            rotations = 0

            def add_halves(key, slot, heads, width):
                nonlocal rotations
                wait_read(pool, key)
                pattern = dict(two=2, f=width // 2)
                a = rot_a[:, rotations % 2, :].rearrange("p (h two f) -> p h two f", **pattern)
                s = rot_b[:, rotations % 2, :].rearrange("p (h two f) -> p h two f", **pattern)
                o = rot[:, slot, :].rearrange("p (h two f) -> p h two f", **pattern)
                if rotations >= 8:
                    pool.wait_ge(psum_filled, U.filled(("qkT", (rotations - 8) // 4, slot)))
                elif rotations >= 4:
                    pool.wait_ge(psum_filled, U.filled(("qiT", slot)))
                then(G.tensor_tensor(o[:, :, 0, :], a[:, :, 0, :], s[:, :, 1, :], ALU.subtract))
                G.tensor_tensor(o[:, :, 1, :], a[:, :, 1, :], s[:, :, 0, :], ALU.add).then_inc(rotated, 1)
                rotations += 1

            for t in range(NT):
                add_halves(("qi", t), t, IH, ID)
            pool.wait_ge(var_ready, NT)
            then(G.tensor_scalar(rstd[:, 4:8], bn2[:, :, 1], EPS, None, ALU.add))
            G.tensor_tensor(rstd[:, 4:8], rstd[:, 4:8], c("nhalf")[:, 0:4], ALU.pow).then_inc(rms, 1)
            pool.wait_ge(sgu_in, 48)
            for t in range(NT):
                pool.wait_ge(vn_ready, t + 1)
                G.tensor_tensor(vn[:, t, :], vn[:, t, :], sgu_g[:, :], ALU.mult).then_inc(vn_scaled, 1)
            for n in range(4):
                for t in range(NT):
                    add_halves(("qk", n, t), t, 4, HD)
            m = moes[0]
            norm_pool(pool, m, then)

            def between(n):
                inverse_rms(pool, BETWEEN_COLUMN[BETWEEN[n]], TILES_BEFORE["between"] + n + 1, then)

            moe_pool(pool, m, lambda: G.memset(meta, 0.0).then_inc(meta_cleared, 1),
                     lambda n: between(0) if n == 5 else None)
            for n in range(1, len(BETWEEN)):
                between(n)
            def root_of(v, width):
                then(G.tensor_scalar(v, v, 1.0 / width, EPS, ALU.mult, ALU.add))
                return G.tensor_tensor(v, v, c("nhalf")[:, 0:v.shape[1]], ALU.pow)

            wait_read2(pool, ("SO", SBH - 1))
            work = at(misc, 1024, [NT, 512])
            v = mixed[:, :, 0:512]
            G.tensor_tensor(work, v, v, ALU.mult).then_inc(squared, 1)
            pool.wait_ge(squares_ready, 1)
            then(root_of(rstd[:, 0:32], SBD))
            for t in range(NT):
                vt = mixed[:, t, 0:512].rearrange("p (h d) -> p h d", d=SBD)
                then(G.tensor_tensor(vt, vt, rstd[:, SBH * t:SBH * t + SBH][:, :, None].broadcast_to([P, SBH, SBD]),
                                     ALU.mult))
            G.tensor_tensor(v, v, sb_gain[:, None, :].broadcast_to([P, NT, 512]), ALU.mult).then_inc(heads_normed, 1)
            then(G.tensor_tensor(hgate, hgate, hg_gain[:, None, :].broadcast_to([P, NT, 512]), ALU.mult))
            for g in range(HGH - 1):
                wait_read2(pool, ("HO", g))
                v, root, work = mixed[:, :, 512 + g * HD:512 + (g + 1) * HD], rstd[:, 32 + 4 * g:36 + 4 * g], \
                    at(misc, 1024, [NT, HD])
                G.tensor_tensor(work, v, v, ALU.mult).then_inc(squared, 1)
                pool.wait_ge(squares_ready, g + 2)
                then(root_of(root, HD))
                then(G.tensor_tensor(v, v, root[:, :, None].broadcast_to([P, NT, HD]), ALU.mult))
                G.tensor_tensor(v, v, hgate[:, :, g * HD:(g + 1) * HD], ALU.mult).then_inc(heads_normed, 1)
            pool.wait_ge(squares_ready, HGH + 1)
            root_of(rstd[:, 32 + 4 * (HGH - 1):32 + 4 * HGH], HD).then_inc(rms, 1)
            m = moes[1]
            norm_pool(pool, m, then)
            moe_pool(pool, m, lambda: None, lambda n: None)
            for t in range(NT):
                inverse_rms(pool, t, TILES_BEFORE["out2"] + t + 1, then)


def kernel(**inputs):
    import concourse.bacc as bacc
    from concourse.bass_utils import run_bass_kernel_spmd as run

    def a(name):
        return np.asarray(inputs[name])

    def chunks(w):
        return w.reshape(w.shape[0] // P, P, w.shape[1]).transpose(1, 0, 2).reshape(P, -1)

    def experts(w):
        e, k, n = w.shape
        return w.reshape(e, k // P, P, n).transpose(0, 2, 1, 3).reshape(e, P, -1)

    def column(v):
        return v.reshape(-1, P).T

    w_in = a("w_in")[0]
    widths = [("q", 1024), ("k", 1024), ("v", 1024), ("qi", 512), ("ki", 64), ("wi", 8), ("su", 1024), ("sv", 1024),
              ("ga", 1024), ("gb", 1024)]
    parts, start = {}, 0
    for name, width in widths:
        parts[name] = w_in[:, start:start + width]
        start += width
    parts["wa"], parts["wb"], parts["wo"] = a("w_branch_a")[0], a("w_branch_b")[0], a("w_out")[0]

    def tile(name):
        if name == "qi":
            return chunks(parts["qi"])
        n = int(name[-1])
        return chunks(parts[name[:-1]][:, n * 512:(n + 1) * 512])

    w_in2 = a("w_in_2")[0]
    order2 = ["sbq", "sbk", "sbv", "hq", "hf", "hi", "hg"]
    parts2 = {name: w_in2[:, n * 512:(n + 1) * 512] for n, name in enumerate(order2)}
    for n in range(2):
        parts2[f"wo2_{n}"] = a("w_out_2")[0][:, n * 512:(n + 1) * 512]

    arrays = {
        "x": a("x")[0],
        "positions": a("positions")[0].reshape(NT, P).T,
        "constants": CONSTANTS,
        "norm1": column(a("norm1_g")[0]),
        "stream_a": np.stack([tile(name) for name in STREAM1]),
        "kiwi": chunks(np.concatenate([parts["ki"], parts["wi"]], axis=1)),
        "sgu_norm": a("sgu_norm_g"),
        "sgu_w": a("sgu_w")[0],
        "sgu_b": a("sgu_b")[0],
        "norm2": a("norm2_g"),
        "router": chunks(np.concatenate([a("w_router_group")[0], a("w_router_expert")[0]], axis=1)),
        "router_b": np.concatenate([a("b_router_group"), a("b_router_expert")], axis=1),
        "expert_in": experts(a("w_expert_in")[0]),
        "expert_out": experts(a("w_expert_out")[0]),
        "meta": a("meta_tokens_2"),
        "lb": a("lb_logits_2").reshape(2, HGH, P).transpose(2, 0, 1).reshape(P, 2 * HGH),
        "mix_norm": a("g_mix_2"),
        "stream_b": np.stack([chunks(parts2[name]) for name in STREAM2]),
        "sb_gain": a("sb_gain_2"),
        "hg_gain": a("hg_gain_2"),
        "ffn_norm": a("g_ffn_2"),
        "router2": chunks(np.concatenate([a("w_router_group_2")[0], a("w_router_expert_2")[0]], axis=1)),
        "router2_b": np.concatenate([a("b_router_group_2"), a("b_router_expert_2")], axis=1),
        "expert_gate": experts(a("w_expert_gate_2")[0]),
        "expert_up": experts(a("w_expert_up_2")[0]),
        "expert_down": experts(a("w_expert_down_2")[0]),
        "final_norm2": a("g_final_2").reshape(1, D),
        "final_norm1": a("norm_f_g").reshape(1, D),
    }
    arrays = {"in_" + name: np.ascontiguousarray(v) for name, v in arrays.items()}
    nc = bacc.Bacc("TRN2", target_bir_lowering=False, num_devices=1)
    args = [nc.dram_tensor(name, v.shape, mybir.dt.from_np(v.dtype), kind="ExternalInput").ap()
            for name, v in arrays.items()]
    args.append(nc.dram_tensor("out_0", (1, SEQ, D), F32, kind="ExternalOutput").ap())
    build(nc, *args)
    r = run(nc, [arrays], core_ids=[0])
    return r.results[0]["out_0"]
```
